# Optimizing a Trainium2 kernel written in Bass

```python
import math
import jax
import jax.numpy as jnp
from jax import lax
import numpy as np

D_MODEL = 1024
BATCH = 1
SEQ = 512
DEPTH = 2

GRID_W = 64
CTX_LEN = 256
EPS = 1e-6
CONV_K = 3

DN_HEADS = 4
DN_DK = 128
DN_DV = 128
DN_DIRS = 2
DN_CHUNK = 64

ATT_HEADS = 8
ATT_KV_HEADS = 2
ATT_HD = 64
ATT_GROUPS = ATT_HEADS // ATT_KV_HEADS
Q_BLOCK = 128
ROPE_THETA = 10000.0
ROPE_AXIS_DIM = ATT_HD // 2

SC_DIM = D_MODEL

D_FF = 2816

N_EVEN = (DEPTH + 1) // 2
N_ODD = DEPTH // 2

DN_K_W = DN_HEADS * DN_DK
DN_V_W = DN_HEADS * DN_DV
DN_SCAL_W = DN_DIRS * DN_HEADS
ATT_Q_W = ATT_HEADS * ATT_HD
ATT_KV_W = ATT_KV_HEADS * ATT_HD
OFF_DN_K = 0
OFF_DN_V = OFF_DN_K + DN_K_W
OFF_DN_ALPHA = OFF_DN_V + DN_V_W
OFF_DN_BETA = OFF_DN_ALPHA + DN_SCAL_W
OFF_ATT_K = OFF_DN_BETA + DN_SCAL_W
OFF_ATT_V = OFF_ATT_K + ATT_KV_W
KV_COLS = OFF_ATT_V + ATT_KV_W
QO_DN_Q = 0
QO_DN_G = QO_DN_Q + DN_K_W
QO_ATT_Q = QO_DN_G + DN_V_W
Q_COLS = QO_ATT_Q + ATT_Q_W
PROJ_COLS = KV_COLS + Q_COLS
MIX_W = DN_V_W + ATT_Q_W

kernel_name = 'hybrid_deltanet_gqa_shortconv_dit_trunk'

def rms_norm(x, w):
    xf = x.astype(jnp.float32)
    y = xf * lax.rsqrt(jnp.mean(xf * xf, axis=-1, keepdims=True) + EPS)
    return (y * w.astype(jnp.float32)).astype(x.dtype)

def l2_norm(x):
    xf = x.astype(jnp.float32)
    return xf * lax.rsqrt(jnp.sum(xf * xf, axis=-1, keepdims=True) + EPS)

def modulate(xn, shift, scale):
    return xn * (1 + scale) + shift

def dwconv(x, w):
    k, ch = w.shape
    pad = (k - 1) // 2
    return lax.conv_general_dilated(
        x, w[:, None, :].astype(x.dtype), window_strides=(1,), padding=[(pad, pad)],
        dimension_numbers=('NWC', 'WIO', 'NWC'), feature_group_count=ch)

def axial_rope(n):
    rows = n // GRID_W
    r = jnp.repeat(jnp.arange(rows, dtype=jnp.float32), GRID_W)
    col = jnp.tile(jnp.arange(GRID_W, dtype=jnp.float32), rows)
    inv = ROPE_THETA ** (-jnp.arange(0, ROPE_AXIS_DIM, 2, dtype=jnp.float32) / ROPE_AXIS_DIM)
    ang = jnp.concatenate([r[:, None] * inv, col[:, None] * inv], axis=-1)
    return jnp.cos(ang), jnp.sin(ang)

def apply_rope(x, cos, sin):
    xf = x.astype(jnp.float32).reshape(x.shape[:-1] + (ATT_HD // 2, 2))
    x0, x1 = xf[..., 0], xf[..., 1]
    cs, sn = cos[None, :, None, :], sin[None, :, None, :]
    out = jnp.stack([x0 * cs - x1 * sn, x0 * sn + x1 * cs], axis=-1)
    return out.reshape(x.shape).astype(x.dtype)

def _to_chunks(a):
    b, t = a.shape[:2]
    a = a.reshape((b, t // DN_CHUNK, DN_CHUNK) + a.shape[2:])
    return jnp.moveaxis(jnp.moveaxis(a, 1, 0), 3, 2)

def _from_chunks(a):
    a = jnp.moveaxis(jnp.moveaxis(a, 3, 2), 0, 1)
    return a.reshape((a.shape[0], a.shape[1] * a.shape[2]) + a.shape[3:])

def _delta_step(s, k_i, u_i, w_i, g_i):
    v_new = u_i - jnp.einsum('bhck,bhkv->bhcv', w_i, s)
    g_last = g_i[..., -1]
    k_dec = k_i * jnp.exp(g_last[..., None] - g_i)[..., None]
    s_next = s * jnp.exp(g_last)[..., None, None] + jnp.einsum('bhck,bhcv->bhkv', k_dec, v_new)
    return v_new, s_next

def chunk_gated_delta(k, v, g, beta, s0, q=None):
    kc, vc, bc = _to_chunks(k), _to_chunks(v), _to_chunks(beta)
    gc = jnp.cumsum(_to_chunks(g), axis=-1)
    idx = jnp.arange(DN_CHUNK)
    incl = idx[:, None] >= idx[None, :]
    strict = idx[:, None] > idx[None, :]
    decay = jnp.where(incl, jnp.exp(jnp.where(incl, gc[..., :, None] - gc[..., None, :], 0.0)), 0.0)
    kb = kc * bc[..., None]
    lower = jnp.where(strict, jnp.einsum('nbhid,nbhjd->nbhij', kb, kc) * decay, 0.0)
    eye = jnp.eye(DN_CHUNK, dtype=jnp.float32)
    tmat = lax.linalg.triangular_solve(eye + lower, jnp.broadcast_to(eye, lower.shape),
                                       left_side=True, lower=True, unit_diagonal=True)
    u = jnp.einsum('nbhij,nbhjd->nbhid', tmat, vc * bc[..., None])
    w = jnp.einsum('nbhij,nbhjd->nbhid', tmat, kb * jnp.exp(gc)[..., None])
    if q is None:
        def state_step(s, inp):
            _, s_next = _delta_step(s, *inp)
            return s_next, None
        s_final, _ = lax.scan(state_step, s0, (kc, u, w, gc))
        return None, s_final
    qc = _to_chunks(q) * (DN_DK ** -0.5)
    intra = jnp.where(incl, jnp.einsum('nbhid,nbhjd->nbhij', qc, kc) * decay, 0.0)

    def out_step(s, inp):
        q_i, a_i, k_i, u_i, w_i, g_i = inp
        v_new, s_next = _delta_step(s, k_i, u_i, w_i, g_i)
        o = (jnp.einsum('bhck,bhkv->bhcv', q_i * jnp.exp(g_i)[..., None], s)
             + jnp.einsum('bhij,bhjv->bhiv', a_i, v_new))
        return s_next, o

    s_final, o = lax.scan(out_step, s0, (qc, intra, kc, u, w, gc))
    return _from_chunks(o), s_final

def run_direction(q, k, v, g, beta, s0, d):
    g_d, b_d = g[:, :, d], beta[:, :, d]
    if d == 1:
        k, v, g_d, b_d = (jnp.flip(a, axis=1) for a in (k, v, g_d, b_d))
        q = None if q is None else jnp.flip(q, axis=1)
    o, s = chunk_gated_delta(k, v, g_d, b_d, s0, q)
    if d == 1 and o is not None:
        o = jnp.flip(o, axis=1)
    return o, s

def dn_prepare(kv_side, q_side, conv_w, a_log, dt_bias):
    b, t = kv_side.shape[:2]
    kv = jax.nn.silu(dwconv(kv_side[..., OFF_DN_K:OFF_DN_ALPHA], conv_w[:, :DN_K_W + DN_V_W]))
    k = l2_norm(kv[..., :DN_K_W].reshape(b, t, DN_HEADS, DN_DK))
    v = kv[..., DN_K_W:].reshape(b, t, DN_HEADS, DN_DV).astype(jnp.float32)
    alpha = kv_side[..., OFF_DN_ALPHA:OFF_DN_BETA].astype(jnp.float32).reshape(b, t, DN_DIRS, DN_HEADS)
    g = -jnp.exp(a_log.astype(jnp.float32)) * jax.nn.softplus(alpha + dt_bias.astype(jnp.float32))
    beta = jax.nn.sigmoid(kv_side[..., OFF_DN_BETA:OFF_ATT_K].astype(jnp.float32).reshape(b, t, DN_DIRS, DN_HEADS))
    q = None
    if q_side is not None:
        qs = jax.nn.silu(dwconv(q_side[..., QO_DN_Q:QO_DN_G], conv_w[:, DN_K_W + DN_V_W:]))
        q = l2_norm(qs.reshape(b, t, DN_HEADS, DN_DK))
    return q, k, v, g, beta

def bidir_deltanet(lat_in, ctx_in):
    b = lat_in[1].shape[0]
    zero = jnp.zeros((b, DN_HEADS, DN_DK, DN_DV), jnp.float32)
    o_lat, o_ctx = [], []
    for d in range(DN_DIRS):
        oc, s_ctx = run_direction(*ctx_in, zero, d)
        ol, _ = run_direction(*lat_in, s_ctx, d)
        o_lat.append(ol)
        o_ctx.append(oc)
    o_lat = o_lat[0] + o_lat[1]
    o_ctx = None if o_ctx[0] is None else o_ctx[0] + o_ctx[1]
    return o_lat, o_ctx

def dn_output(o, gate, w_norm, dtype):
    b, t = o.shape[:2]
    z = gate.astype(jnp.float32).reshape(b, t, DN_HEADS, DN_DV)
    y = rms_norm(o, w_norm) * jax.nn.silu(z)
    return y.reshape(b, t, DN_V_W).astype(dtype)

def _heads(a, nh):
    return a.reshape(a.shape[:2] + (nh, ATT_HD))

def gqa_softmax(q, k, v):
    b, tq = q.shape[:2]
    qg = q.reshape(b, tq, ATT_KV_HEADS, ATT_GROUPS, ATT_HD)
    s = jnp.einsum('bqkgd,bskd->bkgqs', qg, k, preferred_element_type=jnp.float32) * (ATT_HD ** -0.5)
    p = jax.nn.softmax(s, axis=-1).astype(v.dtype)
    o = jnp.einsum('bkgqs,bskd->bqkgd', p, v)
    return o.reshape(b, tq, ATT_Q_W)

def blocked_attention(q, k, v):
    b, n = q.shape[:2]
    nb = n // Q_BLOCK
    qb = jnp.moveaxis(q.reshape(b, nb, Q_BLOCK, ATT_HEADS, ATT_HD), 1, 0)
    o = lax.map(lambda blk: gqa_softmax(blk, k, v), qb)
    return jnp.moveaxis(o, 0, 1).reshape(b, n, ATT_Q_W)

def hybrid_mixer(h, hc, w_in, w_out, conv_w, a_log, dt_bias, dn_norm, q_norm, k_norm, ctx_out):
    p = h @ w_in
    p_kv, p_q = p[..., :KV_COLS], p[..., KV_COLS:]
    if ctx_out:
        pc = hc @ w_in
        pc_kv, pc_q = pc[..., :KV_COLS], pc[..., KV_COLS:]
    else:
        pc_kv, pc_q = hc @ w_in[:, :KV_COLS], None
    lat_in = dn_prepare(p_kv, p_q, conv_w, a_log, dt_bias)
    ctx_in = dn_prepare(pc_kv, pc_q, conv_w, a_log, dt_bias)
    o_lat, o_ctx = bidir_deltanet(lat_in, ctx_in)
    a_lat = dn_output(o_lat, p_q[..., QO_DN_G:QO_ATT_Q], dn_norm, h.dtype)
    cos, sin = axial_rope(h.shape[1])
    q_lat = apply_rope(rms_norm(_heads(p_q[..., QO_ATT_Q:], ATT_HEADS), q_norm), cos, sin)
    k_lat = apply_rope(rms_norm(_heads(p_kv[..., OFF_ATT_K:OFF_ATT_V], ATT_KV_HEADS), k_norm), cos, sin)
    k_ctx = rms_norm(_heads(pc_kv[..., OFF_ATT_K:OFF_ATT_V], ATT_KV_HEADS), k_norm)
    v_ctx = _heads(pc_kv[..., OFF_ATT_V:], ATT_KV_HEADS)
    k_all = jnp.concatenate([k_ctx, k_lat], axis=1)
    v_all = jnp.concatenate([v_ctx, _heads(p_kv[..., OFF_ATT_V:], ATT_KV_HEADS)], axis=1)
    b_lat = blocked_attention(q_lat, k_all, v_all)
    y_lat = jnp.concatenate([a_lat, b_lat], axis=-1) @ w_out
    if not ctx_out:
        return y_lat, None
    a_ctx = dn_output(o_ctx, pc_q[..., QO_DN_G:QO_ATT_Q], dn_norm, hc.dtype)
    q_ctx = rms_norm(_heads(pc_q[..., QO_ATT_Q:], ATT_HEADS), q_norm)
    b_ctx = gqa_softmax(q_ctx, k_ctx, v_ctx)
    y_ctx = jnp.concatenate([a_ctx, b_ctx], axis=-1) @ w_out
    return y_lat, y_ctx

def short_conv_mixer(h, w_in, conv_w, w_out):
    gate_b, gate_c, xt = jnp.split(h @ w_in, 3, axis=-1)
    return (gate_b * dwconv(gate_c * xt, conv_w)) @ w_out

def conv_ffn(h, w_up, conv_w, w_down):
    a, v = jnp.split(h @ w_up, 2, axis=-1)
    return (jax.nn.silu(dwconv(a, conv_w)) * v) @ w_down

def setup_inputs(seed: int = 0) -> dict:
    key = jax.random.key(seed)
    ks = jax.random.split(key, 26)
    f32 = jnp.float32

    def nrm(k, shape, scale):
        return jax.random.normal(k, shape, f32) * scale

    def gain(k, shape):
        return 1.0 + 0.05 * jax.random.normal(k, shape, f32)

    dt = jnp.exp(jax.random.uniform(ks[14], (N_EVEN, DN_DIRS, DN_HEADS), f32,
                                    minval=math.log(1e-3), maxval=math.log(0.1)))
    return {
        'x': nrm(ks[0], (BATCH, SEQ, D_MODEL), 1.0),
        'c': nrm(ks[1], (BATCH, D_MODEL), 1.0),
        'ctx': nrm(ks[2], (BATCH, CTX_LEN, D_MODEL), 1.0),
        'c_ctx': nrm(ks[3], (D_MODEL,), 1.0),
        'mod_w': nrm(ks[4], (DEPTH, D_MODEL, 6 * D_MODEL), D_MODEL ** -0.5),
        'mod_b': nrm(ks[5], (DEPTH, 6 * D_MODEL), 0.02),
        'norm_mix_pre': gain(ks[6], (DEPTH, D_MODEL)),
        'norm_mix_post': gain(ks[7], (DEPTH, D_MODEL)),
        'norm_ffn_pre': gain(ks[8], (DEPTH, D_MODEL)),
        'norm_ffn_post': gain(ks[9], (DEPTH, D_MODEL)),
        'hyb_w_in': nrm(ks[10], (N_EVEN, D_MODEL, PROJ_COLS), D_MODEL ** -0.5),
        'hyb_w_out': nrm(ks[11], (N_EVEN, MIX_W, D_MODEL), MIX_W ** -0.5),
        'dn_conv_w': nrm(ks[12], (N_EVEN, CONV_K, DN_K_W + DN_V_W + DN_K_W), CONV_K ** -0.5),
        'dn_a_log': jnp.log(jax.random.uniform(ks[13], (N_EVEN, DN_DIRS, DN_HEADS), f32, minval=1.0, maxval=16.0)),
        'dn_dt_bias': dt + jnp.log(-jnp.expm1(-dt)),
        'dn_out_norm': gain(ks[15], (N_EVEN, DN_DV)),
        'att_q_norm': gain(ks[16], (N_EVEN, ATT_HD)),
        'att_k_norm': gain(ks[17], (N_EVEN, ATT_HD)),
        'sc_w_in': nrm(ks[18], (N_ODD, D_MODEL, 3 * SC_DIM), D_MODEL ** -0.5),
        'sc_conv_w': nrm(ks[19], (N_ODD, CONV_K, SC_DIM), CONV_K ** -0.5),
        'sc_w_out': nrm(ks[20], (N_ODD, SC_DIM, D_MODEL), SC_DIM ** -0.5),
        'ffn_w_up': nrm(ks[21], (DEPTH, D_MODEL, 2 * D_FF), D_MODEL ** -0.5),
        'ffn_conv_w': nrm(ks[22], (DEPTH, CONV_K, D_FF), CONV_K ** -0.5),
        'ffn_w_down': nrm(ks[23], (DEPTH, D_FF, D_MODEL), D_FF ** -0.5),
    }

def reference(x, c, ctx, c_ctx, mod_w, mod_b, norm_mix_pre, norm_mix_post, norm_ffn_pre, norm_ffn_post,
              hyb_w_in, hyb_w_out, dn_conv_w, dn_a_log, dn_dt_bias, dn_out_norm, att_q_norm, att_k_norm,
              sc_w_in, sc_conv_w, sc_w_out, ffn_w_up, ffn_conv_w, ffn_w_down):
    s_lat = jax.nn.silu(c)[:, None, :]
    s_ctx = jax.nn.silu(c_ctx)
    for layer in range(DEPTH):
        even = layer % 2 == 0
        ctx_live = any(j % 2 == 0 for j in range(layer + 1, DEPTH))
        mod = jnp.split(s_lat @ mod_w[layer] + mod_b[layer], 6, axis=-1)
        h = modulate(rms_norm(x, norm_mix_pre[layer]), mod[0], mod[1])
        if even or ctx_live:
            modc = jnp.split(s_ctx @ mod_w[layer] + mod_b[layer], 6, axis=-1)
            hc = modulate(rms_norm(ctx, norm_mix_pre[layer]), modc[0], modc[1])
        if even:
            e = layer // 2
            y, yc = hybrid_mixer(h, hc, hyb_w_in[e], hyb_w_out[e], dn_conv_w[e], dn_a_log[e], dn_dt_bias[e],
                                 dn_out_norm[e], att_q_norm[e], att_k_norm[e], ctx_live)
        else:
            o = layer // 2
            y = short_conv_mixer(h, sc_w_in[o], sc_conv_w[o], sc_w_out[o])
            yc = short_conv_mixer(hc, sc_w_in[o], sc_conv_w[o], sc_w_out[o]) if ctx_live else None
        x = x + mod[2] * rms_norm(y, norm_mix_post[layer])
        h = modulate(rms_norm(x, norm_ffn_pre[layer]), mod[3], mod[4])
        x = x + mod[5] * rms_norm(conv_ffn(h, ffn_w_up[layer], ffn_conv_w[layer], ffn_w_down[layer]),
                                  norm_ffn_post[layer])
        if ctx_live:
            ctx = ctx + modc[2] * rms_norm(yc, norm_mix_post[layer])
            hc = modulate(rms_norm(ctx, norm_ffn_pre[layer]), modc[3], modc[4])
            ctx = ctx + modc[5] * rms_norm(conv_ffn(hc, ffn_w_up[layer], ffn_conv_w[layer], ffn_w_down[layer]),
                                          norm_ffn_post[layer])
    return x


_drawn_inputs = setup_inputs


def setup_inputs(seed=0):
    import zlib

    import numpy as np

    out = dict(_drawn_inputs(seed))
    spreads = {}
    factors = {'att_q_norm': 8.0, 'att_k_norm': 8.0, 'dn_out_norm': 3.689}
    for name, (base, spread) in spreads.items():
        noise = np.random.default_rng([zlib.crc32(name.encode()), seed]).standard_normal(out[name].shape)
        drawn = base * np.exp(spread * noise) if base else spread * noise
        out[name] = jnp.asarray(drawn.astype(out[name].dtype))
    for name, factor in factors.items():
        out[name] = (out[name] * factor).astype(out[name].dtype)
    return out
```

```python
import numpy as np
from contextlib import ExitStack

import concourse.bass as bass
from concourse import mybir

F32 = mybir.dt.float32
F32R = mybir.dt.float32r
ALU = mybir.AluOpType
ACT = mybir.ActivationFunctionType
AX = mybir.AxisListType

P = 128
D_MODEL, SEQ, CTX = 1024, 512, 256
ALL = CTX + SEQ
EPS = 1e-6
KC = D_MODEL // P
D_FF = 2816
FC = D_FF // P
HEADS, DK = 4, 128
DIRS = 2
A_HEADS, A_KV, HD = 8, 2, 64
GRID_W, ROPE_THETA = 64, 10000.0
NT = ALL // P
NTC = CTX // P
NL = NT - NTC
LEVELS = 7
CHUNK_ORDER = [[0, 1, 2, 3, 4, 5], [1, 0, 5, 4, 3, 2]]
MODS = 6 * KC

C_ID, C_ONE, C_TRI, C_STRICT, C_LVL, C_BLK = 0, 1, 2, 4, 6, 6 + 2 * LEVELS
NCONST = C_BLK + 1

V_MIXPRE, V_MIXPOST, V_FFNPRE, V_FFNPOST = 0, 16, 32, 48
V_C, V_CCTX, V_DNOUT, V_QN, V_KN, V_SCCONV = 64, 72, 80, 81, 82, 83
V_ROWS = [V_SCCONV + 24, 96, 36, 66, 66]

O_ALPHA, O_AK = 1024, 1040
O_Q, O_G, O_AQ = 1296, 1808, 2320

UW = 256
U_HYB, U_WOUT, U_UP0, U_DOWN0 = 0, 12, 16, 38
U_SCIN, U_SCOUT, U_UP1, U_DOWN1 = 50, 62, 66, 88
U_END = 100
DCH = [(0, 8), (8, 7), (15, 7)]


def hybrid_trunk(nc, A, out):
    ctx = ExitStack()
    with ctx:
        base = [(nc.sbuf_base + 31) // 32 * 32]
        end = nc.sbuf_usable_end

        def place(name, cols, dt=F32, at=None):
            off = base[0] if at is None else at
            t = nc.alloc_sbuf_tensor_at(name, [P, cols], dt, offset=off)
            if at is None:
                base[0] += (cols * 4 + 31) // 32 * 32
            assert off + cols * 4 <= end, (name, off + cols * 4, end)
            return t

        def view(tile, pat, **k):
            return tile[:, :].rearrange(pat, **k)

        const = view(place("const", NCONST * P), "p (k n) -> p k n", n=P)
        x = view(place("x", KC * SEQ), "p (c t) -> p c t", t=SEQ)
        vec = view(place("vec", 5 * P), "p (k n) -> p k n", n=P)
        modv = view(place("modv", 2 * MODS * 2), "p (l m w) -> p l m w", l=2, w=2)
        cvec = view(place("cvec", KC * 2), "p (k w) -> p k w", w=2)
        pre_w = view(place("pre_w", 5 * KC), "p (k c) -> p k c", c=KC)
        post_w = view(place("post_w", 4 * KC), "p (k c) -> p k c", c=KC)
        eps = place("eps", 1)
        raw = [place(f"w_raw{i}", KC * UW) for i in range(2)]
        whi = [place(f"w_hi{i}", KC * UW, F32R) for i in range(2)]
        wlo = [place(f"w_lo{i}", KC * UW, F32R) for i in range(2)]
        tmp_at = base[0]
        tmp = [place(f"tmp{i}", SEQ) for i in range(4)]
        R = base[0]
        K = 1024

        def region(name, cols, at, dt=F32):
            return place(name, cols, dt, R + int(at * K))

        h_hi = view(region("h_hi", KC * SEQ, 88, F32R), "p (c t) -> p c t", t=SEQ)
        h_lo = view(region("h_lo", KC * SEQ, 104, F32R), "p (c t) -> p c t", t=SEQ)
        y = view(region("y", KC * SEQ, 88), "p (c t) -> p c t", t=SEQ)
        mid_hi = view(region("mid_hi", FC * SEQ, 0, F32R), "p (c t) -> p c t", t=SEQ)
        mid_lo = view(region("mid_lo", FC * SEQ, 44, F32R), "p (c t) -> p c t", t=SEQ)
        mix_hi = view(region("mix_hi", KC * SEQ, 0, F32R), "p (c t) -> p c t", t=SEQ)
        mix_lo = view(region("mix_lo", KC * SEQ, 16, F32R), "p (c t) -> p c t", t=SEQ)
        cv = view(region("cv", KC * SEQ, 32), "p (c t) -> p c t", t=SEQ)
        xin = view(region("xin", NL * D_MODEL, 0), "p (n c) -> p n c", c=D_MODEL)
        cin = view(region("cin", NTC * D_MODEL, 16), "p (n c) -> p n c", c=D_MODEL)
        vrow = view(region("vrow", 5 * P, 24), "p (k n) -> p k n", n=P)
        ctmp = [region(f"ctmp{i}", CTX, 48 + i) for i in range(4)]
        mraw_a = [view(region(f"mod_raw_a{i}", KC * P, 32 + 4 * i), "p (k n) -> p k n", n=P) for i in range(4)]
        mraw_b = [view(place(f"mod_raw_b{i}", KC * P, F32, tmp_at + 4 * K * i), "p (k n) -> p k n", n=P) for i in range(2)]
        hc_hi = view(region("hc_hi", KC * CTX, 57, F32R), "p (c t) -> p c t", t=CTX)
        hc_lo = view(region("hc_lo", KC * CTX, 65, F32R), "p (c t) -> p c t", t=CTX)
        xc = view(region("xc", KC * CTX, 73), "p (c t) -> p c t", t=CTX)
        kT = view(region("kT", HEADS * ALL, 0), "p (h t) -> p h t", t=ALL)
        qT = view(region("qT", HEADS * SEQ, 12), "p (h t) -> p h t", t=SEQ)
        vT = view(region("vT", HEADS * ALL, 20), "p (h t) -> p h t", t=ALL)
        gT = view(region("gT", HEADS * SEQ, 32), "p (h t) -> p h t", t=SEQ)
        aq = view(region("aq", HEADS * SEQ, 40), "p (h t) -> p h t", t=SEQ)
        ak = region("ak", ALL, 48)
        av = region("av", ALL, 51)
        ab = region("ab", ALL, 54)
        rsq = [region(f"rsq{i}", ALL, 57 + 3 * i) for i in range(2)]
        sqt = [region(f"sqt{i}", ALL, 63 + 3 * i) for i in range(2)]
        cosT = region("cosT", SEQ, 81)
        sinT = region("sinT", SEQ, 83)
        oT = view(region("oT", HEADS * SEQ, 57), "p (h t) -> p h t", t=SEQ)
        S = [view(region(f"S{d}", HEADS * P, 65 + 2 * d), "p (h t) -> p h t", t=P) for d in range(2)]
        smallv = view(region("dn_small", 8 * NT * 8, 69), "p (k n c) -> p k n c", k=8, c=8)
        abt = view(region("abt", NT * 16, 70.5), "p (n c) -> p n c", c=16)
        alog = region("alog", 16, 87)
        DT = []
        spots = [88 + 2 * i for i in range(12)], [112, 114, 116, 118] + [71 + 2 * i for i in range(8)]
        for d in range(2):
            t, free = {}, list(spots[d])
            for n in ("tu", "zs", "bl", "ta", "tb", "qg", "kbvn", "bv", "kd", "nw", "uf"):
                a0 = free.pop(0)
                w = HEADS * P
                if n == "tu":
                    free.pop(0)
                    w *= 2
                v = region(f"dn_{n}{d}", w, a0, F32R if n in ("tu", "zs", "bl") else F32)
                t[n] = view(v, "p (h t) -> p h t", t=P)
            DT.append(t)
        PTh = [view(region(f"PTh{i}", NT * SEQ, a0, F32R), "p (n t) -> p n t", t=SEQ) for i, a0 in enumerate((88, 57))]
        PTl = [view(region(f"PTl{i}", NT * SEQ, a0, F32R), "p (n t) -> p n t", t=SEQ) for i, a0 in enumerate((100, 69))]
        prob = [region(f"prob{i}", ALL, 81 + 3 * i) for i in range(2)]
        stat = region("att_stat", 4 * 32, 112)
        Vh = view(region("Vh", NT * P, 114, F32R), "p (n t) -> p n t", t=P)
        Vl = view(region("Vl", NT * P, 117, F32R), "p (n t) -> p n t", t=P)

        PS = ctx.enter_context(nc.psum_tensor("ps", [P, 8 * 512], F32))

        def bank(b, n=512, o=0):
            return PS[:, b * 512 + o:b * 512 + o + n]

        sems = {}

        def sem(name):
            if name not in sems:
                sems[name] = ctx.enter_context(nc.semaphore(name))
            return sems[name]

        def rep(eng, n, body, peel=0):
            for i in range(peel):
                body(i)
            if n - peel > 1:
                with eng.Fori(peel, n) as i:
                    body(i)
            elif n > peel:
                body(peel)

        def cnt(value):
            return max(value, 0) if isinstance(value, int) else value

        def rawcount(u, s):
            if isinstance(u, int):
                return sum(16 * (3 if 12 <= v < 16 else 4 if v in (10, 11) else 1) for v in range(s, u + 1, 2))
            return 8 * (u - s) + 16 + 112

        C = lambda k, n=1: const[:, k:k + n, :].rearrange("p k n -> p (k n)")
        ident, ones = C(C_ID), C(C_ONE)
        rv = [view(t, "p (k n) -> p k n", n=UW) for t in raw]
        wh = [view(t, "p (k n) -> p k n", n=UW) for t in whi]
        wl = [view(t, "p (k n) -> p k n", n=UW) for t in wlo]
        f32 = lambda a: a.bitcast(F32)
        ytile = lambda t: y[:, bass.ds(t, 1), :].rearrange("p c t -> p (c t)")

        def bc(a, n):
            return a.unsqueeze(2).to_broadcast([a.shape[0], a.shape[1], n])

        def bh(a, n):
            return a.unsqueeze(1).to_broadcast([a.shape[0], n, a.shape[1]])

        EVENTS = [(u, stream, r) for u in range(U_WOUT) for stream in (("ctx", "lat") if u < 6 else ("lat",))
                  for r in range(1 if u == 5 else 2)]
        EV = {(u, stream): n + 1 for n, (u, stream, r) in enumerate(EVENTS)}
        EV_LAT = [n + 1 for n, (u, stream, r) in enumerate(EVENTS) if stream == "lat"]
        LAT_BANK = {e[::2]: n % 4 for n, e in enumerate(e for e in EVENTS if e[1] == "lat")}
        N_CONV = 20

        def hyb_bank(u, stream, r):
            return bank(4 + u % 2, CTX, r * CTX) if stream == "ctx" else bank(LAT_BANK[u, r])

        def conv_jobs(u):
            if u < 4 or u in (6, 7):
                kind, first = (kT, 0) if u < 2 else (vT, 4) if u < 4 else (qT, 8)
                for stream in ("ctx", "lat") if u < 4 else ("lat",):
                    for r in range(2):
                        hd = 2 * (u % 2) + r
                        cols = slice(0, SEQ) if u > 4 else slice(0, CTX) if stream == "ctx" else slice(CTX, ALL)
                        yield stream, r, kind[:, hd, cols], hyb_bank(u, stream, r), first + hd

        items = ([(kT[:, h, :], ALL) for h in range(HEADS)] + [(qT[:, h, :], SEQ) for h in range(HEADS)]
                 + [(aq[:, h, :], SEQ) for h in range(HEADS)] + [(ak[:, :], ALL)])

        def rope_tile(e):
            return aq[:, e, :] if e < 4 else ak[:, CTX:ALL]

        block = ctx.enter_context(nc.Block())


        @block.sync
        def _(sp):
            w_in = A["hyb_w_in"][0].rearrange("(k p) n -> p k n", p=P)
            w_out = A["hyb_w_out"][0]
            sc_in = A["sc_w_in"][0].rearrange("(k p) n -> p k n", p=P)
            sc_out = A["sc_w_out"][0].rearrange("(k p) n -> p k n", p=P)
            up = [A["ffn_w_up"][f].rearrange("(k p) n -> p k n", p=P) for f in range(2)]
            down = [A["ffn_w_down"][f].rearrange("(k p) n -> p k n", p=P) for f in range(2)]

            sp.dma_start(const[:, :, :].rearrange("p k n -> p (k n)"), A["const"]).then_inc(sem("const_in"), 16)
            rows = lambda a: a.rearrange("l (c p) -> (l c) p", p=P)
            for k, r, a in ((0, V_MIXPRE, rows(A["norm_mix_pre"])), (0, V_MIXPOST, rows(A["norm_mix_post"])),
                            (0, V_FFNPRE, rows(A["norm_ffn_pre"])), (0, V_FFNPOST, rows(A["norm_ffn_post"])),
                            (0, V_C, rows(A["c"])), (0, V_CCTX, A["c_ctx"].rearrange("(c p) -> c p", p=P)),
                            (0, V_DNOUT, A["dn_out_norm"]), (0, V_SCCONV, rows(A["sc_conv_w"][0])),
                            (1, 0, rows(A["mod_b"])), (2, 0, rows(A["dn_conv_w"][0])),
                            (3, 0, rows(A["ffn_conv_w"][0])), (4, 0, rows(A["ffn_conv_w"][1]))):
                sp.dma_start(vrow[r:r + a.shape[0], k, :], a).then_inc(sem("vec_in"), 16)
            for half in range(2):
                sp.dma_start(vrow[V_QN:V_QN + 1, 0, half * HD:(half + 1) * HD], A["att_q_norm"]).then_inc(sem("vec_in"), 16)
                sp.dma_start(vrow[V_KN:V_KN + 1, 0, half * HD:(half + 1) * HD], A["att_k_norm"]).then_inc(sem("vec_in"), 16)
            sp.dma_start(cin[:, :, :], A["ctx"][0].rearrange("(n p) c -> p n c", p=P)).then_inc(sem("ctx_in"), 16)
            sp.dma_start(xin[:, :, :], A["x"][0].rearrange("(n p) c -> p n c", p=P)).then_inc(sem("x_in"), 16)

            def load_mod(m):
                src = A["mod_w"][m // MODS].rearrange("(k p) n -> p k n", p=P)[:, :, (m % MODS) * P:(m % MODS + 1) * P]
                if m < 16:
                    sp.wait_ge(sem("mod_done"), cnt(m - 3))
                    sp.dma_start(mraw_a[m % 4][:, :, :], src).then_inc(sem(f"mod_a{m % 4}"), 16)
                else:
                    if m >= 18:
                        sp.wait_ge(sem("mod_done"), cnt(m - 1))
                    sp.dma_start(mraw_b[m % 2][:, :, :], src).then_inc(sem(f"mod_b{m % 2}"), 16)

            def raw_free(u):
                sp.wait_ge(sem("w_lo"), cnt(u - 1))

            for m in range(4):
                load_mod(m)
            for u in range(2):
                sp.dma_start(rv[u][:, :, :], w_in[:, :, u * UW:(u + 1) * UW]).then_inc(sem(f"w_raw{u}"), 16)
            for m in range(4, 16):
                load_mod(m)
            sp.dma_start(cosT[:, :], A["cos"]).then_inc(sem("rope_in"), 16)
            sp.dma_start(sinT[:, :], A["sin"]).then_inc(sem("rope_in"), 16)
            sp.dma_start(alog[:, 0:8], A["dn_a_log"][0].rearrange("d h -> (d h)").unsqueeze(0).to_broadcast([P, 8])).then_inc(sem("gate_in"), 16)
            sp.dma_start(alog[:, 8:16], A["dn_dt_bias"][0].rearrange("d h -> (d h)").unsqueeze(0).to_broadcast([P, 8])).then_inc(sem("gate_in"), 16)
            for u in range(2, 12):
                s = u % 2
                raw_free(u)
                if u < 4:
                    sp.dma_start(rv[s][:, :, :], w_in[:, :, u * UW:(u + 1) * UW]).then_inc(sem(f"w_raw{s}"), 16)
                elif u == 4:
                    sp.dma_start(rv[s][:, :, :], w_in[:, :, O_AK:O_AK + UW]).then_inc(sem(f"w_raw{s}"), 16)
                elif u == 5:
                    sp.dma_start(rv[s][:, :, 0:P], w_in[:, :, O_ALPHA:O_ALPHA + P]).then_inc(sem(f"w_raw{s}"), 16)
                elif u < 8:
                    sp.dma_start(rv[s][:, :, :], w_in[:, :, O_Q + (u - 6) * UW:O_Q + (u - 5) * UW]).then_inc(sem(f"w_raw{s}"), 16)
                elif u < 10:
                    sp.dma_start(rv[s][:, :, :], w_in[:, :, O_G + (u - 8) * UW:O_G + (u - 7) * UW]).then_inc(sem(f"w_raw{s}"), 16)
                else:
                    for r in range(2):
                        for a in range(2):
                            o, to = O_AQ + a * 4 * HD + (2 * (u - 10) + r) * HD, r * P + a * HD
                            sp.dma_start(rv[s][:, :, to:to + HD], w_in[:, :, o:o + HD]).then_inc(sem(f"w_raw{s}"), 16)

            def load_wout(u):
                s, q = u % 2, u - U_WOUT
                raw_free(u)
                cols = slice(q * UW, (q + 1) * UW)
                sp.dma_start(rv[s][:, 0:4, :], w_out[0:512, cols].rearrange("(k p) n -> p k n", p=P)).then_inc(sem(f"w_raw{s}"), 16)
                for a in range(2):
                    part = w_out[512 + 256 * a:768 + 256 * a, cols]
                    sp.dma_start(rv[s][HD * a:HD * (a + 1), 4:8, :], part.rearrange("(t p) n -> p t n", p=HD)).then_inc(sem(f"w_raw{s}"), 16)

            load_wout(12)
            load_wout(13)
            sp.wait_ge(sem("h"), 16)
            for m in range(16, 2 * MODS):
                load_mod(m)
            load_wout(14)
            load_wout(15)

            def ffn_loads(f, U_UP, U_DOWN):
                def upb(i):
                    for part in range(2):
                        u = 2 * i + (U_UP + part)
                        raw_free(u)
                        o = i * UW
                        sp.dma_start(rv[part][:, :, :], up[f][:, :, bass.ds(o + part * D_FF, UW)]).then_inc(sem(f"w_raw{part}"), 16)
                rep(sp, FC // 2, upb)

                def downb(i):
                    for q in range(6):
                        u = 6 * i + (U_DOWN + q)
                        k0, nk = DCH[q % 3]
                        raw_free(u)
                        o = i * (2 * UW) + (q // 3) * UW
                        sp.dma_start(rv[q % 2][:, 0:nk, :], down[f][:, k0:k0 + nk, bass.ds(o, UW)]).then_inc(sem(f"w_raw{q % 2}"), 16)
                rep(sp, 2, downb)

            ffn_loads(0, U_UP0, U_DOWN0)

            def cxb(i):
                for part in range(2):
                    raw_free(2 * i + (U_SCIN + part))
                    sp.dma_start(rv[part][:, :, :], sc_in[:, :, bass.ds(i * UW + (1 + part) * D_MODEL, UW)]).then_inc(sem(f"w_raw{part}"), 16)
            rep(sp, 4, cxb)

            def sqb(src, U0):
                def body(i):
                    for s in range(2):
                        raw_free(2 * i + (U0 + s))
                        sp.dma_start(rv[s][:, :, :], src[:, :, bass.ds(i * (2 * UW) + s * UW, UW)]).then_inc(sem(f"w_raw{s}"), 16)
                rep(sp, 2, body)
            sqb(sc_in, U_SCIN + 8)
            sqb(sc_out, U_SCOUT)
            ffn_loads(1, U_UP1, U_DOWN1)
            for n in range(NL):
                sp.wait_ge(sem("out_ev_a"), n + 1)
                sp.wait_ge(sem("out_ev_d"), n + 1)
                sp.dma_start(out[0, n * P:(n + 1) * P, :], xin[:, n, :]).then_inc(sem("stored"), 16)
            sp.wait_ge(sem("stored"), 16 * NL)

        @block.tensor
        def _(pe):
            mm, tr = nc.tensor.matmul, nc.tensor.transpose

            def mm3(dst, cols, nk, xh, xl, s, k0=0, first=True, last=True):
                for k in range(nk):
                    hi, lo = cols(wh, k), cols(wl, k)
                    mm(dst, hi, xh[:, k0 + k, :], start=first and k == 0, stop=False)
                    mm(dst, hi, xl[:, k0 + k, :], start=False, stop=False)
                    i = mm(dst, lo, xh[:, k0 + k, :], start=False, stop=last and k == nk - 1)
                return i

            def mod_unit(m):
                if m < 16:
                    pe.wait_ge(sem(f"mod_a{m % 4}"), 16 * (m // 4 + 1))
                    w = mraw_a[m % 4]
                else:
                    pe.wait_ge(sem(f"mod_b{m % 2}"), cnt(16 * ((m - 16) // 2 + 1)))
                    w = mraw_b[m % 2]
                for k in range(KC):
                    i = mm(bank(7, 2, 2 * m), w[:, k, :], cvec[:, k, :], start=k == 0, stop=k == KC - 1)
                i.then_inc(sem("mod_done"), 1)

            def stat(idx, n):
                t4 = ctmp if idx == 0 else tmp
                pe.wait_ge(sem("sqadd"), KC * (idx + 1))
                mm(bank(6, n), ones, t4[2][:, 0:n], start=True, stop=True).then_inc(sem("stat"), 1)

            pe.wait_ge(sem("const_in"), 16)
            pe.wait_ge(sem("vec_in"), 16 * 16)
            for k, r in enumerate(V_ROWS):
                i = tr(bank(7 if k < 4 else 6, r, P * (k % 4)), vrow[0:r, k, :], const[0:r, C_ID, 0:r])
            i.then_inc(sem("vecT"), 1)
            pe.wait_ge(sem("ctx_in"), 16)
            for c in range(KC):
                if c % 2 == 0:
                    pe.wait_ge(sem("cev"), cnt(c // 2 - 1))
                for n in range(NTC):
                    i = tr(bank(4 + c // 2 % 2, P, (c % 2) * CTX + n * P), cin[:, n, c * P:(c + 1) * P], ident)
                if c % 2:
                    i.then_inc(sem("cT"), 1)
            pe.wait_ge(sem("x_in"), 16)
            for c in range(KC):
                pe.wait_ge(sem("xev"), cnt(c - 3))
                for n in range(NL):
                    i = tr(bank(c % 4, P, n * P), xin[:, n, c * P:(c + 1) * P], ident)
                i.then_inc(sem("xT"), 1)
            pe.wait_ge(sem("vec"), 1)
            pe.wait_ge(sem("cvec"), 2)
            for m in range(16):
                mod_unit(m)
            stat(0, CTX)
            pe.wait_ge(sem("sd"), 1)
            stat(1, SEQ)

            lat = 0
            pe.wait_ge(sem("h"), 2 * KC)
            for u in range(U_WOUT):
                s = u % 2
                tiles = 1 if u == 5 else 2
                cols = lambda w, k, r: w[s][:, k, r * P:(r + 1) * P]
                pe.wait_ge(sem("w_lo"), u + 1)
                if u < 6:
                    if u >= 2:
                        pe.wait_ge(sem("ev"), cnt(EV[u - 2, "ctx"]))
                    for r in range(tiles):
                        i = mm3(bank(4 + u % 2, CTX, r * CTX), lambda w, k: cols(w, k, r), KC, hc_hi, hc_lo, s)
                    i.then_inc(sem("ctx_tile" if u < 5 else "tile"), 1)
                for r in range(tiles):
                    if lat >= 4:
                        pe.wait_ge(sem("ev"), cnt(EV_LAT[lat - 4]))
                    i = mm3(bank(lat % 4), lambda w, k: cols(w, k, r), KC, h_hi, h_lo, s)
                    i.then_inc(sem("tile"), 1)
                    lat += 1

            for e in range(13):
                n = ALL if e < 4 or e == 12 else SEQ
                w = ones if e < 8 else C(C_BLK)
                pe.wait_ge(sem("nsq"), e + 1)
                pe.wait_ge(sem("nsd"), cnt(e - 1))
                b = 2 * (e % 2)
                i = mm(bank(b, 512), w, sqt[e % 2][:, 0:512], start=True, stop=True)
                if n > 512:
                    i = mm(bank(b + 1, n - 512), w, sqt[e % 2][:, 512:n], start=True, stop=True)
                i.then_inc(sem("nst"), 1)
            pe.wait_ge(sem("ev"), len(EVENTS))
            for n in range(NT):
                i = tr(bank(4, 16, 16 * n), ab[0:16, n * P:(n + 1) * P], const[0:16, C_ID, 0:16])
            i.then_inc(sem("abT"), 1)
            pe.wait_ge(sem("g"), 1)
            gm = smallv[:, 0].rearrange("p n c -> p (n c)")
            for j, w in enumerate((C(C_TRI), C(C_TRI + 1), ones)):
                i = mm(bank(5, 8 * NT, 64 * j), w, gm, start=True, stop=True)
            i.then_inc(sem("gsum"), 1)

            pe.wait_ge(sem("dn_ready"), 1)
            mods = 16
            for s in range(NT):
                for d in range(2):
                    k = 2 * s + d
                    n = CHUNK_ORDER[d][s]
                    T, b0 = DT[d], 3 * d
                    tok = slice(n * P, (n + 1) * P)
                    pe.wait_ge(sem("S"), cnt(2 * (s - 1) + d + 1 if s else 0))
                    pe.wait_ge(sem("vn"), cnt(2 * (s - 1) + d + 1 if s else 0))
                    for h in range(HEADS):
                        i = mm(bank(b0, P, h * P), smallv[:, 0, n, 4 * d + h:4 * d + h + 1].to_broadcast([P, P]),
                               C(C_TRI + d), start=True, stop=True)
                    i.then_inc(sem("gc"), 1)
                    for h in range(HEADS):
                        i = mm(bank(b0 + 1, P, h * P), kT[:, h, tok], kT[:, h, tok], start=True, stop=True)
                    i.then_inc(sem("G"), 1)
                    if n >= NTC:
                        ql = slice((n - NTC) * P, (n - NTC + 1) * P)
                        for h in range(HEADS):
                            i = mm(bank(b0 + 2, P, h * P), kT[:, h, tok], qT[:, h, ql], start=True, stop=True)
                        i.then_inc(sem("QK"), 1)
                for d in range(2):
                    k, n, b0 = 2 * s + d, CHUNK_ORDER[d][s], 3 * d
                    tok = slice(n * P, (n + 1) * P)
                    pe.wait_ge(sem("GA"), k + 1)
                    for h in range(HEADS):
                        i = tr(bank(b0 + 1, P, h * P), kT[:, h, tok], ident)
                    i.then_inc(sem("Ktr"), 1)
                    if n >= NTC:
                        pe.wait_ge(sem("QB"), cnt(k - 3))
                    for h in range(HEADS):
                        i = tr(bank(b0 + 2, P, h * P), vT[:, h, tok], ident)
                    i.then_inc(sem("Vtr"), 1)
                for l in range(LEVELS):
                    for d in range(2):
                        T, q = DT[d], (s * LEVELS + l) * 2 + d
                        pe.wait_ge(sem("Bl"), q + 1)
                        if l:
                            pe.wait_ge(sem("TU"), cnt(q - 1))
                        else:
                            pe.wait_ge(sem("TU0"), 2 * s + d + 1)
                            if CHUNK_ORDER[d][s] >= NTC:
                                pe.wait_ge(sem("egr"), cnt(2 * s + d - 3))
                        for h in range(HEADS):
                            i = mm(bank(3 * d, P, h * P), T["bl"][:, h, :], T["tu"][:, h, :], start=True, stop=True)
                        i.then_inc(sem("Z"), 1)
                    for d in range(2):
                        T, q, b0 = DT[d], (s * LEVELS + l) * 2 + d, 3 * d
                        pe.wait_ge(sem("Zs"), q + 1)
                        if l == 0:
                            pe.wait_ge(sem("bv"), 2 * s + d + 1)
                        for h in range(HEADS):
                            mm(bank(b0 + 1, P, h * P), T["tu"][:, 4 + h, :], T["zs"][:, h, :], start=True, stop=True)
                        for h in range(HEADS):
                            i = mm(bank(b0 + 2, P, h * P), T["zs"][:, h, :], T["tu"][:, 4 + h, :], start=True, stop=True)
                        i.then_inc(sem("dTU"), 1)
                    for _ in range(2):
                        if mods < 2 * MODS:
                            mod_unit(mods)
                            mods += 1
                for d in range(2):
                    T, k = DT[d], 2 * s + d
                    pe.wait_ge(sem("TU"), cnt((s + 1) * LEVELS * 2 - 1 + d))
                    pe.wait_ge(sem("L"), k + 1)
                    for h in range(HEADS):
                        i = mm(bank(3 * d, P, h * P), T["ta"][:, h, :], f32(T["tu"][:, h, :]), start=True, stop=True)
                    i.then_inc(sem("LU"), 1)
                for d in range(2):
                    T, k = DT[d], 2 * s + d
                    pe.wait_ge(sem("R2"), k + 1)
                    for h in range(HEADS):
                        i = mm(bank(3 * d + 1, P, h * P), T["tu"][:, 4 + h, :], T["bl"][:, h, :], start=True, stop=True)
                    i.then_inc(sem("dN"), 1)
                for d in range(2):
                    T, k = DT[d], 2 * s + d
                    pe.wait_ge(sem("Uf"), k + 1)
                    for h in range(HEADS):
                        i = mm(bank(3 * d + 2, P, h * P), T["kbvn"][:, h, :], T["uf"][:, h, :], start=True, stop=True)
                    i.then_inc(sem("WT"), 1)
                for d in range(2):
                    T, k = DT[d], 2 * s + d
                    pe.wait_ge(sem("nW"), k + 1)
                    for h in range(HEADS):
                        i = mm(bank(3 * d, P, h * P), T["uf"][:, h, :], T["bv"][:, h, :], start=True, stop=s == 0)
                        if s:
                            i = mm(bank(3 * d, P, h * P), T["nw"][:, h, :], S[d][:, h, :], start=False, stop=True)
                    i.then_inc(sem("vnp"), 1)
                for d in range(2):
                    T, k, n = DT[d], 2 * s + d, CHUNK_ORDER[d][s]
                    pe.wait_ge(sem("vn"), k + 1)
                    if n >= NTC:
                        pe.wait_ge(sem("intra"), cnt(k - 3))
                        pe.wait_ge(sem("qg"), cnt(k - 3))
                        for h in range(HEADS):
                            mm(bank(3 * d + 1, P, h * P), S[d][:, h, :], T["qg"][:, h, :], start=True, stop=False)
                            i = mm(bank(3 * d + 1, P, h * P), T["kbvn"][:, h, :], T["tb"][:, h, :], start=False, stop=True)
                        i.then_inc(sem("o"), 1)
                    for h in range(HEADS):
                        i = mm(bank(3 * d + 2, P, h * P), T["kd"][:, h, :], T["kbvn"][:, h, :], start=True, stop=True)
                    i.then_inc(sem("Sp"), 1)
            assert mods == 2 * MODS
            for h in range(HEADS):
                pe.wait_ge(sem("osq"), h + 1)
                pe.wait_ge(sem("osd"), cnt(h - 1))
                mm(bank(h % 2), ones, tmp[h % 2][:, :], start=True, stop=True).then_inc(sem("ost"), 1)
            for n in range(NT):
                i = tr(bank(2 + n // 4, P, P * (n % 4)), av[:, n * P:(n + 1) * P], ident)
            i.then_inc(sem("Vatr"), 1)

            NQ = SEQ // P

            def turn(i):
                pe.wait_ge(sem("Pn"), i + 1)
                pe.wait_ge(sem("PT"), i)
                for n in range(NT):
                    j = tr(bank(4 + n // 4, P, P * (n % 4)), prob[i % 2][:, n * P:(n + 1) * P], ident)
                j.then_inc(sem("Ptr"), 1)

            def values(hh):
                pe.wait_ge(sem("PT"), NQ * (hh + 1))
                if hh >= 2:
                    pe.wait_ge(sem("mix0"), cnt(HEADS + hh - 1))
                b = bank(6 + hh % 2)
                for n in range(NT):
                    mm(b, Vh[:, n, :], PTh[hh % 2][:, n, :], start=n == 0, stop=False)
                    mm(b, Vh[:, n, :], PTl[hh % 2][:, n, :], start=False, stop=False)
                    j = mm(b, Vl[:, n, :], PTh[hh % 2][:, n, :], start=False, stop=n == NT - 1)
                j.then_inc(sem("pv"), 1)

            pe.wait_ge(sem("Va"), 1)
            pe.wait_ge(sem("osd"), HEADS)
            pe.wait_ge(sem("modv"), 2)
            for i in range(A_HEADS * NQ + 2):
                if i < A_HEADS * NQ:
                    hh, qt = divmod(i, NQ)
                    t, half = hh % 4, hh // 4
                    r = slice(HD * half, HD * (half + 1))
                    pe.wait_ge(sem("expd"), cnt(i - 1))
                    b = 2 * (i % 2)
                    mm(bank(b), aq[r, t, qt * P:(qt + 1) * P], ak[r, 0:512], start=True, stop=True)
                    mm(bank(b + 1, CTX), aq[r, t, qt * P:(qt + 1) * P], ak[r, 512:768], start=True, stop=True).then_inc(sem("sc"), 1)
                if 1 <= i <= A_HEADS * NQ:
                    turn(i - 1)
                if i >= NQ + 1 and (i - NQ - 1) % NQ == 0:
                    values((i - NQ - 1) // NQ)

            tcol = lambda r: (lambda w, k: w[slot[0]][:, k, r * P:(r + 1) * P])
            slot = [0]

            def out_units(u0, yq):
                def body(i):
                    for s in range(2):
                        slot[0] = s
                        pe.wait_ge(sem("w_lo"), 2 * i + (u0 + s + 1))
                        for r in range(2):
                            t = 4 * i + (2 * s + r)
                            pe.wait_ge(sem("yev"), cnt(t + (8 * yq - 3)))
                            mm3(bank(2 * s + r), tcol(r), KC, mix_hi, mix_lo, s).then_inc(sem("tile"), 1)
                rep(pe, 2, body, peel=yq == 0)

            def ffn(f, U_UP, U_DOWN, yq):
                def up_pair(i, par, j0):
                    for part in range(2):
                        slot[0] = part
                        pe.wait_ge(sem("w_lo"), 2 * i + (U_UP + 2 * j0 + part + 1))
                        for r in range(2):
                            pe.wait_ge(sem(("g" if part else "c3") + "_free"), cnt(2 * i + (FC * f + 2 * j0 + r - 3)))
                            mm3(bank(4 * par + 2 * part + r), tcol(r), KC, h_hi, h_lo, part).then_inc(sem("tile"), 1)

                def up4(i):
                    for par in range(2):
                        up_pair(2 * i, par, par)
                rep(pe, FC // 4, up4, peel=f == 0)
                up_pair(0, 0, FC // 2 - 1)
                pe.wait_ge(sem("mid"), FC * (f + 1))

                def down2(i):
                    for q in range(6):
                        slot[0] = q % 2
                        k0, nk = DCH[q % 3]
                        p = q // 3
                        pe.wait_ge(sem("w_lo"), 6 * i + (U_DOWN + q + 1))
                        for r in range(2):
                            if q % 3 == 0:
                                t = 4 * i + (2 * p + r)
                                pe.wait_ge(sem("yev"), cnt(t + (8 * yq - 3)))
                            mm3(bank(2 * p + r), tcol(r), nk, mid_hi, mid_lo, q % 2, k0,
                                    q % 3 == 0, q % 3 == 2).then_inc(sem("tile"), 1)
                rep(pe, 2, down2)

            def boundary(idx):
                stat(idx, SEQ)
                if idx < 8:
                    stat(idx + 1, SEQ)
                    pe.wait_ge(sem("h"), KC * ((idx + 1) // 2 + 2))

            pe.wait_ge(sem("mix0"), HEADS + A_HEADS)
            out_units(U_WOUT, 0)
            boundary(2)
            ffn(0, U_UP0, U_DOWN0, 1)
            boundary(4)

            def cx(i, par, j0):
                for part in range(2):
                    slot[0] = part
                    pe.wait_ge(sem("w_lo"), 2 * i + (U_SCIN + 2 * j0 + part + 1))
                    for r in range(2):
                        pe.wait_ge(sem("scu" if part else "scc"), cnt(2 * i + (2 * j0 + r - 3)))
                        mm3(bank(4 * par + 2 * part + r), tcol(r), KC, h_hi, h_lo, part).then_inc(sem("tile"), 1)

            def cx2(i):
                for par in range(2):
                    cx(2 * i, par, par)
            rep(pe, 2, cx2, peel=1)
            pe.wait_ge(sem("scu"), KC)

            def gate_b(i):
                for s in range(2):
                    slot[0] = s
                    pe.wait_ge(sem("w_lo"), 2 * i + (U_SCIN + 8 + s + 1))
                    for r in range(2):
                        pe.wait_ge(sem("scb"), cnt(4 * i + (2 * s + r - 3)))
                        mm3(bank(2 * s + r), tcol(r), KC, h_hi, h_lo, s).then_inc(sem("tile"), 1)
            rep(pe, 2, gate_b, peel=1)
            pe.wait_ge(sem("mix1"), KC)
            out_units(U_SCOUT, 2)
            boundary(6)
            ffn(1, U_UP1, U_DOWN1, 3)
            boundary(8)
            pe.wait_ge(sem("x_new"), 4 * KC)
            for n in range(NL):
                for half in range(2):
                    for c in range(4):
                        i = tr(bank(2 * n + half, P, c * P), x[:, 4 * half + c, n * P:(n + 1) * P], ident)
                    i.then_inc(sem("out_T"), 1)

        @block.scalar
        def _(act):
            def split_hi(u, s):
                act.wait_ge(sem(f"w_raw{s}"), rawcount(u, s))
                act.wait_ge(sem("tile"), cnt(2 * u - 2))
                nc.scalar.activation(whi[s][:, :], raw[s][:, :], ACT.Copy).then_inc(sem("w_hi"), 1)

            def squares(idx, src, n, waits):
                for c in range(KC):
                    waits(c)
                    act.wait_ge(sem("sqadd"), cnt(KC * idx + c - 1))
                    nc.scalar.activation((ctmp if idx == 0 else tmp)[c % 2][:, 0:n], src(c), ACT.Square).then_inc(sem("sq"), 1)

            def deviation(idx, n):
                act.wait_ge(sem("stat"), idx + 1)
                nc.scalar.activation((ctmp if idx == 0 else tmp)[3][:, 0:n], bank(6, n), ACT.Sqrt, scale=1.0 / D_MODEL, bias=eps[:, :]).then_inc(sem("sd"), 1)

            def h_high(hb, out_, n, shift):
                for c in range(KC):
                    act.wait_ge(sem("t"), KC * hb + c + 1)
                    nc.scalar.activation(out_[:, c, :], (ctmp if hb == 0 else tmp)[c % 2][:, 0:n], ACT.Identity, bias=shift(c)).then_inc(sem("h_hi"), 1)

            act.wait_ge(sem("vec"), 1)
            for w, row in enumerate((V_C, V_CCTX)):
                nc.scalar.activation(cvec[:, :, w], vec[:, 0, row:row + KC], ACT.Silu).then_inc(sem("cvec"), 1)
            squares(0, lambda c: xc[:, c, :], CTX, lambda c: act.wait_ge(sem("cev"), c // 2 + 1))
            deviation(0, CTX)
            squares(1, lambda c: x[:, c, :], SEQ, lambda c: (act.wait_ge(sem("xev"), c + 1), act.wait_ge(sem("stat"), 1)))
            deviation(1, SEQ)
            split_hi(0, 0)
            split_hi(1, 1)
            h_high(0, hc_hi, CTX, lambda c: modv[:, 0, c, 1:2])
            h_high(1, h_hi, SEQ, lambda c: modv[:, 0, c, 0:1])

            dnw = lambda k, j: vec[:, 2, 12 * k + j:12 * k + j + 1]
            for u in range(U_WOUT):
                act.wait_ge(sem("tile"), 2 * u + 2)
                split_hi(u + 2, u % 2)
                jobs = list(conv_jobs(u))
                for stream, r, dst, ps, j in jobs:
                    if stream == "ctx":
                        act.wait_ge(sem("ctx_tile"), u + 1)
                    else:
                        act.wait_ge(sem("tile"), 2 * u + r + 1)
                    nc.scalar.activation(dst, ps, ACT.Copy, scale=dnw(1, j)).then_inc(sem("cv1"), 1)
                for stream, r, dst, _, _ in jobs:
                    act.wait_ge(sem("ev"), EVENTS.index((u, stream, r)) + 1)
                    nc.scalar.activation(dst, dst, ACT.Silu).then_inc(sem("cvs"), 1)
                if u in (8, 9):
                    for r in range(2):
                        hd = 2 * (u - 8) + r
                        act.wait_ge(sem("ev"), EVENTS.index((u, "lat", r)) + 1)
                        nc.scalar.activation(gT[:, hd, :], gT[:, hd, :], ACT.Silu).then_inc(sem("gate"), 1)

            def item_sd(e):
                n = items[e][1]
                act.wait_ge(sem("nst"), e + 1)
                act.wait_ge(sem("nrm"), cnt(e - 1))
                b = 2 * (e % 2)
                nc.scalar.activation(rsq[e % 2][:, 0:n], bank(b, n), ACT.Sqrt, scale=1.0 if e < 8 else 1.0 / HD, bias=eps[:, :]).then_inc(sem("nsd"), 1)
            for e, (t, n) in enumerate(items):
                act.wait_ge(sem("cvs"), N_CONV)
                act.wait_ge(sem("ev"), len(EVENTS))
                act.wait_ge(sem("nst"), cnt(e - 1))
                nc.scalar.activation(sqt[e % 2][:, 0:n], t, ACT.Square).then_inc(sem("nsq"), 1)
                if e:
                    item_sd(e - 1)
            item_sd(len(items) - 1)
            z, e1, rr = smallv[:, 7], smallv[:, 6], smallv[:, 5]
            act.wait_ge(sem("abt"), 1)
            nc.scalar.activation(smallv[:, 1], abt[:, :, 8:16], ACT.Sigmoid).then_inc(sem("beta"), 1)
            act.wait_ge(sem("z"), 1)
            nc.scalar.activation(e1, z, ACT.Abs).then_inc(sem("gate_a"), 1)
            act.wait_ge(sem("gate_a"), 1)
            nc.scalar.activation(e1, e1, ACT.Exp, scale=-1.0).then_inc(sem("gate_a"), 1)
            act.wait_ge(sem("gate_a"), 2)
            nc.scalar.activation(e1, e1, ACT.Ln, bias=const[:, C_ONE, 0:1]).then_inc(sem("gate_a"), 1)
            act.wait_ge(sem("gate_in"), 32)
            nc.scalar.activation(alog[:, 0:8], alog[:, 0:8], ACT.Exp).then_inc(sem("ea"), 1)
            act.wait_ge(sem("gcv"), 3)
            for j in range(3):
                nc.scalar.activation(smallv[:, 3 + j], smallv[:, 3 + j], ACT.Exp).then_inc(sem("ge"), 1)

            for s in range(NT):
                for d in range(2):
                    k, n, T = 2 * s + d, CHUNK_ORDER[d][s], DT[d]
                    act.wait_ge(sem("dA"), k + 1)
                    nc.scalar.activation(T["ta"][:, :, :], T["ta"][:, :, :], ACT.Exp).then_inc(sem("EA"), 1)
                    if n >= NTC:
                        act.wait_ge(sem("dB"), cnt(k - 3))
                        nc.scalar.activation(T["tb"][:, :, :], T["tb"][:, :, :], ACT.Exp).then_inc(sem("EB"), 1)
                        nc.scalar.activation(T["kbvn"][:, :, :].rearrange("p h t -> p (h t)"), bank(3 * d), ACT.Exp).then_inc(sem("egr"), 1)
                for l in range(LEVELS):
                    for d in range(2):
                        T, q = DT[d], (s * LEVELS + l) * 2 + d
                        act.wait_ge(sem("Z"), q + 1)
                        nc.scalar.activation(T["zs"][:, :, :].rearrange("p h t -> p (h t)"), bank(3 * d), ACT.Copy).then_inc(sem("Zs"), 1)
                for d in range(2):
                    T, k = DT[d], 2 * s + d
                    act.wait_ge(sem("WT"), k + 1)
                    nc.scalar.activation(T["nw"][:, :, :].rearrange("p h t -> p (h t)"), bank(3 * d + 2), ACT.Copy, scale=-1.0).then_inc(sem("nW"), 1)
                for d in range(2):
                    T, k = DT[d], 2 * s + d
                    act.wait_ge(sem("vnp"), k + 1)
                    nc.scalar.activation(T["kbvn"][:, :, :].rearrange("p h t -> p (h t)"), bank(3 * d), ACT.Copy).then_inc(sem("vn"), 1)
            for h in range(HEADS):
                act.wait_ge(sem("oe"), 8)
                act.wait_ge(sem("ost"), cnt(h - 1))
                act.wait_ge(sem("mod_done"), 2 * MODS)
                nc.scalar.activation(tmp[h % 2][:, :], oT[:, h, :], ACT.Square).then_inc(sem("osq"), 1)
                act.wait_ge(sem("ost"), h + 1)
                act.wait_ge(sem("on"), cnt(h - 1))
                nc.scalar.activation(tmp[2 + h % 2][:, :], bank(h % 2), ACT.Sqrt, scale=1.0 / DK, bias=eps[:, :]).then_inc(sem("osd"), 1)
            for h in range(HEADS):
                act.wait_ge(sem("on"), h + 1)
                nc.scalar.activation(mix_hi[:, h, :], oT[:, h, :], ACT.Copy).then_inc(sem("on_hi"), 1)
            act.wait_ge(sem("Vatr"), 1)
            nc.scalar.activation(Vh[:, :, :].rearrange("p n t -> p (n t)"), bank(2, ALL), ACT.Copy).then_inc(sem("Vah"), 1)

            NQ = SEQ // P

            def turn_hi(i):
                hh, qt = divmod(i, NQ)
                act.wait_ge(sem("Ptr"), i + 1)
                if hh >= 2:
                    act.wait_ge(sem("pv"), cnt(hh - 1))
                nc.scalar.activation(PTh[hh % 2][:, :, qt * P:(qt + 1) * P], bank(4, ALL).rearrange("p (n t) -> p n t", t=P), ACT.Copy).then_inc(sem("PTh"), 1)

            def head_hi(hh):
                half, t = hh // 4, hh % 4
                r = slice(HD * half, HD * (half + 1))
                act.wait_ge(sem("pv"), hh + 1)
                nc.scalar.activation(mix_hi[r, 4 + t, :], bank(6 + hh % 2)[r], ACT.Copy).then_inc(sem("ahh"), 1)

            for i in range(A_HEADS * NQ + 2):
                if i < A_HEADS * NQ:
                    act.wait_ge(sem("mx"), i + 1)
                    act.wait_ge(sem("Ptr"), cnt(i - 1))
                    nc.scalar.activation(prob[i % 2][:, :], bank(2 * (i % 2), ALL), ACT.Exp, scale=HD ** -0.5, bias=stat[:, 32 + i:33 + i], accum_out=stat[:, 64 + i:65 + i]).then_inc(sem("expd"), 1)
                if 1 <= i <= A_HEADS * NQ:
                    turn_hi(i - 1)
                if i >= NQ + 1 and (i - NQ - 1) % NQ == 0:
                    head_hi((i - NQ - 1) // NQ)

            def y_squares(u0, yq):
                def body(i):
                    for s in range(2):
                        act.wait_ge(sem("tile"), 4 * i + (2 * u0 + 2 * s + 2))
                        split_hi(2 * i + (u0 + s + 2), s)
                        for r in range(2):
                            t = 4 * i + (2 * s + r)
                            act.wait_ge(sem("sqadd"), cnt(t + (8 * (2 + 2 * yq) - 1)))
                            act.wait_ge(sem("yev"), t + (8 * yq + 1))
                            nc.scalar.activation(tmp[r][:, :], ytile(t), ACT.Square).then_inc(sem("sq"), 1)
                rep(act, 2, body)

            def boundary(idx, hb, shift):
                deviation(idx, SEQ)
                if idx < 8:
                    act.wait_ge(sem("x_new"), cnt(KC * ((idx - 2) // 2) + 1))
                    squares(idx + 1, lambda c: x[:, c, :], SEQ,
                            lambda c: act.wait_ge(sem("x_new"), cnt(KC * ((idx - 2) // 2) + c + 1)))
                    deviation(idx + 1, SEQ)
                    h_high(hb, h_hi, SEQ, shift)

            def ffn(f, U_UP, U_DOWN, yq):
                cw = lambda k, j: vec[:, 3 + f, bass.ds(j + 22 * k, 1)]

                def up_pair(i, par, j0):
                    tl = lambda r: 2 * i + (FC * f + 2 * j0 + r)
                    u = 2 * i + (U_UP + 2 * j0)
                    act.wait_ge(sem("tile"), 4 * i + (2 * (U_UP + 2 * j0) + 2))
                    split_hi(u + 2, 0)
                    for r in range(2):
                        act.wait_ge(sem("mid"), cnt(tl(r) - 3))
                        nc.scalar.activation(tmp[2 * par + r][:, :], bank(4 * par + r), ACT.Copy, scale=cw(1, 2 * i + (2 * j0 + r))).then_inc(sem("c1"), 1)
                    for r in range(2):
                        act.wait_ge(sem("c3_free"), tl(r) + 1)
                        nc.scalar.activation(tmp[2 * par + r][:, :], tmp[2 * par + r][:, :], ACT.Silu).then_inc(sem("sg"), 1)
                    act.wait_ge(sem("tile"), 4 * i + (2 * (U_UP + 2 * j0) + 4))
                    split_hi(u + 3, 1)
                    for r in range(2):
                        act.wait_ge(sem("g_free"), tl(r) + 1)
                        nc.scalar.activation(mid_hi[:, bass.ds(2 * i + (2 * j0 + r), 1), :].rearrange("p c t -> p (c t)"), tmp[2 * par + r][:, :], ACT.Copy).then_inc(sem("ghi"), 1)

                def up4(i):
                    for par in range(2):
                        up_pair(2 * i, par, par)
                rep(act, FC // 4, up4, peel=f == 0)
                up_pair(0, 0, FC // 2 - 1)

                def down2(i, last=False):
                    for q in range(6):
                        act.wait_ge(sem("tile"), 12 * i + (2 * (U_DOWN + q) + 2))
                        if not (last and q >= 4):
                            split_hi(6 * i + (U_DOWN + q + 2), q % 2)
                        if q % 3 == 2:
                            for r in range(2):
                                t = 4 * i + (2 * (q // 3) + r)
                                act.wait_ge(sem("sqadd"), cnt(t + (8 * (2 + 2 * yq) - 1)))
                                act.wait_ge(sem("yev"), t + (8 * yq + 1))
                                nc.scalar.activation(tmp[r][:, :], ytile(t), ACT.Square).then_inc(sem("sq"), 1)
                if f == 0:
                    rep(act, 2, down2)
                else:
                    down2(0)
                    down2(1, True)

            y_squares(U_WOUT, 0)
            boundary(2, 2, lambda c: modv[:, 0, 3 * KC + c, 0:1])
            ffn(0, U_UP0, U_DOWN0, 1)
            boundary(4, 3, lambda c: modv[:, 1, c, 0:1])

            scw = lambda k, j: vec[:, 0, bass.ds(j + (V_SCCONV + 8 * k), 1)]

            def cx(i, par, j0):
                tl = lambda r: 2 * i + (2 * j0 + r)
                for part in range(2):
                    act.wait_ge(sem("tile"), 4 * i + (2 * (U_SCIN + 2 * j0 + part) + 2))
                    split_hi(2 * i + (U_SCIN + 2 * j0 + part + 2), part)
                    for r in range(2):
                        if part == 0:
                            act.wait_ge(sem("scv"), cnt(tl(r) - 3))
                            nc.scalar.activation(tmp[2 * par + r][:, :], bank(4 * par + r), ACT.Copy).then_inc(sem("scc"), 1)
                        else:
                            act.wait_ge(sem("scu"), tl(r) + 1)
                            nc.scalar.activation(cv[:, bass.ds(tl(r), 1), :].rearrange("p c t -> p (c t)"), tmp[2 * par + r][:, :], ACT.Copy, scale=scw(1, tl(r))).then_inc(sem("scv1"), 1)

            def cx2(i):
                for par in range(2):
                    cx(2 * i, par, par)
            rep(act, 2, cx2, peel=1)

            def gate_b(i):
                for s in range(2):
                    act.wait_ge(sem("tile"), 4 * i + (2 * (U_SCIN + 8 + s) + 2))
                    split_hi(2 * i + (U_SCIN + 8 + s + 2), s)
                    for r in range(2):
                        t = 4 * i + (2 * s + r)
                        act.wait_ge(sem("scb"), t + 1)
                        nc.scalar.activation(mix_hi[:, bass.ds(t, 1), :].rearrange("p c t -> p (c t)"), tmp[2 * s + r][:, :], ACT.Copy).then_inc(sem("mhi"), 1)
            rep(act, 2, gate_b)
            y_squares(U_SCOUT, 2)
            boundary(6, 4, lambda c: modv[:, 1, 3 * KC + c, 0:1])
            ffn(1, U_UP1, U_DOWN1, 3)
            boundary(8, 0, None)
            for n in range(NL):
                act.wait_ge(sem("out_T"), 2 * n + 1)
                nc.scalar.activation(xin[:, n, 0:512], bank(2 * n), ACT.Copy).then_inc(sem("out_ev_a"), 1)


        @block.vector
        def _(dve):
            V = nc.vector

            def split_lo(u, s):
                dve.wait_ge(sem("w_hi"), u + 1)
                V.tensor_tensor(wlo[s][:, :], raw[s][:, :], f32(whi[s][:, :]), ALU.subtract).then_inc(sem("w_lo"), 1)

            def rstd(idx, t4, n):
                dve.wait_ge(sem("sd"), idx + 1)
                V.reciprocal(t4[3][:, 0:n], t4[3][:, 0:n]).then_inc(sem("rstd"), 1)
                dve.wait_ge(sem("rstd"), idx + 1)

            def apply_pre(hb, X, t4, n, pre, shift, hi, lo):
                def low(c):
                    dve.wait_ge(sem("h_hi"), KC * hb + c + 1)
                    V.scalar_tensor_tensor(out=lo[:, c, :], in0=t4[c % 2][:, 0:n], scalar=shift(c),
                                               in1=f32(hi[:, c, :]), op0=ALU.add, op1=ALU.subtract).then_inc(sem("h"), 1)
                for c in range(KC):
                    if c >= 2:
                        low(c - 2)
                        dve.wait_ge(sem("h"), cnt(KC * hb + c - 1))
                    V.scalar_tensor_tensor(out=t4[c % 2][:, 0:n], in0=X(c), scalar=pre_w[:, pre, c:c + 1],
                                               in1=t4[3][:, 0:n], op0=ALU.mult, op1=ALU.mult).then_inc(sem("t"), 1)
                low(KC - 2)
                low(KC - 1)

            V.memset(eps[:, :], EPS)
            dve.wait_ge(sem("vecT"), 1)
            for k, r in enumerate(V_ROWS):
                i = V.tensor_copy(vec[:, k, 0:r], bank(7 if k < 4 else 6, r, P * (k % 4)))
            i.then_inc(sem("vec"), 1)
            for p in range(KC // 2):
                dve.wait_ge(sem("cT"), p + 1)
                V.tensor_copy(xc[:, 2 * p:2 * p + 2, :].rearrange("p c t -> p (c t)"), bank(4 + p % 2)).then_inc(sem("cev"), 1)
            for c in range(KC):
                dve.wait_ge(sem("xT"), c + 1)
                V.tensor_copy(x[:, c, :], bank(c % 4)).then_inc(sem("xev"), 1)
            rstd(0, ctmp, CTX)
            rstd(1, tmp, SEQ)
            dve.wait_ge(sem("mod_done"), 16)
            dve.wait_ge(sem("vec"), 1)
            V.tensor_tensor(modv[:, 0, 0:16, :], bank(7, 32).rearrange("p (m w) -> p m w", w=2),
                                bc(vec[:, 1, 0:16], 2), ALU.add).then_inc(sem("modv"), 1)
            dve.wait_ge(sem("modv"), 1)

            def pre_weights(k, l, m, w, row):
                return V.scalar_tensor_tensor(out=pre_w[:, k, :], in0=modv[:, l, m:m + KC, w], scalar=1.0,
                                              in1=vec[:, 0, row:row + KC], op0=ALU.add, op1=ALU.mult)
            pre_weights(0, 0, KC, 0, V_MIXPRE)
            pre_weights(4, 0, KC, 1, V_MIXPRE).then_inc(sem("norm_w"), 1)
            dve.wait_ge(sem("norm_w"), 1)
            split_lo(0, 0)
            split_lo(1, 1)
            apply_pre(0, lambda c: xc[:, c, :], ctmp, CTX, 4, lambda c: modv[:, 0, c, 1:2], hc_hi, hc_lo)
            apply_pre(1, lambda c: x[:, c, :], tmp, SEQ, 0, lambda c: modv[:, 0, c, 0:1], h_hi, h_lo)

            dnw = lambda k, j: vec[:, 2, 12 * k + j:12 * k + j + 1]
            n1 = n2 = 0
            for u in range(U_WOUT):
                split_lo(u + 2, u % 2)
                jobs = list(conv_jobs(u))
                for stream in ("ctx", "lat"):
                    mine = [j for j in jobs if j[0] == stream]
                    for _, r, dst, ps, j in mine:
                        dve.wait_ge(sem("cv1"), cnt(n1 + 2 - r if stream == "ctx" else n1 + 1))
                        n = dst.shape[1]
                        V.scalar_tensor_tensor(out=dst[:, 1:n], in0=ps[:, 0:n - 1], scalar=dnw(0, j), in1=dst[:, 1:n],
                                                   op0=ALU.mult, op1=ALU.add).then_inc(sem("cv2"), 1)
                        n1 += 1
                    for _, r, dst, ps, j in mine:
                        dve.wait_ge(sem("cv2"), n2 + 1)
                        n = dst.shape[1]
                        V.scalar_tensor_tensor(out=dst[:, 0:n - 1], in0=ps[:, 1:n], scalar=dnw(2, j),
                                                   in1=dst[:, 0:n - 1], op0=ALU.mult, op1=ALU.add).then_inc(sem("ev"), 1)
                        n2 += 1
                if not jobs:
                    for e in EVENTS:
                        if e[0] != u:
                            continue
                        _, stream, r = e
                        cols = slice(0, CTX) if stream == "ctx" else slice(CTX, ALL)
                        ps = hyb_bank(*e)
                        if stream == "ctx":
                            dve.wait_ge(sem("ctx_tile" if u < 5 else "tile"), 5 if u < 5 else 11)
                        else:
                            dve.wait_ge(sem("tile"), 12 if u == 5 else 2 * u + r + 1)
                        if u == 4:
                            dst = (ak, av)[r][:, cols]
                        elif u == 5:
                            dst, ps = ab[0:16, cols], ps[0:16]
                        elif u < 10:
                            dst = gT[:, 2 * (u - 8) + r, :]
                        else:
                            dst = aq[:, 2 * (u - 10) + r, :]
                        V.tensor_copy(dst, ps).then_inc(sem("ev"), 1)
            for e, (t, n) in enumerate(items):
                dve.wait_ge(sem("nsd"), e + 1)
                V.reciprocal(rsq[e % 2][:, 0:n], rsq[e % 2][:, 0:n]).then_inc(sem("nrc"), 1)
                dve.wait_ge(sem("nrc"), e + 1)
                if e < 4:
                    i = V.tensor_tensor(t, t, rsq[e % 2][:, 0:n], ALU.mult)
                else:
                    w = DK ** -0.5 if e < 8 else vec[:, 0, (V_QN if e < 12 else V_KN):(V_QN if e < 12 else V_KN) + 1]
                    i = V.scalar_tensor_tensor(out=t, in0=t, scalar=w, in1=rsq[e % 2][:, 0:n], op0=ALU.mult, op1=ALU.mult)
                i.then_inc(sem("nrm"), 1)
            dve.wait_ge(sem("rope_in"), 32)
            for e in range(5):
                t, b = rope_tile(e), sqt[e % 2][:, 0:SEQ]
                dve.wait_ge(sem("nrm"), 9 + e)
                V.stream_shuffle(b, t, [j ^ 1 for j in range(32)]).then_inc(sem("shuf"), 1)
                dve.wait_ge(sem("shuf"), e + 1)
                V.tensor_tensor(b, b, sinT[:, :], ALU.mult).then_inc(sem("rsin"), 1)
                dve.wait_ge(sem("rsin"), e + 1)
                dve.wait_ge(sem("rcos"), e + 1)
                V.tensor_tensor(t, t, b, ALU.add).then_inc(sem("rope"), 1)
            dve.wait_ge(sem("abT"), 1)
            V.tensor_copy(abt[:, :, :].rearrange("p n c -> p (n c)"), bank(4, 16 * NT)).then_inc(sem("abt"), 1)
            dve.wait_ge(sem("abt"), 1)
            dve.wait_ge(sem("gate_in"), 32)
            V.tensor_tensor(smallv[:, 7], abt[:, :, 0:8], bh(alog[:, 8:16], NT), ALU.add).then_inc(sem("z"), 1)
            dve.wait_ge(sem("z"), 1)
            V.tensor_scalar(smallv[:, 5], smallv[:, 7], 0.0, None, ALU.max).then_inc(sem("gate_v"), 1)
            dve.wait_ge(sem("gate_v"), 1)
            dve.wait_ge(sem("gate_a"), 3)
            V.tensor_tensor(smallv[:, 5], smallv[:, 5], smallv[:, 6], ALU.add).then_inc(sem("gate_v"), 1)
            dve.wait_ge(sem("gate_v"), 2)
            dve.wait_ge(sem("ea"), 1)
            V.scalar_tensor_tensor(out=smallv[:, 0], in0=smallv[:, 5], scalar=-1.0, in1=bh(alog[:, 0:8], NT),
                                       op0=ALU.mult, op1=ALU.mult).then_inc(sem("g"), 1)
            dve.wait_ge(sem("gsum"), 1)
            sums = bank(5, 192).rearrange("p (j n c) -> p j n c", j=3, c=8)[:, :, 0:NT]
            for k in (2, 3):
                for d in range(2):
                    i = V.tensor_copy(smallv[:, k, :, 4 * d:4 * d + 4], sums[:, d, :, 4 * d:4 * d + 4])
            i.then_inc(sem("gcv"), 1)
            dve.wait_ge(sem("gcv"), 1)
            V.tensor_tensor(smallv[:, 4], sums[:, 2], smallv[:, 2], ALU.subtract).then_inc(sem("gcv"), 1)
            V.tensor_copy(smallv[:, 5], sums[:, 2]).then_inc(sem("gcv"), 1)
            dve.wait_ge(sem("ge"), 3)
            dve.wait_ge(sem("beta"), 1)
            V.tensor_tensor(smallv[:, 6], smallv[:, 1], smallv[:, 3], ALU.mult).then_inc(sem("dn_ready"), 1)
            dve.wait_ge(sem("dn_ready"), 1)

            per = lambda k, n, d: bc(smallv[:, k, n, 4 * d:4 * d + 4], P)
            pbank = lambda b: bank(b).rearrange("p (h t) -> p h t", t=P)
            for s in range(NT):
                for d in range(2):
                    k, n, T, b0 = 2 * s + d, CHUNK_ORDER[d][s], DT[d], 3 * d
                    dve.wait_ge(sem("gc"), k + 1)
                    V.tensor_tensor(T["ta"][:, :, :], per(2, n, d), pbank(b0), ALU.subtract).then_inc(sem("dA1"), 1)
                    dve.wait_ge(sem("dA1"), k + 1)
                    V.tensor_scalar(T["ta"][:, :, :], T["ta"][:, :, :], 0.0, None, ALU.min).then_inc(sem("dA"), 1)
                    if n >= NTC:
                        V.tensor_tensor(T["tb"][:, :, :], pbank(b0), per(2, n, d), ALU.subtract).then_inc(sem("dB1"), 1)
                        dve.wait_ge(sem("dB1"), k - 3)
                        V.tensor_scalar(T["tb"][:, :, :], T["tb"][:, :, :], 0.0, None, ALU.min).then_inc(sem("dB"), 1)
                for d in range(2):
                    k, n, T, b0 = 2 * s + d, CHUNK_ORDER[d][s], DT[d], 3 * d
                    V.tensor_copy(T["tu"][:, :, :], bh(ident, 8)).then_inc(sem("TU0"), 1)
                    dve.wait_ge(sem("G"), k + 1)
                    dve.wait_ge(sem("EA"), k + 1)
                    V.tensor_tensor(T["ta"][:, :, :], T["ta"][:, :, :], pbank(b0 + 1), ALU.mult).then_inc(sem("GA"), 1)
                    if n >= NTC:
                        dve.wait_ge(sem("QK"), cnt(k - 3))
                        dve.wait_ge(sem("EB"), cnt(k - 3))
                        V.tensor_tensor(T["tb"][:, :, :], T["tb"][:, :, :], pbank(b0 + 2), ALU.mult).then_inc(sem("QB"), 1)
                        dve.wait_ge(sem("egr"), cnt(k - 3))
                        V.tensor_tensor(T["qg"][:, :, :], qT[:, :, (n - NTC) * P:(n - NTC + 1) * P],
                                            T["kbvn"][:, :, :], ALU.mult).then_inc(sem("qg"), 1)
                for d in range(2):
                    k, n, T, b0 = 2 * s + d, CHUNK_ORDER[d][s], DT[d], 3 * d
                    dve.wait_ge(sem("Ktr"), k + 1)
                    if n >= NTC:
                        dve.wait_ge(sem("qg"), cnt(k - 3))
                    V.tensor_tensor(T["kbvn"][:, :, :], pbank(b0 + 1), per(6, n, d), ALU.mult).then_inc(sem("kb"), 1)
                    V.tensor_tensor(T["kd"][:, :, :], pbank(b0 + 1), per(4, n, d), ALU.mult).then_inc(sem("kb"), 1)
                    dve.wait_ge(sem("Vtr"), k + 1)
                    V.tensor_tensor(T["bv"][:, :, :], pbank(b0 + 2), per(1, n, d), ALU.mult).then_inc(sem("bv"), 1)
                for l in range(LEVELS):
                    for d in range(2):
                        T, q = DT[d], (s * LEVELS + l) * 2 + d
                        dve.wait_ge(sem("dTU"), q + 1)
                        V.tensor_tensor(T["tu"][:, :, :].rearrange("p h t -> p (h t)"),
                                            f32(T["tu"][:, :, :]).rearrange("p h t -> p (h t)"),
                                            bank(3 * d + 1, 1024), ALU.subtract).then_inc(sem("TU"), 1)
                for d in range(2):
                    T, k = DT[d], 2 * s + d
                    dve.wait_ge(sem("LU"), k + 1)
                    dve.wait_ge(sem("t0"), k + 1)
                    V.tensor_tensor(T["bl"][:, :, :], T["nw"][:, :, :], pbank(3 * d), ALU.subtract).then_inc(sem("R2"), 1)
                for d in range(2):
                    T, k = DT[d], 2 * s + d
                    dve.wait_ge(sem("dN"), k + 1)
                    V.tensor_tensor(T["uf"][:, :, :], f32(T["tu"][:, 0:4, :]), pbank(3 * d + 1), ALU.add).then_inc(sem("Uf"), 1)
                for d in range(2):
                    T, k, n = DT[d], 2 * s + d, CHUNK_ORDER[d][s]
                    if n >= NTC:
                        dve.wait_ge(sem("o"), cnt(k - 3))
                        dst = oT[:, :, (n - NTC) * P:(n - NTC + 1) * P]
                        if s < 4:
                            i = V.tensor_copy(dst, pbank(3 * d + 1))
                        else:
                            dve.wait_ge(sem("oe"), 4)
                            i = V.tensor_tensor(dst, dst, pbank(3 * d + 1), ALU.add)
                        i.then_inc(sem("oe"), 1)
                    dve.wait_ge(sem("Sp"), k + 1)
                    if s == 0:
                        i = V.tensor_copy(S[d][:, :, :], pbank(3 * d + 2))
                    else:
                        dve.wait_ge(sem("S"), cnt(k - 1))
                        for h in range(HEADS):
                            i = V.scalar_tensor_tensor(out=S[d][:, h, :], in0=S[d][:, h, :],
                                                       scalar=smallv[:, 5, n, 4 * d + h:4 * d + h + 1],
                                                       in1=bank(3 * d + 2, P, h * P), op0=ALU.mult, op1=ALU.add)
                    i.then_inc(sem("S"), 1)
            dve.wait_ge(sem("mod_done"), 2 * MODS)
            V.tensor_tensor(modv[:, 0, 16:MODS, :], bank(7, 64, 32).rearrange("p (m w) -> p m w", w=2),
                            bc(vec[:, 1, 16:MODS], 2), ALU.add)
            V.tensor_tensor(modv[:, 1, :, :], bank(7, 96, 96).rearrange("p (m w) -> p m w", w=2),
                                bc(vec[:, 1, MODS:2 * MODS], 2), ALU.add).then_inc(sem("modv"), 1)
            dve.wait_ge(sem("modv"), 2)
            pre_weights(1, 0, 4 * KC, 0, V_FFNPRE)
            pre_weights(2, 1, KC, 0, V_MIXPRE + KC)
            pre_weights(3, 1, 4 * KC, 0, V_FFNPRE + KC)
            for k, l, m, row in ((0, 0, 2, V_MIXPOST), (1, 0, 5, V_FFNPOST), (2, 1, 2, V_MIXPOST + KC), (3, 1, 5, V_FFNPOST + KC)):
                i = V.tensor_tensor(post_w[:, k, :], modv[:, l, m * KC:(m + 1) * KC, 0], vec[:, 0, row:row + KC], ALU.mult)
            i.then_inc(sem("norm_w"), 1)
            dve.wait_ge(sem("gate"), HEADS)
            for h in range(HEADS):
                dve.wait_ge(sem("osd"), h + 1)
                V.reciprocal(tmp[2 + h % 2][:, :], tmp[2 + h % 2][:, :]).then_inc(sem("orc"), 1)
                dve.wait_ge(sem("orc"), h + 1)
                V.scalar_tensor_tensor(out=oT[:, h, :], in0=oT[:, h, :], scalar=vec[:, 0, V_DNOUT:V_DNOUT + 1],
                                           in1=tmp[2 + h % 2][:, :], op0=ALU.mult, op1=ALU.mult).then_inc(sem("on1"), 1)
                dve.wait_ge(sem("on1"), h + 1)
                V.tensor_tensor(oT[:, h, :], oT[:, h, :], gT[:, h, :], ALU.mult).then_inc(sem("on"), 1)
            for h in range(HEADS):
                dve.wait_ge(sem("on_hi"), h + 1)
                V.tensor_tensor(mix_lo[:, h, :], oT[:, h, :], f32(mix_hi[:, h, :]), ALU.subtract).then_inc(sem("mix0"), 1)
            dve.wait_ge(sem("Vah"), 1)
            V.tensor_tensor(Vl[:, :, :].rearrange("p n t -> p (n t)"), bank(2, ALL),
                                f32(Vh[:, :, :]).rearrange("p n t -> p (n t)"), ALU.subtract).then_inc(sem("Va"), 1)

            NQ = SEQ // P

            def normalize(i):
                dve.wait_ge(sem("expd"), i + 1)
                V.reciprocal(stat[:, 96 + i:97 + i], stat[:, 64 + i:65 + i]).then_inc(sem("rc1"), 1)
                dve.wait_ge(sem("rc1"), i + 1)
                V.tensor_scalar(prob[i % 2][:, :], prob[i % 2][:, :], stat[:, 96 + i:97 + i], None, ALU.mult).then_inc(sem("Pn"), 1)

            def turn_lo(i):
                hh, qt = divmod(i, NQ)
                dve.wait_ge(sem("PTh"), i + 1)
                dst = slice(qt * P, (qt + 1) * P)
                V.tensor_tensor(PTl[hh % 2][:, :, dst], bank(4, ALL).rearrange("p (n t) -> p n t", t=P),
                                    f32(PTh[hh % 2][:, :, dst]), ALU.subtract).then_inc(sem("PT"), 1)

            def head_lo(hh):
                half, t = hh // 4, hh % 4
                r = slice(HD * half, HD * (half + 1))
                dve.wait_ge(sem("ahh"), hh + 1)
                V.tensor_tensor(mix_lo[r, 4 + t, :], bank(6 + hh % 2)[r], f32(mix_hi[r, 4 + t, :]), ALU.subtract).then_inc(sem("mix0"), 1)

            for i in range(A_HEADS * NQ + 2):
                if i < A_HEADS * NQ:
                    dve.wait_ge(sem("sc"), i + 1)
                    V.tensor_reduce(stat[:, i:i + 1], bank(2 * (i % 2), ALL), AX.X, ALU.max).then_inc(sem("mx1"), 1)
                    dve.wait_ge(sem("mx1"), i + 1)
                    V.tensor_scalar(stat[:, 32 + i:33 + i], stat[:, i:i + 1], -HD ** -0.5, None, ALU.mult).then_inc(sem("mx"), 1)
                if 1 <= i <= A_HEADS * NQ:
                    normalize(i - 1)
                    turn_lo(i - 1)
                if i >= NQ + 1 and (i - NQ - 1) % NQ == 0:
                    head_lo((i - NQ - 1) // NQ)

            def y_out(u0, yq):
                def body(i):
                    for s in range(2):
                        split_lo(2 * i + (u0 + s + 2), s)
                        for r in range(2):
                            dve.wait_ge(sem("tile"), 4 * i + (2 * (u0 + s) + r + 1))
                            V.tensor_copy(y[:, bass.ds(4 * i + (2 * s + r), 1), :].rearrange("p c t -> p (c t)"),
                                              bank(2 * s + r)).then_inc(sem("yev"), 1)
                rep(dve, 2, body)

            def boundary(idx, post, pre, hb, shift):
                rstd(idx, tmp, SEQ)
                dve.wait_ge(sem("norm_w"), 2)
                dve.wait_ge(sem("yev"), cnt(KC * ((idx - 2) // 2 + 1)))
                b = KC * ((idx - 2) // 2)
                for c in range(KC + 1):
                    if c < KC:
                        V.scalar_tensor_tensor(out=y[:, c, :], in0=y[:, c, :], scalar=post_w[:, post, c:c + 1],
                                                   in1=tmp[3][:, :], op0=ALU.mult, op1=ALU.mult).then_inc(sem("yn"), 1)
                    if c:
                        dve.wait_ge(sem("yn"), b + c)
                        V.tensor_tensor(x[:, c - 1, :], x[:, c - 1, :], y[:, c - 1, :], ALU.add).then_inc(sem("x_new"), 1)
                if idx < 8:
                    rstd(idx + 1, tmp, SEQ)
                    apply_pre(hb, lambda c: x[:, c, :], tmp, SEQ, pre, shift, h_hi, h_lo)

            def conv(src, acc, w, name, count, last):
                for r in range(2):
                    V.scalar_tensor_tensor(out=acc(r)[:, 1:SEQ], in0=src(r)[:, 0:SEQ - 1], scalar=w(0, r),
                                               in1=acc(r)[:, 1:SEQ], op0=ALU.mult, op1=ALU.add).then_inc(sem(name), 1)
                for r in range(2):
                    dve.wait_ge(sem(name), count(r))
                    V.scalar_tensor_tensor(out=acc(r)[:, 0:SEQ - 1], in0=src(r)[:, 1:SEQ], scalar=w(2, r),
                                               in1=acc(r)[:, 0:SEQ - 1], op0=ALU.mult, op1=ALU.add).then_inc(sem(last), 1)

            def ffn(f, U_UP, U_DOWN, yq):
                def up_pair(i, par, j0):
                    tl = lambda r: 2 * i + (FC * f + 2 * j0 + r)
                    u = 2 * i + (U_UP + 2 * j0)
                    split_lo(u + 2, 0)
                    dve.wait_ge(sem("c1"), tl(1) + 1)
                    conv(lambda r: bank(4 * par + r), lambda r: tmp[2 * par + r],
                         lambda k, r: vec[:, 3 + f, bass.ds(2 * i + (2 * j0 + r + 22 * k), 1)],
                         "c2", lambda r: tl(r) + 1, "c3_free")
                    split_lo(u + 3, 1)
                    for r in range(2):
                        dve.wait_ge(sem("sg"), tl(r) + 1)
                        V.tensor_tensor(tmp[2 * par + r][:, :], tmp[2 * par + r][:, :], bank(4 * par + 2 + r), ALU.mult).then_inc(sem("g_free"), 1)
                    for r in range(2):
                        dve.wait_ge(sem("ghi"), tl(r) + 1)
                        j = 2 * i + (2 * j0 + r)
                        flat = lambda m: m[:, bass.ds(j, 1), :].rearrange("p c t -> p (c t)")
                        V.tensor_tensor(flat(mid_lo), tmp[2 * par + r][:, :], f32(flat(mid_hi)), ALU.subtract).then_inc(sem("mid"), 1)

                def up4(i):
                    for par in range(2):
                        up_pair(2 * i, par, par)
                rep(dve, FC // 4, up4)
                up_pair(0, 0, FC // 2 - 1)

                def down2(i, last=False):
                    for q in range(6):
                        if not (last and q >= 4):
                            split_lo(6 * i + (U_DOWN + q + 2), q % 2)
                        if q % 3 == 2:
                            for r in range(2):
                                dve.wait_ge(sem("tile"), 12 * i + (2 * (U_DOWN + q) + r + 1))
                                t = 4 * i + (2 * (q // 3) + r)
                                V.tensor_copy(y[:, bass.ds(t, 1), :].rearrange("p c t -> p (c t)"),
                                                  bank(2 * (q // 3) + r)).then_inc(sem("yev"), 1)
                if f == 0:
                    rep(dve, 2, down2)
                else:
                    down2(0)
                    down2(1, True)

            y_out(U_WOUT, 0)
            boundary(2, 0, 1, 2, lambda c: modv[:, 0, 3 * KC + c, 0:1])
            ffn(0, U_UP0, U_DOWN0, 1)
            boundary(4, 1, 2, 3, lambda c: modv[:, 1, c, 0:1])

            def cx(i, par, j0):
                tl = lambda r: 2 * i + (2 * j0 + r)
                flat = lambda r: cv[:, bass.ds(tl(r), 1), :].rearrange("p c t -> p (c t)")
                split_lo(2 * i + (U_SCIN + 2 * j0 + 2), 0)
                split_lo(2 * i + (U_SCIN + 2 * j0 + 3), 1)
                for r in range(2):
                    dve.wait_ge(sem("scc"), tl(r) + 1)
                    V.tensor_tensor(tmp[2 * par + r][:, :], tmp[2 * par + r][:, :], bank(4 * par + 2 + r), ALU.mult).then_inc(sem("scu"), 1)
                dve.wait_ge(sem("scu"), tl(1) + 1)
                dve.wait_ge(sem("scv1"), tl(1) + 1)
                conv(lambda r: tmp[2 * par + r], flat,
                     lambda k, r: vec[:, 0, bass.ds(2 * i + (2 * j0 + r + V_SCCONV + 8 * k), 1)],
                     "scv2", lambda r: tl(r) + 1, "scv")

            def cx2(i):
                for par in range(2):
                    cx(2 * i, par, par)
            rep(dve, 2, cx2)

            def gate_b(i):
                for s in range(2):
                    split_lo(2 * i + (U_SCIN + 8 + s + 2), s)
                    for r in range(2):
                        t = 4 * i + (2 * s + r)
                        dve.wait_ge(sem("tile"), 4 * i + (2 * (U_SCIN + 8 + s) + r + 1))
                        dve.wait_ge(sem("scv"), KC)
                        V.tensor_tensor(tmp[2 * s + r][:, :], bank(2 * s + r),
                                            cv[:, bass.ds(t, 1), :].rearrange("p c t -> p (c t)"), ALU.mult).then_inc(sem("scb"), 1)
                    for r in range(2):
                        t = 4 * i + (2 * s + r)
                        flat = lambda m: m[:, bass.ds(t, 1), :].rearrange("p c t -> p (c t)")
                        dve.wait_ge(sem("mhi"), t + 1)
                        V.tensor_tensor(flat(mix_lo), tmp[2 * s + r][:, :], f32(flat(mix_hi)), ALU.subtract).then_inc(sem("mix1"), 1)
            rep(dve, 2, gate_b)
            y_out(U_SCOUT, 2)
            boundary(6, 2, 3, 4, lambda c: modv[:, 1, 3 * KC + c, 0:1])
            ffn(1, U_UP1, U_DOWN1, 3)
            boundary(8, 3, None, None, None)
            for n in range(NL):
                dve.wait_ge(sem("out_T"), 2 * n + 2)
                V.tensor_copy(xin[:, n, 512:1024], bank(2 * n + 1)).then_inc(sem("out_ev_d"), 1)

        @block.gpsimd
        def _(pool):
            G = nc.gpsimd

            def add_squares(idx):
                t4, n = (ctmp, CTX) if idx == 0 else (tmp, SEQ)
                pool.wait_ge(sem("stat"), idx)
                for c in range(KC):
                    pool.wait_ge(sem("sq"), KC * idx + c + 1)
                    acc, t = t4[2][:, 0:n], t4[c % 2][:, 0:n]
                    if c == 0:
                        i = G.tensor_copy(acc, t)
                    else:
                        pool.wait_ge(sem("sqadd"), KC * idx + c)
                        i = G.tensor_tensor(acc, acc, t, ALU.add)
                    i.then_inc(sem("sqadd"), 1)

            add_squares(0)
            add_squares(1)
            pool.wait_ge(sem("rope_in"), 32)
            for e in range(5):
                pool.wait_ge(sem("shuf"), e + 1)
                G.tensor_tensor(rope_tile(e), rope_tile(e), cosT[:, :], ALU.mult).then_inc(sem("rcos"), 1)
            pool.wait_ge(sem("dn_ready"), 1)
            for s in range(NT):
                for d in range(2):
                    k, n, T = 2 * s + d, CHUNK_ORDER[d][s], DT[d]
                    pool.wait_ge(sem("GA"), k + 1)
                    G.tensor_tensor(T["ta"][:, :, :], T["ta"][:, :, :], bc(smallv[:, 1, n, 4 * d:4 * d + 4], P), ALU.mult).then_inc(sem("Lb"), 1)
                    pool.wait_ge(sem("Lb"), k + 1)
                    G.tensor_tensor(T["ta"][:, :, :], T["ta"][:, :, :], bh(C(C_STRICT + d), HEADS), ALU.mult).then_inc(sem("L"), 1)
                for l in range(LEVELS):
                    for d in range(2):
                        T, q, k = DT[d], (s * LEVELS + l) * 2 + d, 2 * s + d
                        if l == 0:
                            pool.wait_ge(sem("L"), k + 1)
                            pool.wait_ge(sem("dN"), cnt(k - 1))
                        else:
                            pool.wait_ge(sem("Z"), cnt(q - 1))
                        G.tensor_tensor(T["bl"][:, :, :], T["ta"][:, :, :], bh(C(C_LVL + LEVELS * d + l), HEADS), ALU.mult).then_inc(sem("Bl"), 1)
                    if l == 1:
                        for d in range(2):
                            k, n, T = 2 * s + d, CHUNK_ORDER[d][s], DT[d]
                            if n >= NTC:
                                pool.wait_ge(sem("QB"), cnt(k - 3))
                                G.tensor_tensor(T["tb"][:, :, :], T["tb"][:, :, :], bh(C(C_TRI + d), HEADS), ALU.mult).then_inc(sem("intra"), 1)
                for d in range(2):
                    T, k = DT[d], 2 * s + d
                    pool.wait_ge(sem("TU"), cnt((s + 1) * LEVELS * 2 - 1 + d))
                    G.tensor_tensor(T["nw"][:, :, :], bh(ident, HEADS), f32(T["tu"][:, 0:4, :]), ALU.subtract).then_inc(sem("t0"), 1)
            for idx in range(2, 9):
                add_squares(idx)


def constants():
    c = np.zeros((P, NCONST, P), np.float32)
    i = np.arange(P)
    r, q = i[:, None], i[None, :]
    c[:, C_ID] = r == q
    c[:, C_ONE] = 1
    c[:, C_TRI], c[:, C_TRI + 1] = r <= q, r >= q
    c[:, C_STRICT], c[:, C_STRICT + 1] = r > q, r < q
    for l in range(LEVELS):
        s = 1 << l
        low = (r // (2 * s) == q // (2 * s)) & (r // s % 2 == 1) & (q // s % 2 == 0)
        c[:, C_LVL + l], c[:, C_LVL + LEVELS + l] = low, low.T
    c[:, C_BLK] = r // HD == q // HD
    t = np.arange(SEQ)
    inv = (np.float32(ROPE_THETA) ** (-np.arange(0, HD // 2, 2, dtype=np.float32) / np.float32(HD // 2))).astype(np.float32)
    ang = np.concatenate([(t // GRID_W).astype(np.float32)[:, None] * inv, (t % GRID_W).astype(np.float32)[:, None] * inv], 1)
    pair = (i % HD) // 2
    cos = np.cos(ang).T[pair].astype(np.float32)
    sin = np.sin(ang).T[pair].astype(np.float32) * np.where(i % 2 == 0, -1, 1).astype(np.float32)[:, None]
    return {"const": c.reshape(P, NCONST * P), "cos": np.ascontiguousarray(cos), "sin": np.ascontiguousarray(sin)}


_INS = ['x', 'c', 'ctx', 'c_ctx', 'mod_w', 'mod_b', 'norm_mix_pre', 'norm_mix_post', 'norm_ffn_pre', 'norm_ffn_post',
        'hyb_w_in', 'hyb_w_out', 'dn_conv_w', 'dn_a_log', 'dn_dt_bias', 'dn_out_norm', 'att_q_norm', 'att_k_norm',
        'sc_w_in', 'sc_conv_w', 'sc_w_out', 'ffn_w_up', 'ffn_conv_w', 'ffn_w_down']


def kernel(**inputs):
    import concourse.bacc as bacc
    from concourse.bass_utils import run_bass_kernel_spmd

    nc = bacc.Bacc("TRN2", target_bir_lowering=False, num_devices=1)
    arrays = {name: np.ascontiguousarray(inputs[name]) for name in _INS}
    arrays.update(constants())
    args = {name: nc.dram_tensor(f"in_{name}", a.shape, mybir.dt.from_np(a.dtype), kind="ExternalInput").ap()
            for name, a in arrays.items()}
    out = nc.dram_tensor("out", (1, SEQ, D_MODEL), F32, kind="ExternalOutput").ap()
    hybrid_trunk(nc, args, out)
    r = run_bass_kernel_spmd(nc, [{f"in_{name}": a for name, a in arrays.items()}], core_ids=[0])
    return r.results[0]["out"]
```

```python
import numpy as np
from contextlib import ExitStack

import concourse.bass as bass
from concourse import mybir

F32 = mybir.dt.float32
F32R = mybir.dt.float32r
ALU = mybir.AluOpType
ACT = mybir.ActivationFunctionType
AX = mybir.AxisListType

P = 128
D_MODEL, SEQ, CTX = 1024, 512, 256
ALL = CTX + SEQ
EPS = 1e-6
KC = D_MODEL // P
D_FF = 2816
FC = D_FF // P
HEADS, DK = 4, 128
DIRS = 2
A_HEADS, A_KV, HD = 8, 2, 64
GRID_W, ROPE_THETA = 64, 10000.0
NT = ALL // P
NTC = CTX // P
NL = NT - NTC
LEVELS = 7
CHUNK_ORDER = [[0, 1, 2, 3, 4, 5], [1, 0, 5, 4, 3, 2]]
MODS = 6 * KC

C_ID, C_ONE, C_TRI, C_STRICT, C_LVL, C_BLK = 0, 1, 2, 4, 6, 6 + 2 * LEVELS
NCONST = C_BLK + 1

V_MIXPRE, V_MIXPOST, V_FFNPRE, V_FFNPOST = 0, 16, 32, 48
V_C, V_CCTX, V_DNOUT, V_QN, V_KN, V_SCCONV = 64, 72, 80, 81, 82, 83
V_ROWS = [V_SCCONV + 24, 96, 36, 66, 66]

O_ALPHA, O_AK = 1024, 1040
O_Q, O_G, O_AQ = 1296, 1808, 2320

UW = 256
U_HYB, U_WOUT, U_UP0, U_DOWN0 = 0, 12, 16, 38
U_SCIN, U_SCOUT, U_UP1, U_DOWN1 = 50, 62, 66, 88
MSLOTS = 6
H_SC, H_FFN = 3, (2, 4)
POST = (2, 4, 6, 8)
DCH = [(0, 8), (8, 7), (15, 7)]


def hybrid_trunk(nc, A, out):
    ctx = ExitStack()
    with ctx:
        base = [(nc.sbuf_base + 31) // 32 * 32]
        end = nc.sbuf_usable_end

        def place(name, cols, dt=F32, at=None):
            off = base[0] if at is None else at
            t = nc.alloc_sbuf_tensor_at(name, [P, cols], dt, offset=off)
            if at is None:
                base[0] += (cols * 4 + 31) // 32 * 32
            assert off + cols * 4 <= end, (name, off + cols * 4, end)
            return t

        def view(tile, pat, **k):
            return tile[:, :].rearrange(pat, **k)

        const = view(place("const", NCONST * P), "p (k n) -> p k n", n=P)
        x = view(place("x", KC * SEQ), "p (c t) -> p c t", t=SEQ)
        vec = view(place("vec", 5 * P), "p (k n) -> p k n", n=P)
        modv = view(place("modv", 2 * MODS * 2), "p (l m w) -> p l m w", l=2, w=2)
        cvec = view(place("cvec", KC * 2), "p (k w) -> p k w", w=2)
        pre_w = view(place("pre_w", 5 * KC), "p (k c) -> p k c", c=KC)
        post_w = view(place("post_w", 4 * KC), "p (k c) -> p k c", c=KC)
        eps = place("eps", 1)
        dev = place("norm_dev", 9 * NL)
        ring_at = base[0]
        raw = [place(f"w_raw{i}", KC * UW) for i in range(2)]
        whi = [place(f"w_hi{i}", KC * UW, F32R) for i in range(2)]
        wlo = [place(f"w_lo{i}", KC * UW, F32R) for i in range(2)]
        tmp_at = base[0]
        tmp = [place(f"tmp{i}", SEQ) for i in range(4)]
        R = base[0]
        K = 1024

        def region(name, cols, at, dt=F32):
            return place(name, cols, dt, R + int(at * K))

        h_hi = view(region("h_hi", KC * SEQ, 88, F32R), "p (c t) -> p c t", t=SEQ)
        h_lo = view(region("h_lo", KC * SEQ, 104, F32R), "p (c t) -> p c t", t=SEQ)
        y = view(region("y", KC * SEQ, 88), "p (c t) -> p c t", t=SEQ)
        mid_hi = view(region("mid_hi", FC * SEQ, 0, F32R), "p (c t) -> p c t", t=SEQ)
        mid_lo = view(region("mid_lo", FC * SEQ, 44, F32R), "p (c t) -> p c t", t=SEQ)
        mix_hi = view(region("mix_hi", KC * SEQ, 0, F32R), "p (c t) -> p c t", t=SEQ)
        mix_lo = view(region("mix_lo", KC * SEQ, 16, F32R), "p (c t) -> p c t", t=SEQ)
        cv = view(region("cv", KC * SEQ, 32), "p (c t) -> p c t", t=SEQ)
        xin = view(region("xin", NL * D_MODEL, 0), "p (n c) -> p n c", c=D_MODEL)
        cin = view(region("cin", NTC * D_MODEL, 16), "p (n c) -> p n c", c=D_MODEL)
        vrow = view(region("vrow", 5 * P, 24), "p (k n) -> p k n", n=P)
        ctmp = [region(f"ctmp{i}", CTX, 48 + i) for i in range(4)]
        mraw_a = [view(place(f"mod_raw_a{i}", KC * UW, F32, a0), "p (k n) -> p k n", n=UW) for i, a0 in
                  enumerate([ring_at + KC * UW * 4 * j for j in range(2, 6)] + [R + j * K for j in (32, 40, 96, 104)])]
        mod_row = region("mod_row", 16 * P, 88)
        mraw_b = [view(place(f"mod_raw_b{i}", KC * P, F32, a0), "p (k n) -> p k n", n=P)
                  for i, a0 in enumerate((tmp_at, tmp_at + 4 * K, R + 73 * K, R + 77 * K))]
        macc_b = [region(f"mod_acc_b{i}", P, 85 + i / 2) for i in range(4)]
        mraw_c = [view(place(f"mod_raw_c{i}", KC * UW, F32, ring_at + KC * UW * 4 * i), "p (k n) -> p k n", n=UW)
                  for i in range(MSLOTS)]
        hc_hi = view(region("hc_hi", KC * CTX, 57, F32R), "p (c t) -> p c t", t=CTX)
        hc_lo = view(region("hc_lo", KC * CTX, 65, F32R), "p (c t) -> p c t", t=CTX)
        xc = view(region("xc", KC * CTX, 73), "p (c t) -> p c t", t=CTX)
        kT = view(region("kT", HEADS * ALL, 0), "p (h t) -> p h t", t=ALL)
        qT = view(region("qT", HEADS * SEQ, 12), "p (h t) -> p h t", t=SEQ)
        vT = view(region("vT", HEADS * ALL, 20), "p (h t) -> p h t", t=ALL)
        gT = view(region("gT", HEADS * SEQ, 32), "p (h t) -> p h t", t=SEQ)
        aq = view(region("aq", HEADS * SEQ, 40), "p (h t) -> p h t", t=SEQ)
        ak = region("ak", ALL, 48)
        av = region("av", ALL, 51)
        ab = region("ab", ALL, 54)
        nsm = region("item_dev", 96, 57)
        sqt = [region(f"sqt{i}", ALL, 63 + 3 * i) for i in range(2)]
        cosT = region("cosT", SEQ, 81)
        sinT = region("sinT", SEQ, 83)
        oT = view(region("oT", HEADS * SEQ, 57), "p (h t) -> p h t", t=SEQ)
        S = [view(region(f"S{d}", HEADS * P, 65 + 2 * d), "p (h t) -> p h t", t=P) for d in range(2)]
        smallv = view(region("dn_small", 8 * NT * 8, 69), "p (k n c) -> p k n c", k=8, c=8)
        abt = view(region("abt", NT * 16, 70.5), "p (n c) -> p n c", c=16)
        alog = region("alog", 16, 87)
        DT = []
        spots = [88 + 2 * i for i in range(12)], [112, 114, 116, 118] + [71 + 2 * i for i in range(8)]
        for d in range(2):
            t, free = {}, list(spots[d])
            for n in ("tu", "zs", "bl", "ta", "tb", "qg", "kbvn", "bv", "kd", "nw", "uf"):
                a0 = free.pop(0)
                w = HEADS * P
                if n == "tu":
                    free.pop(0)
                    w *= 2
                v = region(f"dn_{n}{d}", w, a0, F32R if n in ("tu", "zs", "bl") else F32)
                t[n] = view(v, "p (h t) -> p h t", t=P)
            DT.append(t)
        PTh = [view(region(f"PTh{i}", NT * SEQ, a0, F32R), "p (n t) -> p n t", t=SEQ) for i, a0 in enumerate((88, 57))]
        PTl = [view(region(f"PTl{i}", NT * SEQ, a0, F32R), "p (n t) -> p n t", t=SEQ) for i, a0 in enumerate((100, 69))]
        prob = [region(f"prob{i}", ALL, a0) for i, a0 in enumerate((81, 84, 54))]
        stat = region("att_stat", 4 * 32, 112)
        Vh = view(region("Vh", NT * P, 114, F32R), "p (n t) -> p n t", t=P)
        Vl = view(region("Vl", NT * P, 117, F32R), "p (n t) -> p n t", t=P)

        PS = ctx.enter_context(nc.psum_tensor("ps", [P, 8 * 512], F32))

        def bank(b, n=512, o=0):
            return PS[:, b * 512 + o:b * 512 + o + n]

        sems = {}

        def sem(name):
            if name not in sems:
                sems[name] = ctx.enter_context(nc.semaphore(name))
            return sems[name]

        def rep(eng, n, body, peel=0):
            for i in range(peel):
                body(i)
            if n - peel > 1:
                with eng.Fori(peel, n) as i:
                    body(i)
            elif n > peel:
                body(peel)

        def cnt(value):
            return max(value, 0) if isinstance(value, int) else value

        def mod_group(u):
            return [m for g in range(16) if 2 + g * 10 // 16 == u for m in (16 + 2 * g, 17 + 2 * g)]

        def acc_b(m):
            return 3 * (m - 15)

        def acc_c(j):
            return 3 * (MODS - 16 + j + 1)

        def landed(i, phase_b):
            return lambda n: 16 * (n + 1 + (0 if phase_b or i >= 4 else (MODS - 16) // 4))

        MOD_LEVEL = [LEVELS * (j // 4) + 2 * (j % 4) for j in range(MODS // 2)]

        def mod_at(q, lag):
            return [j for j, q0 in enumerate(MOD_LEVEL) if q0 + lag == q]

        def sq_adds(idx):
            return sum(KC if i in POST else 3 for i in range(idx))

        def sq_cols(idx):
            return sum(0 if i in POST else 4 for i in range(idx))

        def rawcount(u, s):
            if isinstance(u, int):
                return sum(16 * (3 if 12 <= v < 16 else 4 if v in (10, 11) else 1) for v in range(s, u + 1, 2))
            return 8 * (u - s) + 16 + 112

        C = lambda k, n=1: const[:, k:k + n, :].rearrange("p k n -> p (k n)")
        ident, ones = C(C_ID), C(C_ONE)
        rv = [view(t, "p (k n) -> p k n", n=UW) for t in raw]
        wh = [view(t, "p (k n) -> p k n", n=UW) for t in whi]
        wl = [view(t, "p (k n) -> p k n", n=UW) for t in wlo]
        f32 = lambda a: a.bitcast(F32)
        ytile = lambda t: y[:, bass.ds(t, 1), :].rearrange("p c t -> p (c t)")

        def bc(a, n):
            return a.unsqueeze(2).to_broadcast([a.shape[0], a.shape[1], n])

        def bh(a, n):
            return a.unsqueeze(1).to_broadcast([a.shape[0], n, a.shape[1]])

        EVENTS = [(u, stream, r) for u in range(U_WOUT) for stream in (("ctx", "lat") if u < 6 else ("lat",))
                  for r in range(1 if u == 5 else 2)]
        EV = {(u, stream): n + 1 for n, (u, stream, r) in enumerate(EVENTS)}
        EV_LAT = [n + 1 for n, (u, stream, r) in enumerate(EVENTS) if stream == "lat"]
        LAT_BANK = {e[::2]: n % 4 for n, e in enumerate(e for e in EVENTS if e[1] == "lat")}
        N_CONV = 20

        def hyb_bank(u, stream, r):
            return bank(4 + u % 2, CTX, r * CTX) if stream == "ctx" else bank(LAT_BANK[u, r])

        def conv_jobs(u):
            if u < 4 or u in (6, 7):
                kind, first = (kT, 0) if u < 2 else (vT, 4) if u < 4 else (qT, 8)
                for stream in ("ctx", "lat") if u < 4 else ("lat",):
                    for r in range(2):
                        hd = 2 * (u % 2) + r
                        cols = slice(0, SEQ) if u > 4 else slice(0, CTX) if stream == "ctx" else slice(CTX, ALL)
                        yield stream, r, kind[:, hd, cols], hyb_bank(u, stream, r), first + hd

        items = ([(kT[:, h, :], ALL) for h in range(HEADS)] + [(qT[:, h, :], SEQ) for h in range(HEADS)]
                 + [(aq[:, h, :], SEQ) for h in range(HEADS)] + [(ak[:, :], ALL)])

        ITEM_GROUPS = [range(0, 4), range(4, 8), range(8, 13)]

        def item_group(e):
            return min(e // 4, 2)

        def item_col(e, j):
            return e * NT + j if e < 4 else 4 * NT + (e - 4) * NL + j if e < 8 else 4 * (NT + NL) + 2 * (NL * (e - 8) + j)

        item_cols = [slice(0, 4 * NT), slice(4 * NT, 4 * (NT + NL)), slice(4 * (NT + NL), 4 * (NT + NL) + 8 * NL + 2 * NT)]

        def rope_tile(e):
            return aq[:, e, :] if e < 4 else ak[:, CTX:ALL]

        block = ctx.enter_context(nc.Block())


        @block.sync
        def _(sp):
            w_in = A["hyb_w_in"][0].rearrange("(k p) n -> p k n", p=P)
            w_out = A["hyb_w_out"][0]
            sc_in = A["sc_w_in"][0].rearrange("(k p) n -> p k n", p=P)
            sc_out = A["sc_w_out"][0].rearrange("(k p) n -> p k n", p=P)
            up = [A["ffn_w_up"][f].rearrange("(k p) n -> p k n", p=P) for f in range(2)]
            down = [A["ffn_w_down"][f].rearrange("(k p) n -> p k n", p=P) for f in range(2)]

            sp.dma_start(const[:, :, :].rearrange("p k n -> p (k n)"), A["const"]).then_inc(sem("const_in"), 16)
            rows = lambda a: a.rearrange("l (c p) -> (l c) p", p=P)
            for k, r, a in ((0, V_MIXPRE, rows(A["norm_mix_pre"])), (0, V_MIXPOST, rows(A["norm_mix_post"])),
                            (0, V_FFNPRE, rows(A["norm_ffn_pre"])), (0, V_FFNPOST, rows(A["norm_ffn_post"])),
                            (0, V_C, rows(A["c"])), (0, V_CCTX, A["c_ctx"].rearrange("(c p) -> c p", p=P)),
                            (0, V_DNOUT, A["dn_out_norm"]), (0, V_SCCONV, rows(A["sc_conv_w"][0])),
                            (1, 0, rows(A["mod_b"])), (2, 0, rows(A["dn_conv_w"][0])),
                            (3, 0, rows(A["ffn_conv_w"][0])), (4, 0, rows(A["ffn_conv_w"][1]))):
                sp.dma_start(vrow[r:r + a.shape[0], k, :], a).then_inc(sem("vec_in"), 16)
            for half in range(2):
                sp.dma_start(vrow[V_QN:V_QN + 1, 0, half * HD:(half + 1) * HD], A["att_q_norm"]).then_inc(sem("vec_in"), 16)
                sp.dma_start(vrow[V_KN:V_KN + 1, 0, half * HD:(half + 1) * HD], A["att_k_norm"]).then_inc(sem("vec_in"), 16)
            sp.dma_start(cin[:, :, :], A["ctx"][0].rearrange("(n p) c -> p n c", p=P)).then_inc(sem("ctx_in"), 16)
            sp.dma_start(xin[:, :, :], A["x"][0].rearrange("(n p) c -> p n c", p=P)).then_inc(sem("x_in"), 16)

            def load_mod(m):
                src = A["mod_w"][m // MODS].rearrange("(k p) n -> p k n", p=P)[:, :, (m % MODS) * P:(m % MODS + 1) * P]
                """Modulation tile m, 16 to 47."""
                if m >= 20:
                    sp.wait_ge(sem("mod_acc"), acc_b(m - 4))
                sp.dma_start(mraw_b[m % 4][:, :, :], src).then_inc(sem(f"mod_in{m % 4}"), 16)

            def load_mod_pair(j):
                s = j % MSLOTS
                src = A["mod_w"][1].rearrange("(k p) n -> p k n", p=P)[:, :, j * UW:(j + 1) * UW]
                if j >= MSLOTS:
                    sp.wait_ge(sem("mod_done"), MODS - 16 + 2 * (j - MSLOTS + 1))
                sp.dma_start(mraw_c[s][:, :, :], src).then_inc(sem(f"mod_in{s}"), 16)

            def raw_free(u):
                sp.wait_ge(sem("w_lo"), cnt(u - 1))

            for j in range(8):
                src = A["mod_w"][0].rearrange("(k p) n -> p k n", p=P)[:, :, j * UW:(j + 1) * UW]
                sp.dma_start(mraw_a[j][:, :, :], src).then_inc(sem(f"mod_a{j // 4}"), 16)
            for u in range(2):
                sp.dma_start(rv[u][:, :, :], w_in[:, :, u * UW:(u + 1) * UW]).then_inc(sem(f"w_raw{u}"), 16)
            sp.dma_start(cosT[:, :], A["cos"]).then_inc(sem("rope_in"), 16)
            sp.dma_start(sinT[:, :], A["sin"]).then_inc(sem("rope_in"), 16)
            sp.dma_start(alog[:, 0:8], A["dn_a_log"][0].rearrange("d h -> (d h)").unsqueeze(0).to_broadcast([P, 8])).then_inc(sem("gate_in"), 16)
            sp.dma_start(alog[:, 8:16], A["dn_dt_bias"][0].rearrange("d h -> (d h)").unsqueeze(0).to_broadcast([P, 8])).then_inc(sem("gate_in"), 16)
            for u in range(2, 12):
                s = u % 2
                if u == 4:
                    sp.wait_ge(sem("h"), 2 * KC)
                if u >= 5:
                    for m in mod_group(u - 3):
                        load_mod(m)
                raw_free(u)
                if u < 4:
                    sp.dma_start(rv[s][:, :, :], w_in[:, :, u * UW:(u + 1) * UW]).then_inc(sem(f"w_raw{s}"), 16)
                elif u == 4:
                    sp.dma_start(rv[s][:, :, :], w_in[:, :, O_AK:O_AK + UW]).then_inc(sem(f"w_raw{s}"), 16)
                elif u == 5:
                    sp.dma_start(rv[s][:, :, 0:P], w_in[:, :, O_ALPHA:O_ALPHA + P]).then_inc(sem(f"w_raw{s}"), 16)
                elif u < 8:
                    sp.dma_start(rv[s][:, :, :], w_in[:, :, O_Q + (u - 6) * UW:O_Q + (u - 5) * UW]).then_inc(sem(f"w_raw{s}"), 16)
                elif u < 10:
                    sp.dma_start(rv[s][:, :, :], w_in[:, :, O_G + (u - 8) * UW:O_G + (u - 7) * UW]).then_inc(sem(f"w_raw{s}"), 16)
                else:
                    for r in range(2):
                        for a in range(2):
                            o, to = O_AQ + a * 4 * HD + (2 * (u - 10) + r) * HD, r * P + a * HD
                            sp.dma_start(rv[s][:, :, to:to + HD], w_in[:, :, o:o + HD]).then_inc(sem(f"w_raw{s}"), 16)

            def load_wout(u):
                s, q = u % 2, u - U_WOUT
                raw_free(u)
                cols = slice(q * UW, (q + 1) * UW)
                sp.dma_start(rv[s][:, 0:4, :], w_out[0:512, cols].rearrange("(k p) n -> p k n", p=P)).then_inc(sem(f"w_raw{s}"), 16)
                for a in range(2):
                    part = w_out[512 + 256 * a:768 + 256 * a, cols]
                    sp.dma_start(rv[s][HD * a:HD * (a + 1), 4:8, :], part.rearrange("(t p) n -> p t n", p=HD)).then_inc(sem(f"w_raw{s}"), 16)

            for u in range(9, 12):
                for m in mod_group(u):
                    load_mod(m)
            sp.wait_ge(sem("tile"), 2 * U_WOUT)
            sp.wait_ge(sem("mod_acc"), acc_b(MODS - 1))
            for j in range(MODS // 2):
                load_mod_pair(j)
            sp.wait_ge(sem("mod_done"), 2 * MODS - 16)
            load_wout(12)
            load_wout(13)
            load_wout(14)
            load_wout(15)

            def ffn_loads(f, U_UP, U_DOWN):
                def upb(i):
                    for part in range(2):
                        u = 2 * i + (U_UP + part)
                        raw_free(u)
                        o = i * UW
                        sp.dma_start(rv[part][:, :, :], up[f][:, :, bass.ds(o + part * D_FF, UW)]).then_inc(sem(f"w_raw{part}"), 16)
                rep(sp, FC // 2, upb)

                def downb(i):
                    for q in range(6):
                        u = 6 * i + (U_DOWN + q)
                        k0, nk = DCH[q % 3]
                        raw_free(u)
                        o = i * (2 * UW) + (q // 3) * UW
                        sp.dma_start(rv[q % 2][:, 0:nk, :], down[f][:, k0:k0 + nk, bass.ds(o, UW)]).then_inc(sem(f"w_raw{q % 2}"), 16)
                rep(sp, 2, downb)

            ffn_loads(0, U_UP0, U_DOWN0)

            def cxb(i):
                for part in range(2):
                    raw_free(2 * i + (U_SCIN + part))
                    sp.dma_start(rv[part][:, :, :], sc_in[:, :, bass.ds(i * UW + (1 + part) * D_MODEL, UW)]).then_inc(sem(f"w_raw{part}"), 16)
            rep(sp, 4, cxb)

            def sqb(src, U0):
                def body(i):
                    for s in range(2):
                        raw_free(2 * i + (U0 + s))
                        sp.dma_start(rv[s][:, :, :], src[:, :, bass.ds(i * (2 * UW) + s * UW, UW)]).then_inc(sem(f"w_raw{s}"), 16)
                rep(sp, 2, body)
            sqb(sc_in, U_SCIN + 8)
            sqb(sc_out, U_SCOUT)
            ffn_loads(1, U_UP1, U_DOWN1)
            for n in range(NL):
                sp.wait_ge(sem("out_ev_a"), n + 1)
                sp.wait_ge(sem("out_ev_d"), n + 1)
                sp.dma_start(out[0, n * P:(n + 1) * P, :], xin[:, n, :]).then_inc(sem("stored"), 16)
            sp.wait_ge(sem("stored"), 16 * NL)

        @block.tensor
        def _(pe):
            mm, tr = nc.tensor.matmul, nc.tensor.transpose

            def mm3(dst, cols, nk, xh, xl, s, k0=0, first=True, last=True):
                for k in range(nk):
                    hi, lo = cols(wh, k), cols(wl, k)
                    mm(dst, hi, xh[:, k0 + k, :], start=first and k == 0, stop=False)
                    mm(dst, hi, xl[:, k0 + k, :], start=False, stop=False)
                    i = mm(dst, lo, xh[:, k0 + k, :], start=False, stop=last and k == nk - 1)
                return i

            def mm3_first(banks, s, xh, xl, h_count, names, shared=False):
                for k in range(KC):
                    pe.wait_ge(sem("h"), h_count + k + 1)
                    for r, b in enumerate(banks):
                        hi, lo = (w[s][:, k, r * P:(r + 1) * P] for w in (wh, wl))
                        own = r == 0 or not shared
                        mm(b, hi, xh[:, k, :], start=k == 0 and own, stop=False)
                        mm(b, hi, xl[:, k, :], start=False, stop=False)
                        i = mm(b, lo, xh[:, k, :], start=False, stop=k == KC - 1 and (r == 1 or not shared))
                        if k == KC - 1 and names[r]:
                            i.then_inc(sem(names[r]), 1)

            def mod_column(m, acc):
                mm(bank(7, 1, 16 + m), acc, ones[:, 0:1], start=True, stop=True).then_inc(sem("mod_done"), 1)

            def sum_columns(sq, idx, n, first, last):
                for j in range(n // P):
                    i = mm(bank(6, 1, NL * idx + j), sq[:, j * P:(j + 1) * P], ones[:, 0:1],
                           start=first and j == 0, stop=last and j == n // P - 1)
                return i

            def rows(idx, n, b):
                pe.wait_ge(sem("rstd"), idx + 1)
                for j in range(n // P):
                    i = mm(bank(b, P, j * P), dev[:, NL * idx + j:NL * idx + j + 1].to_broadcast([P, P]), ident,
                           start=True, stop=True)
                i.then_inc(sem("rrow"), 1)

            def pre_stat(idx, n, b):
                t4 = ctmp if idx == 0 else tmp
                for c in range(1, KC, 2):
                    pe.wait_ge(sem("sq"), KC * idx + c + 1)
                    sum_columns(t4[c % 2], idx, n, c == 1, False).then_inc(sem("sqcol"), 1)
                pe.wait_ge(sem("sqadd"), sq_adds(idx + 1))
                sum_columns(t4[2], idx, n, False, True).then_inc(sem("stat"), 1)
                rows(idx, n, b)

            def post_stat(idx):
                pe.wait_ge(sem("sqadd"), sq_adds(idx + 1))
                sum_columns(tmp[2], idx, SEQ, True, True).then_inc(sem("stat"), 1)
                rows(idx, SEQ, 5)

            pe.wait_ge(sem("const_in"), 16)
            pe.wait_ge(sem("vec_in"), 16 * 16)
            for k, r in enumerate(V_ROWS):
                i = tr(bank(7 if k < 4 else 6, r, P * (k % 4)), vrow[0:r, k, :], const[0:r, C_ID, 0:r])
            i.then_inc(sem("vecT"), 1)
            pe.wait_ge(sem("ctx_in"), 16)
            for c in range(KC):
                if c % 2 == 0:
                    pe.wait_ge(sem("cev"), cnt(c // 2 - 1))
                for n in range(NTC):
                    i = tr(bank(4 + c // 2 % 2, P, (c % 2) * CTX + n * P), cin[:, n, c * P:(c + 1) * P], ident)
                if c % 2:
                    i.then_inc(sem("cT"), 1)
            pe.wait_ge(sem("x_in"), 16)
            for c in range(KC):
                pe.wait_ge(sem("xev"), cnt(c - 3))
                for n in range(NL):
                    i = tr(bank(c % 4, P, n * P), xin[:, n, c * P:(c + 1) * P], ident)
                i.then_inc(sem("xT"), 1)
            pe.wait_ge(sem("vec"), 1)
            pe.wait_ge(sem("cvec"), 2)
            pre_stat(0, CTX, 5)
            pre_stat(1, SEQ, 3)
            for j in range(8):
                if j % 4 == 0:
                    pe.wait_ge(sem(f"mod_a{j // 4}"), 64)
                if j >= 2:
                    pe.wait_ge(sem("mrow"), j - 1)
                for k in range(KC):
                    i = mm(bank(j % 2, UW)[0:2], cvec[:, k, :], mraw_a[j][:, k, :], start=k == 0, stop=k == KC - 1)
                i.then_inc(sem("mod_a"), 1)
            pe.wait_ge(sem("mrow"), 8)
            for m in range(16):
                i = tr(bank(7, 2, 2 * m), mod_row[0:2, m * P:(m + 1) * P], const[0:2, C_ID, 0:2])
            i.then_inc(sem("mod_turn"), 1)

            lat = 2
            pe.wait_ge(sem("w_lo"), 1)
            mm3_first([bank(4, CTX, r * CTX) for r in range(2)], 0, hc_hi, hc_lo, 0, (None, "ctx_tile"), True)
            mm3_first([bank(r) for r in range(2)], 0, h_hi, h_lo, KC, ("tile", "tile"))
            for u in range(1, U_WOUT):
                s = u % 2
                tiles = 1 if u == 5 else 2
                cols = lambda w, k, r: w[s][:, k, r * P:(r + 1) * P]
                pe.wait_ge(sem("w_lo"), u + 1)
                if u < 6:
                    if u >= 2:
                        pe.wait_ge(sem("ev"), cnt(EV[u - 2, "ctx"]))
                    for r in range(tiles):
                        i = mm3(bank(4 + u % 2, CTX, r * CTX), lambda w, k: cols(w, k, r), KC, hc_hi, hc_lo, s)
                    i.then_inc(sem("ctx_tile" if u < 5 else "tile"), 1)
                for r in range(tiles):
                    if lat >= 4:
                        pe.wait_ge(sem("ev"), cnt(EV_LAT[lat - 4]))
                    i = mm3(bank(lat % 4), lambda w, k: cols(w, k, r), KC, h_hi, h_lo, s)
                    i.then_inc(sem("tile"), 1)
                    lat += 1

                for m in mod_group(u - 1) + (mod_group(u) if u == U_WOUT - 1 else []):
                    pe.wait_ge(sem("mod_acc"), acc_b(m))
                    mod_column(m, macc_b[m % 4][:, :])
                if u == 7:
                    pe.wait_ge(sem("ev"), EV[5, "lat"])
                    for n in range(NT):
                        i = tr(bank(4, 16, 16 * n), ab[0:16, n * P:(n + 1) * P], const[0:16, C_ID, 0:16])
                    i.then_inc(sem("abT"), 1)
                if u == 10:
                    pe.wait_ge(sem("g"), 1)
                    gm = smallv[:, 0].rearrange("p n c -> p (n c)")
                    for j, w in enumerate((C(C_TRI), C(C_TRI + 1), ones)):
                        i = mm(bank(5, 8 * NT, 64 * j), w, gm, start=True, stop=True)
                    i.then_inc(sem("gsum"), 1)

            def item_rows(e):
                n = items[e][1]
                b = 2 * (e % 2)
                pe.wait_ge(sem("nrc"), item_group(e) + 1)
                pe.wait_ge(sem("nrm"), cnt(e - 1))
                for j in range(n // P):
                    c0 = item_col(e, j)
                    if e < 8:
                        i = mm(bank(b, P, j * P), nsm[:, c0:c0 + 1].to_broadcast([P, P]), ident, start=True, stop=True)
                    else:
                        for half in range(2):
                            i = mm(bank(b, P, j * P)[HD * half:HD * (half + 1)],
                                   nsm[:, c0 + half:c0 + half + 1].to_broadcast([P, HD]), ident, start=True, stop=True)
                i.then_inc(sem("nrow"), 1)

            for g, es in enumerate(ITEM_GROUPS):
                for e in es:
                    n = items[e][1]
                    pe.wait_ge(sem("nsq"), e + 1)
                    if e == ITEM_GROUPS[1][0]:
                        pe.wait_ge(sem("gcv"), 3)
                    for j in range(n // P):
                        i = mm(bank(4 + g % 2, 1 if e < 8 else 2, item_col(e, j)), sqt[e % 2][:, j * P:(j + 1) * P],
                               ones[:, 0:1] if e < 8 else const[:, C_BLK, 0:P:HD], start=True, stop=True)
                    i.then_inc(sem("nst"), 1)
                if g:
                    for e in ITEM_GROUPS[g - 1]:
                        item_rows(e)
            for e in ITEM_GROUPS[-1]:
                item_rows(e)

            def mod_columns(q):
                for j in mod_at(q, 4):
                    pe.wait_ge(sem("mod_acc"), acc_c(j))
                    for part in range(2):
                        mod_column(48 + 2 * j + part, mraw_c[j % MSLOTS][:, 0, part * P:(part + 1) * P])

            pe.wait_ge(sem("dn_ready"), 1)
            for s in range(NT):
                for d in range(2):
                    k = 2 * s + d
                    n = CHUNK_ORDER[d][s]
                    T, b0 = DT[d], 3 * d
                    tok = slice(n * P, (n + 1) * P)
                    pe.wait_ge(sem("S"), cnt(2 * (s - 1) + d + 1 if s else 0))
                    pe.wait_ge(sem("vn"), cnt(2 * (s - 1) + d + 1 if s else 0))
                    for h in range(HEADS):
                        i = mm(bank(b0, P, h * P), smallv[:, 0, n, 4 * d + h:4 * d + h + 1].to_broadcast([P, P]),
                               C(C_TRI + d), start=True, stop=True)
                    i.then_inc(sem("gc"), 1)
                    for h in range(HEADS):
                        i = mm(bank(b0 + 1, P, h * P), kT[:, h, tok], kT[:, h, tok], start=True, stop=True)
                    i.then_inc(sem("G"), 1)
                    if n >= NTC:
                        ql = slice((n - NTC) * P, (n - NTC + 1) * P)
                        for h in range(HEADS):
                            i = mm(bank(b0 + 2, P, h * P), kT[:, h, tok], qT[:, h, ql], start=True, stop=True)
                        i.then_inc(sem("QK"), 1)
                for d in range(2):
                    k, n, b0 = 2 * s + d, CHUNK_ORDER[d][s], 3 * d
                    tok = slice(n * P, (n + 1) * P)
                    pe.wait_ge(sem("GA"), k + 1)
                    for h in range(HEADS):
                        i = tr(bank(b0 + 1, P, h * P), kT[:, h, tok], ident)
                    i.then_inc(sem("Ktr"), 1)
                    if n >= NTC:
                        pe.wait_ge(sem("QB"), cnt(k - 3))
                    for h in range(HEADS):
                        i = tr(bank(b0 + 2, P, h * P), vT[:, h, tok], ident)
                    i.then_inc(sem("Vtr"), 1)
                for l in range(LEVELS):
                    for d in range(2):
                        T, q = DT[d], (s * LEVELS + l) * 2 + d
                        pe.wait_ge(sem("Bl"), q + 1)
                        if l:
                            pe.wait_ge(sem("TU"), cnt(q - 1))
                        else:
                            pe.wait_ge(sem("TU0"), 2 * s + d + 1)
                            if CHUNK_ORDER[d][s] >= NTC:
                                pe.wait_ge(sem("egr"), cnt(2 * s + d - 3))
                        for h in range(HEADS):
                            i = mm(bank(3 * d, P, h * P), T["bl"][:, h, :], T["tu"][:, h, :], start=True, stop=True)
                        i.then_inc(sem("Z"), 1)
                    for d in range(2):
                        T, q, b0 = DT[d], (s * LEVELS + l) * 2 + d, 3 * d
                        pe.wait_ge(sem("Zs"), q + 1)
                        if l == 0:
                            pe.wait_ge(sem("bv"), 2 * s + d + 1)
                        for h in range(HEADS):
                            mm(bank(b0 + 1, P, h * P), T["tu"][:, 4 + h, :], T["zs"][:, h, :], start=True, stop=True)
                        for h in range(HEADS):
                            i = mm(bank(b0 + 2, P, h * P), T["zs"][:, h, :], T["tu"][:, 4 + h, :], start=True, stop=True)
                        i.then_inc(sem("dTU"), 1)
                    mod_columns(s * LEVELS + l)
                for d in range(2):
                    T, k = DT[d], 2 * s + d
                    pe.wait_ge(sem("TU"), cnt((s + 1) * LEVELS * 2 - 1 + d))
                    pe.wait_ge(sem("L"), k + 1)
                    for h in range(HEADS):
                        i = mm(bank(3 * d, P, h * P), T["ta"][:, h, :], f32(T["tu"][:, h, :]), start=True, stop=True)
                    i.then_inc(sem("LU"), 1)
                for d in range(2):
                    T, k = DT[d], 2 * s + d
                    pe.wait_ge(sem("R2"), k + 1)
                    for h in range(HEADS):
                        i = mm(bank(3 * d + 1, P, h * P), T["tu"][:, 4 + h, :], T["bl"][:, h, :], start=True, stop=True)
                    i.then_inc(sem("dN"), 1)
                for d in range(2):
                    T, k = DT[d], 2 * s + d
                    pe.wait_ge(sem("Uf"), k + 1)
                    for h in range(HEADS):
                        i = mm(bank(3 * d + 2, P, h * P), T["kbvn"][:, h, :], T["uf"][:, h, :], start=True, stop=True)
                    i.then_inc(sem("WT"), 1)
                for d in range(2):
                    T, k = DT[d], 2 * s + d
                    pe.wait_ge(sem("nW"), k + 1)
                    for h in range(HEADS):
                        i = mm(bank(3 * d, P, h * P), T["uf"][:, h, :], T["bv"][:, h, :], start=True, stop=s == 0)
                        if s:
                            i = mm(bank(3 * d, P, h * P), T["nw"][:, h, :], S[d][:, h, :], start=False, stop=True)
                    i.then_inc(sem("vnp"), 1)
                for d in range(2):
                    T, k, n = DT[d], 2 * s + d, CHUNK_ORDER[d][s]
                    pe.wait_ge(sem("vn"), k + 1)
                    if n >= NTC:
                        pe.wait_ge(sem("intra"), cnt(k - 3))
                        pe.wait_ge(sem("qg"), cnt(k - 3))
                        for h in range(HEADS):
                            mm(bank(3 * d + 1, P, h * P), S[d][:, h, :], T["qg"][:, h, :], start=True, stop=False)
                            i = mm(bank(3 * d + 1, P, h * P), T["kbvn"][:, h, :], T["tb"][:, h, :], start=False, stop=True)
                        i.then_inc(sem("o"), 1)
                    for h in range(HEADS):
                        i = mm(bank(3 * d + 2, P, h * P), T["kd"][:, h, :], T["kbvn"][:, h, :], start=True, stop=True)
                    i.then_inc(sem("Sp"), 1)
            for q in range(LEVELS * NT, LEVELS * NT + 5):
                mod_columns(q)
            for h in range(HEADS):
                pe.wait_ge(sem("osq"), h + 1)
                pe.wait_ge(sem("osd"), cnt(h - 1))
                mm(bank(h % 2), ones, tmp[h % 2][:, :], start=True, stop=True).then_inc(sem("ost"), 1)
            for n in range(NT):
                i = tr(bank(2 + n // 4, P, P * (n % 4)), av[:, n * P:(n + 1) * P], ident)
            i.then_inc(sem("Vatr"), 1)

            NQ = SEQ // P

            def turn(i):
                pe.wait_ge(sem("Pn"), i + 1)
                pe.wait_ge(sem("PT"), i)
                for n in range(NT):
                    j = tr(bank(4 + n // 4, P, P * (n % 4)), prob[i % 3][:, n * P:(n + 1) * P], ident)
                j.then_inc(sem("Ptr"), 1)

            def values(hh):
                pe.wait_ge(sem("PT"), NQ * (hh + 1))
                if hh >= 1:
                    pe.wait_ge(sem("mix0"), HEADS + hh)
                b = bank(6)
                for n in range(NT):
                    mm(b, Vh[:, n, :], PTh[hh % 2][:, n, :], start=n == 0, stop=False)
                    mm(b, Vh[:, n, :], PTl[hh % 2][:, n, :], start=False, stop=False)
                    j = mm(b, Vl[:, n, :], PTh[hh % 2][:, n, :], start=False, stop=n == NT - 1)
                j.then_inc(sem("pv"), 1)

            pe.wait_ge(sem("Va"), 1)
            pe.wait_ge(sem("osd"), HEADS)
            for i in range(A_HEADS * NQ + NQ):
                if i >= 2 * NQ - 1 and i % NQ == NQ - 1:
                    values(i // NQ - 1)
                if i < A_HEADS * NQ:
                    hh, qt = divmod(i, NQ)
                    t, half = hh % 4, hh // 4
                    r = slice(HD * half, HD * (half + 1))
                    pe.wait_ge(sem("expd"), cnt(i - 1))
                    b = 2 * (i % 2)
                    mm(bank(b), aq[r, t, qt * P:(qt + 1) * P], ak[r, 0:512], start=True, stop=True)
                    mm(bank(b + 1, CTX), aq[r, t, qt * P:(qt + 1) * P], ak[r, 512:768], start=True, stop=True).then_inc(sem("sc"), 1)
                if 2 <= i < A_HEADS * NQ + 2:
                    turn(i - 2)

            tcol = lambda r: (lambda w, k: w[slot[0]][:, k, r * P:(r + 1) * P])
            slot = [0]

            def out_units(u0, yq):
                def body(i):
                    for s in range(2):
                        slot[0] = s
                        pe.wait_ge(sem("w_lo"), 2 * i + (u0 + s + 1))
                        for r in range(2):
                            t = 4 * i + (2 * s + r)
                            pe.wait_ge(sem("yev"), cnt(t + (8 * yq - 3)))
                            mm3(bank(2 * s + r), tcol(r), KC, mix_hi, mix_lo, s).then_inc(sem("tile"), 1)
                rep(pe, 2, body, peel=yq == 0)

            def ffn(f, U_UP, U_DOWN, yq):
                def up_pair(i, par, j0, first=False):
                    for part in range(2):
                        slot[0] = part
                        if first and part == 0:
                            pe.wait_ge(sem("w_lo"), U_UP + 1)
                            mm3_first([bank(r) for r in range(2)], 0, h_hi, h_lo, KC * H_FFN[f], ("tile", "tile"))
                            continue
                        pe.wait_ge(sem("w_lo"), 2 * i + (U_UP + 2 * j0 + part + 1))
                        for r in range(2):
                            pe.wait_ge(sem(("g" if part else "c3") + "_free"), cnt(2 * i + (FC * f + 2 * j0 + r - 3)))
                            mm3(bank(4 * par + 2 * part + r), tcol(r), KC, h_hi, h_lo, part).then_inc(sem("tile"), 1)

                def up4(i):
                    for par in range(2):
                        up_pair(2 * i, par, par, first=isinstance(i, int) and i == par)
                rep(pe, FC // 4, up4, peel=1)
                up_pair(0, 0, FC // 2 - 1)
                pe.wait_ge(sem("mid"), FC * (f + 1))

                def down2(i):
                    for q in range(6):
                        slot[0] = q % 2
                        k0, nk = DCH[q % 3]
                        p = q // 3
                        pe.wait_ge(sem("w_lo"), 6 * i + (U_DOWN + q + 1))
                        for r in range(2):
                            if q % 3 == 0:
                                t = 4 * i + (2 * p + r)
                                pe.wait_ge(sem("yev"), cnt(t + (8 * yq - 3)))
                            mm3(bank(2 * p + r), tcol(r), nk, mid_hi, mid_lo, q % 2, k0,
                                    q % 3 == 0, q % 3 == 2).then_inc(sem("tile"), 1)
                rep(pe, 2, down2)

            def boundary(idx):
                post_stat(idx)
                if idx < 8:
                    pe.wait_ge(sem("x_new"), KC * ((idx - 2) // 2 + 1))
                    pre_stat(idx + 1, SEQ, 5)

            pe.wait_ge(sem("mix0"), HEADS + A_HEADS)
            out_units(U_WOUT, 0)
            boundary(2)
            ffn(0, U_UP0, U_DOWN0, 1)
            boundary(4)

            def cx(i, par, j0):
                for part in range(2):
                    slot[0] = part
                    if isinstance(i, int) and i == j0 == part == 0:
                        pe.wait_ge(sem("w_lo"), U_SCIN + 1)
                        mm3_first([bank(r) for r in range(2)], 0, h_hi, h_lo, KC * H_SC, ("tile", "tile"))
                        continue
                    pe.wait_ge(sem("w_lo"), 2 * i + (U_SCIN + 2 * j0 + part + 1))
                    for r in range(2):
                        pe.wait_ge(sem("scu" if part else "scc"), cnt(2 * i + (2 * j0 + r - 3)))
                        mm3(bank(4 * par + 2 * part + r), tcol(r), KC, h_hi, h_lo, part).then_inc(sem("tile"), 1)

            def cx2(i):
                for par in range(2):
                    cx(2 * i, par, par)
            rep(pe, 2, cx2, peel=1)
            pe.wait_ge(sem("scu"), KC)

            def gate_b(i):
                for s in range(2):
                    slot[0] = s
                    pe.wait_ge(sem("w_lo"), 2 * i + (U_SCIN + 8 + s + 1))
                    for r in range(2):
                        pe.wait_ge(sem("scb"), cnt(4 * i + (2 * s + r - 3)))
                        mm3(bank(2 * s + r), tcol(r), KC, h_hi, h_lo, s).then_inc(sem("tile"), 1)
            rep(pe, 2, gate_b, peel=1)
            pe.wait_ge(sem("mix1"), KC)
            out_units(U_SCOUT, 2)
            boundary(6)
            ffn(1, U_UP1, U_DOWN1, 3)
            boundary(8)
            pe.wait_ge(sem("x_new"), 4 * KC)
            for n in range(NL):
                for half in range(2):
                    for c in range(4):
                        i = tr(bank(2 * n + half, P, c * P), x[:, 4 * half + c, n * P:(n + 1) * P], ident)
                    i.then_inc(sem("out_T"), 1)

        @block.scalar
        def _(act):
            def split_hi(u, s):
                act.wait_ge(sem(f"w_raw{s}"), rawcount(u, s))
                act.wait_ge(sem("tile"), cnt(2 * u - 2))
                nc.scalar.activation(whi[s][:, :], raw[s][:, :], ACT.Copy).then_inc(sem("w_hi"), 1)

            def squares(idx, src, n, waits):
                t4 = ctmp if idx == 0 else tmp
                for c in range(KC):
                    waits(c)
                    if c >= 3 and c % 2:
                        act.wait_ge(sem("sqcol"), sq_cols(idx) + c // 2)
                    if c >= 4 and c % 2 == 0:
                        act.wait_ge(sem("sqadd"), sq_adds(idx) + c // 2 - 1)
                    nc.scalar.activation(t4[2 if c == 0 else c % 2][:, 0:n], src(c), ACT.Square).then_inc(sem("sq"), 1)

            def deviation(idx, n):
                act.wait_ge(sem("stat"), idx + 1)
                cols = slice(NL * idx, NL * idx + n // P)
                nc.scalar.activation(dev[:, cols], bank(6)[:, cols], ACT.Sqrt, scale=1.0 / D_MODEL,
                                     bias=eps[:, :]).then_inc(sem("sd"), 1)

            def h_high(hb, out_, n, shift):
                for c in range(KC):
                    act.wait_ge(sem("t"), KC * hb + c + 1)
                    nc.scalar.activation(out_[:, c, :], (ctmp if hb == 0 else tmp)[c % 2][:, 0:n], ACT.Identity, bias=shift(c)).then_inc(sem("h_hi"), 1)

            act.wait_ge(sem("vec"), 1)
            for w, row in enumerate((V_C, V_CCTX)):
                nc.scalar.activation(cvec[:, :, w], vec[:, 0, row:row + KC], ACT.Silu).then_inc(sem("cvec"), 1)
            squares(0, lambda c: xc[:, c, :], CTX, lambda c: act.wait_ge(sem("cev"), c // 2 + 1))
            deviation(0, CTX)
            squares(1, lambda c: x[:, c, :], SEQ, lambda c: (act.wait_ge(sem("xev"), c + 1), act.wait_ge(sem("stat"), 1)))
            deviation(1, SEQ)
            act.wait_ge(sem("mod_a"), 8)
            split_hi(0, 0)
            split_hi(1, 1)
            h_high(0, hc_hi, CTX, lambda c: modv[:, 0, c, 1:2])
            h_high(1, h_hi, SEQ, lambda c: modv[:, 0, c, 0:1])

            def products(slot):
                for k in range(KC):
                    i = nc.scalar.activation(slot[:, k, :], slot[:, k, :], ACT.Copy, scale=cvec[:, k, 0:1])
                i.then_inc(sem("mod_prod"), 1)

            dnw = lambda k, j: vec[:, 2, 12 * k + j:12 * k + j + 1]
            for u in range(U_WOUT):
                act.wait_ge(sem("tile"), 2 * u + 2)
                if u + 2 < U_WOUT:
                    split_hi(u + 2, u % 2)
                jobs = list(conv_jobs(u))
                for stream, r, dst, ps, j in jobs:
                    if stream == "ctx":
                        act.wait_ge(sem("ctx_tile"), u + 1)
                    else:
                        act.wait_ge(sem("tile"), 2 * u + r + 1)
                    nc.scalar.activation(dst, ps, ACT.Copy, scale=dnw(1, j)).then_inc(sem("cv1"), 1)
                for stream, r, dst, _, _ in jobs:
                    act.wait_ge(sem("ev"), EVENTS.index((u, stream, r)) + 1)
                    nc.scalar.activation(dst, dst, ACT.Silu).then_inc(sem("cvs"), 1)
                if u in (8, 9):
                    for r in range(2):
                        hd = 2 * (u - 8) + r
                        act.wait_ge(sem("ev"), EVENTS.index((u, "lat", r)) + 1)
                        nc.scalar.activation(gT[:, hd, :], gT[:, hd, :], ACT.Silu).then_inc(sem("gate"), 1)
                for m in mod_group(u):
                    act.wait_ge(sem(f"mod_in{m % 4}"), landed(m % 4, True)((m - 16) // 4))
                    products(mraw_b[m % 4])
                if u == 8:
                    z, e1 = smallv[:, 7], smallv[:, 6]
                    act.wait_ge(sem("abt"), 1)
                    nc.scalar.activation(smallv[:, 1], abt[:, :, 8:16], ACT.Sigmoid).then_inc(sem("beta"), 1)
                    act.wait_ge(sem("z"), 1)
                    nc.scalar.activation(e1, z, ACT.Abs).then_inc(sem("gate_a"), 1)
                    act.wait_ge(sem("gate_a"), 1)
                    nc.scalar.activation(e1, e1, ACT.Exp, scale=-1.0).then_inc(sem("gate_a"), 1)
                    act.wait_ge(sem("gate_in"), 32)
                    nc.scalar.activation(alog[:, 0:8], alog[:, 0:8], ACT.Exp).then_inc(sem("ea"), 1)
                    act.wait_ge(sem("gate_a"), 2)
                    nc.scalar.activation(e1, e1, ACT.Ln, bias=const[:, C_ONE, 0:1]).then_inc(sem("gate_a"), 1)

            def group_sd(g):
                act.wait_ge(sem("nst"), ITEM_GROUPS[g][-1] + 1)
                nc.scalar.activation(nsm[:, item_cols[g]], bank(4 + g % 2)[:, item_cols[g]], ACT.Sqrt,
                                     scale=1.0 / HD if g == 2 else 1.0, bias=eps[:, :]).then_inc(sem("nsd"), 1)

            for e, (t, n) in enumerate(items):
                act.wait_ge(sem("cvs"), N_CONV)
                act.wait_ge(sem("ev"), len(EVENTS))
                if e >= 2:
                    act.wait_ge(sem("nst"), e - 1)
                nc.scalar.activation(sqt[e % 2][:, 0:n], t, ACT.Square).then_inc(sem("nsq"), 1)
                if e in (5, 9):
                    group_sd(e // 4 - 1)
            group_sd(2)
            act.wait_ge(sem("gcv"), 3)
            for j in range(3):
                nc.scalar.activation(smallv[:, 3 + j], smallv[:, 3 + j], ACT.Exp).then_inc(sem("ge"), 1)

            for s in range(NT):
                for d in range(2):
                    k, n, T = 2 * s + d, CHUNK_ORDER[d][s], DT[d]
                    act.wait_ge(sem("dA"), k + 1)
                    nc.scalar.activation(T["ta"][:, :, :], T["ta"][:, :, :], ACT.Exp).then_inc(sem("EA"), 1)
                    if n >= NTC:
                        act.wait_ge(sem("dB"), cnt(k - 3))
                        nc.scalar.activation(T["tb"][:, :, :], T["tb"][:, :, :], ACT.Exp).then_inc(sem("EB"), 1)
                        nc.scalar.activation(T["kbvn"][:, :, :].rearrange("p h t -> p (h t)"), bank(3 * d), ACT.Exp).then_inc(sem("egr"), 1)
                for l in range(LEVELS):
                    for d in range(2):
                        T, q = DT[d], (s * LEVELS + l) * 2 + d
                        act.wait_ge(sem("Z"), q + 1)
                        nc.scalar.activation(T["zs"][:, :, :].rearrange("p h t -> p (h t)"), bank(3 * d), ACT.Copy).then_inc(sem("Zs"), 1)
                    for j in mod_at(s * LEVELS + l, 0):
                        act.wait_ge(sem(f"mod_in{j % MSLOTS}"), landed(j % MSLOTS, False)(j // MSLOTS))
                        products(mraw_c[j % MSLOTS])
                for d in range(2):
                    T, k = DT[d], 2 * s + d
                    act.wait_ge(sem("WT"), k + 1)
                    nc.scalar.activation(T["nw"][:, :, :].rearrange("p h t -> p (h t)"), bank(3 * d + 2), ACT.Copy, scale=-1.0).then_inc(sem("nW"), 1)
                for d in range(2):
                    T, k = DT[d], 2 * s + d
                    act.wait_ge(sem("vnp"), k + 1)
                    nc.scalar.activation(T["kbvn"][:, :, :].rearrange("p h t -> p (h t)"), bank(3 * d), ACT.Copy).then_inc(sem("vn"), 1)
            for h in range(HEADS):
                act.wait_ge(sem("oe"), 8)
                act.wait_ge(sem("ost"), cnt(h - 1))
                act.wait_ge(sem("mod_done"), MODS - 16)
                nc.scalar.activation(tmp[h % 2][:, :], oT[:, h, :], ACT.Square).then_inc(sem("osq"), 1)
                act.wait_ge(sem("ost"), h + 1)
                act.wait_ge(sem("on"), cnt(h - 1))
                nc.scalar.activation(tmp[2 + h % 2][:, :], bank(h % 2), ACT.Sqrt, scale=1.0 / DK, bias=eps[:, :]).then_inc(sem("osd"), 1)
            for h in range(HEADS):
                act.wait_ge(sem("on"), h + 1)
                nc.scalar.activation(mix_hi[:, h, :], oT[:, h, :], ACT.Copy).then_inc(sem("on_hi"), 1)
            act.wait_ge(sem("Vatr"), 1)
            nc.scalar.activation(Vh[:, :, :].rearrange("p n t -> p (n t)"), bank(2, ALL), ACT.Copy).then_inc(sem("Vah"), 1)

            NQ = SEQ // P

            def turn_hi(i):
                hh, qt = divmod(i, NQ)
                act.wait_ge(sem("Ptr"), i + 1)
                if hh >= 2:
                    act.wait_ge(sem("pv"), cnt(hh - 1))
                nc.scalar.activation(PTh[hh % 2][:, :, qt * P:(qt + 1) * P], bank(4, ALL).rearrange("p (n t) -> p n t", t=P), ACT.Copy).then_inc(sem("PTh"), 1)

            def head_hi(hh):
                half, t = hh // 4, hh % 4
                r = slice(HD * half, HD * (half + 1))
                act.wait_ge(sem("pv"), hh + 1)
                nc.scalar.activation(mix_hi[r, 4 + t, :], bank(6)[r], ACT.Copy).then_inc(sem("ahh"), 1)

            for i in range(A_HEADS * NQ + NQ + 1):
                if i < A_HEADS * NQ:
                    act.wait_ge(sem("mx"), i + 1)
                    act.wait_ge(sem("Ptr"), cnt(i - 2))
                    nc.scalar.activation(prob[i % 3][:, :], bank(2 * (i % 2), ALL), ACT.Exp, scale=HD ** -0.5, bias=stat[:, 32 + i:33 + i], accum_out=stat[:, 64 + i:65 + i]).then_inc(sem("expd"), 1)
                if 2 <= i < A_HEADS * NQ + 2:
                    turn_hi(i - 2)
                if i >= 2 * NQ and i % NQ == 0:
                    head_hi(i // NQ - 2)
                if i == A_HEADS * NQ:
                    act.wait_ge(sem("mod_done"), 2 * MODS - 16)
                    split_hi(U_WOUT, 0)
                    split_hi(U_WOUT + 1, 1)

            def y_squares(u0, yq):
                def body(i):
                    for s in range(2):
                        act.wait_ge(sem("tile"), 4 * i + (2 * u0 + 2 * s + 2))
                        split_hi(2 * i + (u0 + s + 2), s)
                        for r in range(2):
                            t = 4 * i + (2 * s + r)
                            act.wait_ge(sem("sqadd"), t + (sq_adds(2 + 2 * yq) - 1))
                            act.wait_ge(sem("yev"), t + (8 * yq + 1))
                            nc.scalar.activation(tmp[r][:, :], ytile(t), ACT.Square).then_inc(sem("sq"), 1)
                rep(act, 2, body)

            def boundary(idx, hb, shift):
                deviation(idx, SEQ)
                if idx < 8:
                    act.wait_ge(sem("x_new"), cnt(KC * ((idx - 2) // 2) + 1))
                    squares(idx + 1, lambda c: x[:, c, :], SEQ,
                            lambda c: act.wait_ge(sem("x_new"), cnt(KC * ((idx - 2) // 2) + c + 1)))
                    deviation(idx + 1, SEQ)
                    h_high(hb, h_hi, SEQ, shift)

            def ffn(f, U_UP, U_DOWN, yq):
                cw = lambda k, j: vec[:, 3 + f, bass.ds(j + 22 * k, 1)]

                def up_pair(i, par, j0):
                    tl = lambda r: 2 * i + (FC * f + 2 * j0 + r)
                    u = 2 * i + (U_UP + 2 * j0)
                    act.wait_ge(sem("tile"), 4 * i + (2 * (U_UP + 2 * j0) + 2))
                    split_hi(u + 2, 0)
                    for r in range(2):
                        act.wait_ge(sem("mid"), cnt(tl(r) - 3))
                        nc.scalar.activation(tmp[2 * par + r][:, :], bank(4 * par + r), ACT.Copy, scale=cw(1, 2 * i + (2 * j0 + r))).then_inc(sem("c1"), 1)
                    for r in range(2):
                        act.wait_ge(sem("c3_free"), tl(r) + 1)
                        nc.scalar.activation(tmp[2 * par + r][:, :], tmp[2 * par + r][:, :], ACT.Silu).then_inc(sem("sg"), 1)
                    act.wait_ge(sem("tile"), 4 * i + (2 * (U_UP + 2 * j0) + 4))
                    split_hi(u + 3, 1)
                    for r in range(2):
                        act.wait_ge(sem("g_free"), tl(r) + 1)
                        nc.scalar.activation(mid_hi[:, bass.ds(2 * i + (2 * j0 + r), 1), :].rearrange("p c t -> p (c t)"), tmp[2 * par + r][:, :], ACT.Copy).then_inc(sem("ghi"), 1)

                def up4(i):
                    for par in range(2):
                        up_pair(2 * i, par, par)
                rep(act, FC // 4, up4, peel=f == 0)
                up_pair(0, 0, FC // 2 - 1)

                def down2(i, last=False):
                    for q in range(6):
                        act.wait_ge(sem("tile"), 12 * i + (2 * (U_DOWN + q) + 2))
                        if not (last and q >= 4):
                            split_hi(6 * i + (U_DOWN + q + 2), q % 2)
                        if q % 3 == 2:
                            for r in range(2):
                                t = 4 * i + (2 * (q // 3) + r)
                                act.wait_ge(sem("sqadd"), t + (sq_adds(2 + 2 * yq) - 1))
                                act.wait_ge(sem("yev"), t + (8 * yq + 1))
                                nc.scalar.activation(tmp[r][:, :], ytile(t), ACT.Square).then_inc(sem("sq"), 1)
                if f == 0:
                    rep(act, 2, down2)
                else:
                    down2(0)
                    down2(1, True)

            y_squares(U_WOUT, 0)
            boundary(2, 2, lambda c: modv[:, 0, 3 * KC + c, 0:1])
            ffn(0, U_UP0, U_DOWN0, 1)
            boundary(4, 3, lambda c: modv[:, 1, c, 0:1])

            scw = lambda k, j: vec[:, 0, bass.ds(j + (V_SCCONV + 8 * k), 1)]

            def cx(i, par, j0):
                tl = lambda r: 2 * i + (2 * j0 + r)
                for part in range(2):
                    act.wait_ge(sem("tile"), 4 * i + (2 * (U_SCIN + 2 * j0 + part) + 2))
                    split_hi(2 * i + (U_SCIN + 2 * j0 + part + 2), part)
                    for r in range(2):
                        if part == 0:
                            act.wait_ge(sem("scv"), cnt(tl(r) - 3))
                            nc.scalar.activation(tmp[2 * par + r][:, :], bank(4 * par + r), ACT.Copy).then_inc(sem("scc"), 1)
                        else:
                            act.wait_ge(sem("scu"), tl(r) + 1)
                            nc.scalar.activation(cv[:, bass.ds(tl(r), 1), :].rearrange("p c t -> p (c t)"), tmp[2 * par + r][:, :], ACT.Copy, scale=scw(1, tl(r))).then_inc(sem("scv1"), 1)

            def cx2(i):
                for par in range(2):
                    cx(2 * i, par, par)
            rep(act, 2, cx2, peel=1)

            def gate_b(i):
                for s in range(2):
                    act.wait_ge(sem("tile"), 4 * i + (2 * (U_SCIN + 8 + s) + 2))
                    split_hi(2 * i + (U_SCIN + 8 + s + 2), s)
                    for r in range(2):
                        t = 4 * i + (2 * s + r)
                        act.wait_ge(sem("scb"), t + 1)
                        nc.scalar.activation(mix_hi[:, bass.ds(t, 1), :].rearrange("p c t -> p (c t)"), tmp[2 * s + r][:, :], ACT.Copy).then_inc(sem("mhi"), 1)
            rep(act, 2, gate_b)
            y_squares(U_SCOUT, 2)
            boundary(6, 4, lambda c: modv[:, 1, 3 * KC + c, 0:1])
            ffn(1, U_UP1, U_DOWN1, 3)
            boundary(8, 0, None)
            for n in range(NL):
                act.wait_ge(sem("out_T"), 2 * n + 1)
                nc.scalar.activation(xin[:, n, 0:512], bank(2 * n), ACT.Copy).then_inc(sem("out_ev_a"), 1)


        @block.vector
        def _(dve):
            V = nc.vector

            def split_lo(u, s):
                dve.wait_ge(sem("w_hi"), u + 1)
                V.tensor_tensor(wlo[s][:, :], raw[s][:, :], f32(whi[s][:, :]), ALU.subtract).then_inc(sem("w_lo"), 1)

            def rstd(idx, n):
                dve.wait_ge(sem("sd"), idx + 1)
                cols = slice(NL * idx, NL * idx + n // P)
                V.reciprocal(dev[:, cols], dev[:, cols]).then_inc(sem("rstd"), 1)

            def apply_pre(hb, X, t4, row, n, pre, shift, hi, lo):
                def low(c):
                    dve.wait_ge(sem("h_hi"), KC * hb + c + 1)
                    V.scalar_tensor_tensor(out=lo[:, c, :], in0=t4[c % 2][:, 0:n], scalar=shift(c),
                                               in1=f32(hi[:, c, :]), op0=ALU.add, op1=ALU.subtract).then_inc(sem("h"), 1)
                for c in range(KC):
                    if c >= 2:
                        low(c - 2)
                        dve.wait_ge(sem("h"), cnt(KC * hb + c - 1))
                    V.scalar_tensor_tensor(out=t4[c % 2][:, 0:n], in0=X(c), scalar=pre_w[:, pre, c:c + 1],
                                               in1=row, op0=ALU.mult, op1=ALU.mult).then_inc(sem("t"), 1)
                low(KC - 2)
                low(KC - 1)

            V.memset(eps[:, :], EPS)
            dve.wait_ge(sem("vecT"), 1)
            for k, r in enumerate(V_ROWS):
                i = V.tensor_copy(vec[:, k, 0:r], bank(7 if k < 4 else 6, r, P * (k % 4)))
            i.then_inc(sem("vec"), 1)
            for p in range(KC // 2):
                dve.wait_ge(sem("cT"), p + 1)
                V.tensor_copy(xc[:, 2 * p:2 * p + 2, :].rearrange("p c t -> p (c t)"), bank(4 + p % 2)).then_inc(sem("cev"), 1)
            for c in range(KC):
                dve.wait_ge(sem("xT"), c + 1)
                V.tensor_copy(x[:, c, :], bank(c % 4)).then_inc(sem("xev"), 1)
            rstd(0, CTX)
            rstd(1, SEQ)
            for j in range(8):
                dve.wait_ge(sem("mod_a"), j + 1)
                V.tensor_copy(mod_row[0:2, j * UW:(j + 1) * UW], bank(j % 2, UW)[0:2]).then_inc(sem("mrow"), 1)
            dve.wait_ge(sem("mod_turn"), 1)
            dve.wait_ge(sem("vec"), 1)
            V.tensor_tensor(modv[:, 0, 0:16, :], bank(7, 32).rearrange("p (m w) -> p m w", w=2),
                            bc(vec[:, 1, 0:16], 2), ALU.add).then_inc(sem("modv"), 1)
            dve.wait_ge(sem("modv"), 1)

            def pre_weights(k, l, m, w, row):
                return V.scalar_tensor_tensor(out=pre_w[:, k, :], in0=modv[:, l, m:m + KC, w], scalar=1.0,
                                              in1=vec[:, 0, row:row + KC], op0=ALU.add, op1=ALU.mult)
            pre_weights(0, 0, KC, 0, V_MIXPRE)
            pre_weights(4, 0, KC, 1, V_MIXPRE).then_inc(sem("norm_w"), 1)
            dve.wait_ge(sem("norm_w"), 1)
            split_lo(0, 0)
            split_lo(1, 1)
            dve.wait_ge(sem("rrow"), 2)
            apply_pre(0, lambda c: xc[:, c, :], ctmp, bank(5, CTX), CTX, 4, lambda c: modv[:, 0, c, 1:2], hc_hi, hc_lo)
            apply_pre(1, lambda c: x[:, c, :], tmp, bank(3), SEQ, 0, lambda c: modv[:, 0, c, 0:1], h_hi, h_lo)

            dnw = lambda k, j: vec[:, 2, 12 * k + j:12 * k + j + 1]
            n1 = n2 = 0
            for u in range(U_WOUT):
                if u + 2 < U_WOUT:
                    split_lo(u + 2, u % 2)
                jobs = list(conv_jobs(u))
                for stream in ("ctx", "lat"):
                    mine = [j for j in jobs if j[0] == stream]
                    for _, r, dst, ps, j in mine:
                        dve.wait_ge(sem("cv1"), cnt(n1 + 2 - r if stream == "ctx" else n1 + 1))
                        n = dst.shape[1]
                        V.scalar_tensor_tensor(out=dst[:, 1:n], in0=ps[:, 0:n - 1], scalar=dnw(0, j), in1=dst[:, 1:n],
                                                   op0=ALU.mult, op1=ALU.add).then_inc(sem("cv2"), 1)
                        n1 += 1
                    for _, r, dst, ps, j in mine:
                        dve.wait_ge(sem("cv2"), n2 + 1)
                        n = dst.shape[1]
                        V.scalar_tensor_tensor(out=dst[:, 0:n - 1], in0=ps[:, 1:n], scalar=dnw(2, j),
                                                   in1=dst[:, 0:n - 1], op0=ALU.mult, op1=ALU.add).then_inc(sem("ev"), 1)
                        n2 += 1
                if not jobs:
                    for e in EVENTS:
                        if e[0] != u:
                            continue
                        _, stream, r = e
                        cols = slice(0, CTX) if stream == "ctx" else slice(CTX, ALL)
                        ps = hyb_bank(*e)
                        if stream == "ctx":
                            dve.wait_ge(sem("ctx_tile" if u < 5 else "tile"), 5 if u < 5 else 11)
                        else:
                            dve.wait_ge(sem("tile"), 12 if u == 5 else 2 * u + r + 1)
                        if u == 4:
                            dst = (ak, av)[r][:, cols]
                        elif u == 5:
                            dst, ps = ab[0:16, cols], ps[0:16]
                        elif u < 10:
                            dst = gT[:, 2 * (u - 8) + r, :]
                        else:
                            dst = aq[:, 2 * (u - 10) + r, :]
                        V.tensor_copy(dst, ps).then_inc(sem("ev"), 1)
                if u == 8:
                    dve.wait_ge(sem("abT"), 1)
                    V.tensor_copy(abt[:, :, :].rearrange("p n c -> p (n c)"), bank(4, 16 * NT)).then_inc(sem("abt"), 1)
                    dve.wait_ge(sem("abt"), 1)
                    dve.wait_ge(sem("gate_in"), 32)
                    V.tensor_tensor(smallv[:, 7], abt[:, :, 0:8], bh(alog[:, 8:16], NT), ALU.add).then_inc(sem("z"), 1)
                    dve.wait_ge(sem("z"), 1)
                    V.tensor_scalar(smallv[:, 5], smallv[:, 7], 0.0, None, ALU.max).then_inc(sem("gate_v"), 1)
                if u == 9:
                    dve.wait_ge(sem("gate_v"), 1)
                    dve.wait_ge(sem("gate_a"), 3)
                    V.tensor_tensor(smallv[:, 5], smallv[:, 5], smallv[:, 6], ALU.add).then_inc(sem("gate_v"), 1)
                    dve.wait_ge(sem("gate_v"), 2)
                    dve.wait_ge(sem("ea"), 1)
                    V.scalar_tensor_tensor(out=smallv[:, 0], in0=smallv[:, 5], scalar=-1.0, in1=bh(alog[:, 0:8], NT),
                                           op0=ALU.mult, op1=ALU.mult).then_inc(sem("g"), 1)
            dve.wait_ge(sem("gsum"), 1)
            sums = bank(5, 192).rearrange("p (j n c) -> p j n c", j=3, c=8)[:, :, 0:NT]
            for k in (2, 3):
                for d in range(2):
                    i = V.tensor_copy(smallv[:, k, :, 4 * d:4 * d + 4], sums[:, d, :, 4 * d:4 * d + 4])
            i.then_inc(sem("gcv"), 1)
            dve.wait_ge(sem("gcv"), 1)
            V.tensor_tensor(smallv[:, 4], sums[:, 2], smallv[:, 2], ALU.subtract).then_inc(sem("gcv"), 1)
            V.tensor_copy(smallv[:, 5], sums[:, 2]).then_inc(sem("gcv"), 1)
            def normed(e):
                t, n = items[e]
                dve.wait_ge(sem("nrow"), e + 1)
                w = 1.0 if e < 4 else DK ** -0.5 if e < 8 else vec[:, 0, V_QN:V_QN + 1] if e < 12 else vec[:, 0, V_KN:V_KN + 1]
                V.scalar_tensor_tensor(out=t, in0=t, scalar=w, in1=bank(2 * (e % 2), n), op0=ALU.mult,
                                       op1=ALU.mult).then_inc(sem("nrm"), 1)

            for g in range(3):
                dve.wait_ge(sem("nsd"), g + 1)
                V.reciprocal(nsm[:, item_cols[g]], nsm[:, item_cols[g]]).then_inc(sem("nrc"), 1)
                if g:
                    for e in ITEM_GROUPS[g - 1]:
                        normed(e)
            for e in ITEM_GROUPS[-1]:
                normed(e)
            dve.wait_ge(sem("rope_in"), 32)
            for e in range(5):
                t, b = rope_tile(e), sqt[e % 2][:, 0:SEQ]
                dve.wait_ge(sem("nrm"), 9 + e)
                V.stream_shuffle(b, t, [j ^ 1 for j in range(32)]).then_inc(sem("shuf"), 1)
                dve.wait_ge(sem("shuf"), e + 1)
                V.tensor_tensor(b, b, sinT[:, :], ALU.mult).then_inc(sem("rsin"), 1)
                dve.wait_ge(sem("rsin"), e + 1)
                dve.wait_ge(sem("rcos"), e + 1)
                V.tensor_tensor(t, t, b, ALU.add).then_inc(sem("rope"), 1)
            dve.wait_ge(sem("ge"), 3)
            dve.wait_ge(sem("beta"), 1)
            V.tensor_tensor(smallv[:, 6], smallv[:, 1], smallv[:, 3], ALU.mult).then_inc(sem("dn_ready"), 1)
            dve.wait_ge(sem("dn_ready"), 1)

            per = lambda k, n, d: bc(smallv[:, k, n, 4 * d:4 * d + 4], P)
            pbank = lambda b: bank(b).rearrange("p (h t) -> p h t", t=P)
            for s in range(NT):
                for d in range(2):
                    k, n, T, b0 = 2 * s + d, CHUNK_ORDER[d][s], DT[d], 3 * d
                    dve.wait_ge(sem("gc"), k + 1)
                    V.tensor_tensor(T["ta"][:, :, :], per(2, n, d), pbank(b0), ALU.subtract).then_inc(sem("dA1"), 1)
                    dve.wait_ge(sem("dA1"), k + 1)
                    V.tensor_scalar(T["ta"][:, :, :], T["ta"][:, :, :], 0.0, None, ALU.min).then_inc(sem("dA"), 1)
                    if n >= NTC:
                        V.tensor_tensor(T["tb"][:, :, :], pbank(b0), per(2, n, d), ALU.subtract).then_inc(sem("dB1"), 1)
                        dve.wait_ge(sem("dB1"), k - 3)
                        V.tensor_scalar(T["tb"][:, :, :], T["tb"][:, :, :], 0.0, None, ALU.min).then_inc(sem("dB"), 1)
                for d in range(2):
                    k, n, T, b0 = 2 * s + d, CHUNK_ORDER[d][s], DT[d], 3 * d
                    V.tensor_copy(T["tu"][:, :, :], bh(ident, 8)).then_inc(sem("TU0"), 1)
                    dve.wait_ge(sem("G"), k + 1)
                    dve.wait_ge(sem("EA"), k + 1)
                    V.tensor_tensor(T["ta"][:, :, :], T["ta"][:, :, :], pbank(b0 + 1), ALU.mult).then_inc(sem("GA"), 1)
                    if n >= NTC:
                        dve.wait_ge(sem("QK"), cnt(k - 3))
                        dve.wait_ge(sem("EB"), cnt(k - 3))
                        V.tensor_tensor(T["tb"][:, :, :], T["tb"][:, :, :], pbank(b0 + 2), ALU.mult).then_inc(sem("QB"), 1)
                        dve.wait_ge(sem("egr"), cnt(k - 3))
                        V.tensor_tensor(T["qg"][:, :, :], qT[:, :, (n - NTC) * P:(n - NTC + 1) * P],
                                            T["kbvn"][:, :, :], ALU.mult).then_inc(sem("qg"), 1)
                for d in range(2):
                    k, n, T, b0 = 2 * s + d, CHUNK_ORDER[d][s], DT[d], 3 * d
                    dve.wait_ge(sem("Ktr"), k + 1)
                    if n >= NTC:
                        dve.wait_ge(sem("qg"), cnt(k - 3))
                    V.tensor_tensor(T["kbvn"][:, :, :], pbank(b0 + 1), per(6, n, d), ALU.mult).then_inc(sem("kb"), 1)
                    V.tensor_tensor(T["kd"][:, :, :], pbank(b0 + 1), per(4, n, d), ALU.mult).then_inc(sem("kb"), 1)
                    dve.wait_ge(sem("Vtr"), k + 1)
                    V.tensor_tensor(T["bv"][:, :, :], pbank(b0 + 2), per(1, n, d), ALU.mult).then_inc(sem("bv"), 1)
                for l in range(LEVELS):
                    for d in range(2):
                        T, q = DT[d], (s * LEVELS + l) * 2 + d
                        dve.wait_ge(sem("dTU"), q + 1)
                        V.tensor_tensor(T["tu"][:, :, :].rearrange("p h t -> p (h t)"),
                                            f32(T["tu"][:, :, :]).rearrange("p h t -> p (h t)"),
                                            bank(3 * d + 1, 1024), ALU.subtract).then_inc(sem("TU"), 1)
                for d in range(2):
                    T, k = DT[d], 2 * s + d
                    dve.wait_ge(sem("LU"), k + 1)
                    dve.wait_ge(sem("t0"), k + 1)
                    V.tensor_tensor(T["bl"][:, :, :], T["nw"][:, :, :], pbank(3 * d), ALU.subtract).then_inc(sem("R2"), 1)
                for d in range(2):
                    T, k = DT[d], 2 * s + d
                    dve.wait_ge(sem("dN"), k + 1)
                    V.tensor_tensor(T["uf"][:, :, :], f32(T["tu"][:, 0:4, :]), pbank(3 * d + 1), ALU.add).then_inc(sem("Uf"), 1)
                for d in range(2):
                    T, k, n = DT[d], 2 * s + d, CHUNK_ORDER[d][s]
                    if n >= NTC:
                        dve.wait_ge(sem("o"), cnt(k - 3))
                        dst = oT[:, :, (n - NTC) * P:(n - NTC + 1) * P]
                        if s < 4:
                            i = V.tensor_copy(dst, pbank(3 * d + 1))
                        else:
                            dve.wait_ge(sem("oe"), 4)
                            i = V.tensor_tensor(dst, dst, pbank(3 * d + 1), ALU.add)
                        i.then_inc(sem("oe"), 1)
                    dve.wait_ge(sem("Sp"), k + 1)
                    if s == 0:
                        i = V.tensor_copy(S[d][:, :, :], pbank(3 * d + 2))
                    else:
                        dve.wait_ge(sem("S"), cnt(k - 1))
                        for h in range(HEADS):
                            i = V.scalar_tensor_tensor(out=S[d][:, h, :], in0=S[d][:, h, :],
                                                       scalar=smallv[:, 5, n, 4 * d + h:4 * d + h + 1],
                                                       in1=bank(3 * d + 2, P, h * P), op0=ALU.mult, op1=ALU.add)
                    i.then_inc(sem("S"), 1)
            dve.wait_ge(sem("mod_done"), 2 * MODS - 16)
            V.tensor_tensor(modv[:, 0, 16:MODS, 0], bank(7, MODS - 16, 32), vec[:, 1, 16:MODS], ALU.add).then_inc(sem("modv"), 1)
            V.tensor_tensor(modv[:, 1, :, 0], bank(7, MODS, 16 + MODS), vec[:, 1, MODS:2 * MODS], ALU.add).then_inc(sem("modv"), 1)
            dve.wait_ge(sem("modv"), 3)
            pre_weights(1, 0, 4 * KC, 0, V_FFNPRE)
            pre_weights(2, 1, KC, 0, V_MIXPRE + KC)
            pre_weights(3, 1, 4 * KC, 0, V_FFNPRE + KC)
            for k, l, m, row in ((0, 0, 2, V_MIXPOST), (1, 0, 5, V_FFNPOST), (2, 1, 2, V_MIXPOST + KC), (3, 1, 5, V_FFNPOST + KC)):
                i = V.tensor_tensor(post_w[:, k, :], modv[:, l, m * KC:(m + 1) * KC, 0], vec[:, 0, row:row + KC], ALU.mult)
            i.then_inc(sem("norm_w"), 1)

            dve.wait_ge(sem("gate"), HEADS)
            for h in range(HEADS):
                dve.wait_ge(sem("osd"), h + 1)
                V.reciprocal(tmp[2 + h % 2][:, :], tmp[2 + h % 2][:, :]).then_inc(sem("orc"), 1)
                dve.wait_ge(sem("orc"), h + 1)
                V.scalar_tensor_tensor(out=oT[:, h, :], in0=oT[:, h, :], scalar=vec[:, 0, V_DNOUT:V_DNOUT + 1],
                                           in1=tmp[2 + h % 2][:, :], op0=ALU.mult, op1=ALU.mult).then_inc(sem("on1"), 1)
                dve.wait_ge(sem("on1"), h + 1)
                V.tensor_tensor(oT[:, h, :], oT[:, h, :], gT[:, h, :], ALU.mult).then_inc(sem("on"), 1)
            for h in range(HEADS):
                dve.wait_ge(sem("on_hi"), h + 1)
                V.tensor_tensor(mix_lo[:, h, :], oT[:, h, :], f32(mix_hi[:, h, :]), ALU.subtract).then_inc(sem("mix0"), 1)
            dve.wait_ge(sem("Vah"), 1)
            V.tensor_tensor(Vl[:, :, :].rearrange("p n t -> p (n t)"), bank(2, ALL),
                                f32(Vh[:, :, :]).rearrange("p n t -> p (n t)"), ALU.subtract).then_inc(sem("Va"), 1)

            NQ = SEQ // P

            def normalize(i):
                dve.wait_ge(sem("expd"), i + 1)
                V.reciprocal(stat[:, 96 + i:97 + i], stat[:, 64 + i:65 + i]).then_inc(sem("rc1"), 1)
                dve.wait_ge(sem("rc1"), i + 1)
                V.tensor_scalar(prob[i % 3][:, :], prob[i % 3][:, :], stat[:, 96 + i:97 + i], None, ALU.mult).then_inc(sem("Pn"), 1)

            def turn_lo(i):
                hh, qt = divmod(i, NQ)
                dve.wait_ge(sem("PTh"), i + 1)
                dst = slice(qt * P, (qt + 1) * P)
                V.tensor_tensor(PTl[hh % 2][:, :, dst], bank(4, ALL).rearrange("p (n t) -> p n t", t=P),
                                    f32(PTh[hh % 2][:, :, dst]), ALU.subtract).then_inc(sem("PT"), 1)

            def head_lo(hh):
                half, t = hh // 4, hh % 4
                r = slice(HD * half, HD * (half + 1))
                dve.wait_ge(sem("ahh"), hh + 1)
                V.tensor_tensor(mix_lo[r, 4 + t, :], bank(6)[r], f32(mix_hi[r, 4 + t, :]), ALU.subtract).then_inc(sem("mix0"), 1)

            for i in range(A_HEADS * NQ + NQ + 1):
                if 3 <= i < A_HEADS * NQ + 3:
                    turn_lo(i - 3)
                if i < A_HEADS * NQ:
                    dve.wait_ge(sem("sc"), i + 1)
                    V.tensor_reduce(stat[:, i:i + 1], bank(2 * (i % 2), ALL), AX.X, ALU.max).then_inc(sem("mx1"), 1)
                    dve.wait_ge(sem("mx1"), i + 1)
                    V.tensor_scalar(stat[:, 32 + i:33 + i], stat[:, i:i + 1], -HD ** -0.5, None, ALU.mult).then_inc(sem("mx"), 1)
                if 1 <= i <= A_HEADS * NQ:
                    normalize(i - 1)
                if i >= 2 * NQ and i % NQ == 0:
                    head_lo(i // NQ - 2)
                if i == A_HEADS * NQ:
                    split_lo(U_WOUT, 0)
                    split_lo(U_WOUT + 1, 1)

            def y_out(u0, yq):
                def body(i):
                    for s in range(2):
                        split_lo(2 * i + (u0 + s + 2), s)
                        for r in range(2):
                            dve.wait_ge(sem("tile"), 4 * i + (2 * (u0 + s) + r + 1))
                            V.tensor_copy(y[:, bass.ds(4 * i + (2 * s + r), 1), :].rearrange("p c t -> p (c t)"),
                                              bank(2 * s + r)).then_inc(sem("yev"), 1)
                rep(dve, 2, body)

            def boundary(idx, post, pre, hb, shift):
                rstd(idx, SEQ)
                dve.wait_ge(sem("rrow"), idx + 1)
                dve.wait_ge(sem("norm_w"), 2)
                dve.wait_ge(sem("yev"), cnt(KC * ((idx - 2) // 2 + 1)))
                b = KC * ((idx - 2) // 2)
                for c in range(KC + 1):
                    if c < KC:
                        V.scalar_tensor_tensor(out=y[:, c, :], in0=y[:, c, :], scalar=post_w[:, post, c:c + 1],
                                                   in1=bank(5), op0=ALU.mult, op1=ALU.mult).then_inc(sem("yn"), 1)
                    if c:
                        dve.wait_ge(sem("yn"), b + c)
                        V.tensor_tensor(x[:, c - 1, :], x[:, c - 1, :], y[:, c - 1, :], ALU.add).then_inc(sem("x_new"), 1)
                if idx < 8:
                    rstd(idx + 1, SEQ)
                    dve.wait_ge(sem("rrow"), idx + 2)
                    apply_pre(hb, lambda c: x[:, c, :], tmp, bank(5), SEQ, pre, shift, h_hi, h_lo)

            def conv(src, acc, w, name, count, last):
                for r in range(2):
                    V.scalar_tensor_tensor(out=acc(r)[:, 1:SEQ], in0=src(r)[:, 0:SEQ - 1], scalar=w(0, r),
                                               in1=acc(r)[:, 1:SEQ], op0=ALU.mult, op1=ALU.add).then_inc(sem(name), 1)
                for r in range(2):
                    dve.wait_ge(sem(name), count(r))
                    V.scalar_tensor_tensor(out=acc(r)[:, 0:SEQ - 1], in0=src(r)[:, 1:SEQ], scalar=w(2, r),
                                               in1=acc(r)[:, 0:SEQ - 1], op0=ALU.mult, op1=ALU.add).then_inc(sem(last), 1)

            def ffn(f, U_UP, U_DOWN, yq):
                def up_pair(i, par, j0):
                    tl = lambda r: 2 * i + (FC * f + 2 * j0 + r)
                    u = 2 * i + (U_UP + 2 * j0)
                    split_lo(u + 2, 0)
                    dve.wait_ge(sem("c1"), tl(1) + 1)
                    conv(lambda r: bank(4 * par + r), lambda r: tmp[2 * par + r],
                         lambda k, r: vec[:, 3 + f, bass.ds(2 * i + (2 * j0 + r + 22 * k), 1)],
                         "c2", lambda r: tl(r) + 1, "c3_free")
                    split_lo(u + 3, 1)
                    for r in range(2):
                        dve.wait_ge(sem("sg"), tl(r) + 1)
                        V.tensor_tensor(tmp[2 * par + r][:, :], tmp[2 * par + r][:, :], bank(4 * par + 2 + r), ALU.mult).then_inc(sem("g_free"), 1)
                    for r in range(2):
                        dve.wait_ge(sem("ghi"), tl(r) + 1)
                        j = 2 * i + (2 * j0 + r)
                        flat = lambda m: m[:, bass.ds(j, 1), :].rearrange("p c t -> p (c t)")
                        V.tensor_tensor(flat(mid_lo), tmp[2 * par + r][:, :], f32(flat(mid_hi)), ALU.subtract).then_inc(sem("mid"), 1)

                def up4(i):
                    for par in range(2):
                        up_pair(2 * i, par, par)
                rep(dve, FC // 4, up4)
                up_pair(0, 0, FC // 2 - 1)

                def down2(i, last=False):
                    for q in range(6):
                        if not (last and q >= 4):
                            split_lo(6 * i + (U_DOWN + q + 2), q % 2)
                        if q % 3 == 2:
                            for r in range(2):
                                dve.wait_ge(sem("tile"), 12 * i + (2 * (U_DOWN + q) + r + 1))
                                t = 4 * i + (2 * (q // 3) + r)
                                V.tensor_copy(y[:, bass.ds(t, 1), :].rearrange("p c t -> p (c t)"),
                                                  bank(2 * (q // 3) + r)).then_inc(sem("yev"), 1)
                if f == 0:
                    rep(dve, 2, down2)
                else:
                    down2(0)
                    down2(1, True)

            y_out(U_WOUT, 0)
            boundary(2, 0, 1, 2, lambda c: modv[:, 0, 3 * KC + c, 0:1])
            ffn(0, U_UP0, U_DOWN0, 1)
            boundary(4, 1, 2, 3, lambda c: modv[:, 1, c, 0:1])

            def cx(i, par, j0):
                tl = lambda r: 2 * i + (2 * j0 + r)
                flat = lambda r: cv[:, bass.ds(tl(r), 1), :].rearrange("p c t -> p (c t)")
                split_lo(2 * i + (U_SCIN + 2 * j0 + 2), 0)
                split_lo(2 * i + (U_SCIN + 2 * j0 + 3), 1)
                for r in range(2):
                    dve.wait_ge(sem("scc"), tl(r) + 1)
                    V.tensor_tensor(tmp[2 * par + r][:, :], tmp[2 * par + r][:, :], bank(4 * par + 2 + r), ALU.mult).then_inc(sem("scu"), 1)
                dve.wait_ge(sem("scu"), tl(1) + 1)
                dve.wait_ge(sem("scv1"), tl(1) + 1)
                conv(lambda r: tmp[2 * par + r], flat,
                     lambda k, r: vec[:, 0, bass.ds(2 * i + (2 * j0 + r + V_SCCONV + 8 * k), 1)],
                     "scv2", lambda r: tl(r) + 1, "scv")

            def cx2(i):
                for par in range(2):
                    cx(2 * i, par, par)
            rep(dve, 2, cx2)

            def gate_b(i):
                for s in range(2):
                    split_lo(2 * i + (U_SCIN + 8 + s + 2), s)
                    for r in range(2):
                        t = 4 * i + (2 * s + r)
                        dve.wait_ge(sem("tile"), 4 * i + (2 * (U_SCIN + 8 + s) + r + 1))
                        dve.wait_ge(sem("scv"), KC)
                        V.tensor_tensor(tmp[2 * s + r][:, :], bank(2 * s + r),
                                            cv[:, bass.ds(t, 1), :].rearrange("p c t -> p (c t)"), ALU.mult).then_inc(sem("scb"), 1)
                    for r in range(2):
                        t = 4 * i + (2 * s + r)
                        flat = lambda m: m[:, bass.ds(t, 1), :].rearrange("p c t -> p (c t)")
                        dve.wait_ge(sem("mhi"), t + 1)
                        V.tensor_tensor(flat(mix_lo), tmp[2 * s + r][:, :], f32(flat(mix_hi)), ALU.subtract).then_inc(sem("mix1"), 1)
            rep(dve, 2, gate_b)
            y_out(U_SCOUT, 2)
            boundary(6, 2, 3, 4, lambda c: modv[:, 1, 3 * KC + c, 0:1])
            ffn(1, U_UP1, U_DOWN1, 3)
            boundary(8, 3, None, None, None)
            for n in range(NL):
                dve.wait_ge(sem("out_T"), 2 * n + 2)
                V.tensor_copy(xin[:, n, 512:1024], bank(2 * n + 1)).then_inc(sem("out_ev_d"), 1)

        @block.gpsimd
        def _(pool):
            G = nc.gpsimd

            def pre_squares(idx):
                t4, n = (ctmp, CTX) if idx == 0 else (tmp, SEQ)
                for c in range(2, KC, 2):
                    pool.wait_ge(sem("sq"), KC * idx + c + 1)
                    if c > 2:
                        pool.wait_ge(sem("sqadd"), sq_adds(idx) + c // 2 - 1)
                    G.tensor_tensor(t4[2][:, 0:n], t4[2][:, 0:n], t4[c % 2][:, 0:n], ALU.add).then_inc(sem("sqadd"), 1)

            def post_squares(idx):
                pool.wait_ge(sem("stat"), idx)
                for c in range(KC):
                    pool.wait_ge(sem("sq"), KC * idx + c + 1)
                    if c == 0:
                        i = G.tensor_copy(tmp[2][:, :], tmp[0][:, :])
                    else:
                        pool.wait_ge(sem("sqadd"), sq_adds(idx) + c)
                        i = G.tensor_tensor(tmp[2][:, :], tmp[2][:, :], tmp[c % 2][:, :], ALU.add)
                    i.then_inc(sem("sqadd"), 1)

            def mod_add(n, dst, a, b):
                if n % 3:
                    pool.wait_ge(sem("mod_acc"), n)
                G.tensor_tensor(dst, a, b, ALU.add).then_inc(sem("mod_acc"), 1)

            def mod_half(n, slot):
                w = 4 >> (n % 3)
                mod_add(n, slot[:, 0:w, :], slot[:, 0:w, :], slot[:, w:2 * w, :])

            pre_squares(0)
            pre_squares(1)
            pool.wait_ge(sem("h"), KC)
            for m in range(16, MODS):
                pool.wait_ge(sem("mod_prod"), m - 15)
                mod_half(3 * (m - 16), mraw_b[m % 4])
                mod_half(3 * (m - 16) + 1, mraw_b[m % 4])
                if m >= 20:
                    pool.wait_ge(sem("mod_done"), m - 19)
                mod_add(3 * (m - 16) + 2, macc_b[m % 4][:, :], mraw_b[m % 4][:, 0, :], mraw_b[m % 4][:, 1, :])
            pool.wait_ge(sem("rope_in"), 32)
            for e in range(5):
                pool.wait_ge(sem("shuf"), e + 1)
                G.tensor_tensor(rope_tile(e), rope_tile(e), cosT[:, :], ALU.mult).then_inc(sem("rcos"), 1)

            def mod_level(q):
                for lag, parts in ((3, (1, 2)), (2, (0,))):
                    for j in mod_at(q, lag):
                        pool.wait_ge(sem("mod_prod"), MODS - 16 + j + 1)
                        for part in parts:
                            mod_half(3 * (MODS - 16 + j) + part, mraw_c[j % MSLOTS])

            pool.wait_ge(sem("dn_ready"), 1)
            for s in range(NT):
                for d in range(2):
                    k, n, T = 2 * s + d, CHUNK_ORDER[d][s], DT[d]
                    pool.wait_ge(sem("GA"), k + 1)
                    G.tensor_tensor(T["ta"][:, :, :], T["ta"][:, :, :], bc(smallv[:, 1, n, 4 * d:4 * d + 4], P), ALU.mult).then_inc(sem("Lb"), 1)
                    pool.wait_ge(sem("Lb"), k + 1)
                    G.tensor_tensor(T["ta"][:, :, :], T["ta"][:, :, :], bh(C(C_STRICT + d), HEADS), ALU.mult).then_inc(sem("L"), 1)
                for l in range(LEVELS):
                    for d in range(2):
                        T, q, k = DT[d], (s * LEVELS + l) * 2 + d, 2 * s + d
                        if l == 0:
                            pool.wait_ge(sem("L"), k + 1)
                            pool.wait_ge(sem("dN"), cnt(k - 1))
                        else:
                            pool.wait_ge(sem("Z"), cnt(q - 1))
                        G.tensor_tensor(T["bl"][:, :, :], T["ta"][:, :, :], bh(C(C_LVL + LEVELS * d + l), HEADS), ALU.mult).then_inc(sem("Bl"), 1)
                    if l == 1:
                        for d in range(2):
                            k, n, T = 2 * s + d, CHUNK_ORDER[d][s], DT[d]
                            if n >= NTC:
                                pool.wait_ge(sem("QB"), cnt(k - 3))
                                G.tensor_tensor(T["tb"][:, :, :], T["tb"][:, :, :], bh(C(C_TRI + d), HEADS), ALU.mult).then_inc(sem("intra"), 1)
                    mod_level(s * LEVELS + l)
                for d in range(2):
                    T, k = DT[d], 2 * s + d
                    pool.wait_ge(sem("TU"), cnt((s + 1) * LEVELS * 2 - 1 + d))
                    G.tensor_tensor(T["nw"][:, :, :], bh(ident, HEADS), f32(T["tu"][:, 0:4, :]), ALU.subtract).then_inc(sem("t0"), 1)
            for q in range(LEVELS * NT, LEVELS * NT + 4):
                mod_level(q)
            for idx in range(2, 9):
                if idx in POST:
                    post_squares(idx)
                else:
                    pre_squares(idx)


def constants():
    c = np.zeros((P, NCONST, P), np.float32)
    i = np.arange(P)
    r, q = i[:, None], i[None, :]
    c[:, C_ID] = r == q
    c[:, C_ONE] = 1
    c[:, C_TRI], c[:, C_TRI + 1] = r <= q, r >= q
    c[:, C_STRICT], c[:, C_STRICT + 1] = r > q, r < q
    for l in range(LEVELS):
        s = 1 << l
        low = (r // (2 * s) == q // (2 * s)) & (r // s % 2 == 1) & (q // s % 2 == 0)
        c[:, C_LVL + l], c[:, C_LVL + LEVELS + l] = low, low.T
    c[:, C_BLK] = r // HD == q // HD
    t = np.arange(SEQ)
    inv = (np.float32(ROPE_THETA) ** (-np.arange(0, HD // 2, 2, dtype=np.float32) / np.float32(HD // 2))).astype(np.float32)
    ang = np.concatenate([(t // GRID_W).astype(np.float32)[:, None] * inv, (t % GRID_W).astype(np.float32)[:, None] * inv], 1)
    pair = (i % HD) // 2
    cos = np.cos(ang).T[pair].astype(np.float32)
    sin = np.sin(ang).T[pair].astype(np.float32) * np.where(i % 2 == 0, -1, 1).astype(np.float32)[:, None]
    return {"const": c.reshape(P, NCONST * P), "cos": np.ascontiguousarray(cos), "sin": np.ascontiguousarray(sin)}


_INS = ['x', 'c', 'ctx', 'c_ctx', 'mod_w', 'mod_b', 'norm_mix_pre', 'norm_mix_post', 'norm_ffn_pre', 'norm_ffn_post',
        'hyb_w_in', 'hyb_w_out', 'dn_conv_w', 'dn_a_log', 'dn_dt_bias', 'dn_out_norm', 'att_q_norm', 'att_k_norm',
        'sc_w_in', 'sc_conv_w', 'sc_w_out', 'ffn_w_up', 'ffn_conv_w', 'ffn_w_down']


def kernel(**inputs):
    import concourse.bacc as bacc
    from concourse.bass_utils import run_bass_kernel_spmd

    nc = bacc.Bacc("TRN2", target_bir_lowering=False, num_devices=1)
    arrays = {name: np.ascontiguousarray(inputs[name]) for name in _INS}
    arrays.update(constants())
    args = {name: nc.dram_tensor(f"in_{name}", a.shape, mybir.dt.from_np(a.dtype), kind="ExternalInput").ap()
            for name, a in arrays.items()}
    out = nc.dram_tensor("out", (1, SEQ, D_MODEL), F32, kind="ExternalOutput").ap()
    hybrid_trunk(nc, args, out)
    r = run_bass_kernel_spmd(nc, [{f"in_{name}": a for name, a in arrays.items()}], core_ids=[0])
    return r.results[0]["out"]
```

```python
import numpy as np
from contextlib import ExitStack

import concourse.bass as bass
from concourse import mybir

F32 = mybir.dt.float32
F32R = mybir.dt.float32r
ALU = mybir.AluOpType
ACT = mybir.ActivationFunctionType
AX = mybir.AxisListType

P = 128
D_MODEL, SEQ, CTX = 1024, 512, 256
ALL = CTX + SEQ
EPS = 1e-6
KC = D_MODEL // P
D_FF = 2816
FC = D_FF // P
HEADS, DK = 4, 128
A_HEADS, HD = 8, 64
GRID_W, ROPE_THETA = 64, 10000.0
NT = ALL // P
NTC = CTX // P
NL = NT - NTC
LEVELS = 7
CHUNK_ORDER = [[0, 1, 2, 3, 4, 5], [1, 0, 5, 4, 3, 2]]
MODS = 6 * KC

C_ID, C_ONE, C_TRI, C_STRICT, C_LVL, C_BLK = 0, 1, 2, 4, 6, 6 + 2 * LEVELS
NCONST = C_BLK + 1

V_MIXPRE, V_MIXPOST, V_FFNPRE, V_FFNPOST = 0, 16, 32, 48
V_C, V_CCTX, V_DNOUT, V_QN, V_KN, V_SCCONV = 64, 72, 80, 81, 82, 83
V_ROWS = [V_SCCONV + 24, 96, 36, 66, 66]

O_ALPHA, O_AK = 1024, 1040
O_Q, O_G, O_AQ = 1296, 1808, 2320

UW = 256
U_WOUT, U_UP0, U_DOWN0 = 12, 16, 38
U_SCIN, U_SCOUT, U_UP1, U_DOWN1 = 50, 62, 66, 88
MSLOTS = 6
H_SC, H_FFN = 3, (2, 4)
POST = (0, 1, 2, 4, 6, 8)
DCH = [(0, 8), (8, 7), (15, 7)]


def hybrid_trunk(nc, A, out):
    ctx = ExitStack()
    with ctx:
        base = [(nc.sbuf_base + 31) // 32 * 32]
        end = nc.sbuf_usable_end

        def place(name, cols, dt=F32, at=None):
            off = base[0] if at is None else at
            t = nc.alloc_sbuf_tensor_at(name, [P, cols], dt, offset=off)
            if at is None:
                base[0] += (cols * 4 + 31) // 32 * 32
            assert off + cols * 4 <= end, (name, off + cols * 4, end)
            return t

        def view(tile, pat, **k):
            return tile[:, :].rearrange(pat, **k)

        const = view(place("const", NCONST * P), "p (k n) -> p k n", n=P)
        x = view(place("x", KC * SEQ), "p (c t) -> p c t", t=SEQ)
        vec = view(place("vec", 5 * P), "p (k n) -> p k n", n=P)
        modv = view(place("modv", 2 * MODS * 2), "p (l m w) -> p l m w", l=2, w=2)
        cvec = view(place("cvec", KC * 2), "p (k w) -> p k w", w=2)
        pre_w = view(place("pre_w", 5 * KC), "p (k c) -> p k c", c=KC)
        post_w = view(place("post_w", 4 * KC), "p (k c) -> p k c", c=KC)
        eps = place("eps", 1)
        odev = place("head_dev", HEADS * NL)
        dev = place("norm_dev", 9 * NL)
        ring_at = base[0]
        raw = [place(f"w_raw{i}", KC * UW) for i in range(2)]
        whi = [place(f"w_hi{i}", KC * UW, F32R) for i in range(2)]
        wlo = [place(f"w_lo{i}", KC * UW, F32R) for i in range(2)]
        tmp_at = base[0]
        tmp = [place(f"tmp{i}", SEQ) for i in range(4)]
        R = base[0]
        K = 1024

        def region(name, cols, at, dt=F32):
            return place(name, cols, dt, R + int(at * K))

        h_hi = view(region("h_hi", KC * SEQ, 88, F32R), "p (c t) -> p c t", t=SEQ)
        h_lo = view(region("h_lo", KC * SEQ, 104, F32R), "p (c t) -> p c t", t=SEQ)
        y = view(region("y", KC * SEQ, 88), "p (c t) -> p c t", t=SEQ)
        mid_hi = view(region("mid_hi", FC * SEQ, 0, F32R), "p (c t) -> p c t", t=SEQ)
        mid_lo = view(region("mid_lo", FC * SEQ, 44, F32R), "p (c t) -> p c t", t=SEQ)
        mix_hi = view(region("mix_hi", KC * SEQ, 0, F32R), "p (c t) -> p c t", t=SEQ)
        mix_lo = view(region("mix_lo", KC * SEQ, 16, F32R), "p (c t) -> p c t", t=SEQ)
        cv = view(region("cv", KC * SEQ, 32), "p (c t) -> p c t", t=SEQ)
        xin = view(region("xin", NL * D_MODEL, 0), "p (n c) -> p n c", c=D_MODEL)
        cin = view(region("cin", NTC * D_MODEL, 16), "p (n c) -> p n c", c=D_MODEL)
        vrow = view(region("vrow", 5 * P, 24), "p (k n) -> p k n", n=P)
        ctmp = [region(f"ctmp{i}", CTX, 48 + i) for i in range(4)]
        mraw_a = [view(place(f"mod_raw_a{i}", KC * UW, F32, a0), "p (k n) -> p k n", n=UW) for i, a0 in
                  enumerate([ring_at + KC * UW * 4 * j for j in range(2, 6)] + [R + j * K for j in (32, 40, 96, 104)])]
        mod_row = region("mod_row", 16 * P, 88)
        mraw_b = [view(place(f"mod_raw_b{i}", KC * P, F32, a0), "p (k n) -> p k n", n=P)
                  for i, a0 in enumerate((tmp_at, tmp_at + 4 * K, R + 73 * K, R + 77 * K))]
        macc_b = [region(f"mod_acc_b{i}", P, 85 + i / 2) for i in range(4)]
        mraw_c = [view(place(f"mod_raw_c{i}", KC * UW, F32, ring_at + KC * UW * 4 * i), "p (k n) -> p k n", n=UW)
                  for i in range(MSLOTS)]
        hc_hi = view(region("hc_hi", KC * CTX, 57, F32R), "p (c t) -> p c t", t=CTX)
        hc_lo = view(region("hc_lo", KC * CTX, 65, F32R), "p (c t) -> p c t", t=CTX)
        xc = view(region("xc", KC * CTX, 73), "p (c t) -> p c t", t=CTX)
        kT = view(region("kT", HEADS * ALL, 0), "p (h t) -> p h t", t=ALL)
        qT = view(region("qT", HEADS * SEQ, 12), "p (h t) -> p h t", t=SEQ)
        vT = view(region("vT", HEADS * ALL, 20), "p (h t) -> p h t", t=ALL)
        gT = view(region("gT", HEADS * SEQ, 32), "p (h t) -> p h t", t=SEQ)
        aq = view(region("aq", HEADS * SEQ, 40), "p (h t) -> p h t", t=SEQ)
        ak = region("ak", ALL, 48)
        av = region("av", ALL, 51)
        ab = region("ab", ALL, 54)
        nsm = region("item_dev", 96, 57)
        sqt = [region(f"sqt{i}", ALL, 63 + 3 * i) for i in range(2)]
        cosT = region("cosT", SEQ, 58)
        sinT = region("sinT", SEQ, 60)
        oT = view(region("oT", HEADS * SEQ, 57), "p (h t) -> p h t", t=SEQ)
        S = [view(region(f"S{d}", HEADS * P, 65 + 2 * d), "p (h t) -> p h t", t=P) for d in range(2)]
        smallv = view(region("dn_small", 8 * NT * 8, 69), "p (k n c) -> p k n c", k=8, c=8)
        abt = view(region("abt", NT * 16, 70.5), "p (n c) -> p n c", c=16)
        alog = region("alog", 16, 87)
        DT = []
        spots = [88 + 2 * i for i in range(12)], [112, 114, 116, 118] + [71 + 2 * i for i in range(8)]
        for d in range(2):
            t, free = {}, list(spots[d])
            for n in ("tu", "zs", "bl", "ta", "tb", "qg", "kbvn", "bv", "kd", "nw", "uf"):
                a0 = free.pop(0)
                w = HEADS * P
                if n == "tu":
                    free.pop(0)
                    w *= 2
                v = region(f"dn_{n}{d}", w, a0, F32R if n in ("tu", "zs", "bl") else F32)
                t[n] = view(v, "p (h t) -> p h t", t=P)
            DT.append(t)
        PTh = [view(region(f"PTh{i}", NT * SEQ, a0, F32R), "p (n t) -> p n t", t=SEQ) for i, a0 in enumerate((88, 57))]
        PTl = [view(region(f"PTl{i}", NT * SEQ, a0, F32R), "p (n t) -> p n t", t=SEQ) for i, a0 in enumerate((100, 69))]
        prob = [region(f"prob{i}", ALL, a0) for i, a0 in enumerate((81, 84, 54))]
        stat = region("att_stat", 4 * 32, 112)
        Vh = view(region("Vh", NT * P, 114, F32R), "p (n t) -> p n t", t=P)
        Vl = view(region("Vl", NT * P, 117, F32R), "p (n t) -> p n t", t=P)

        PS = ctx.enter_context(nc.psum_tensor("ps", [P, 8 * 512], F32))

        def bank(b, n=512, o=0):
            return PS[:, b * 512 + o:b * 512 + o + n]

        sems = {}

        def sem(name):
            if name not in sems:
                sems[name] = ctx.enter_context(nc.semaphore(name))
            return sems[name]

        def rep(eng, n, body, peel=0):
            for i in range(peel):
                body(i)
            if n - peel > 1:
                with eng.Fori(peel, n) as i:
                    body(i)
            elif n > peel:
                body(peel)

        def cnt(value):
            return max(value, 0) if isinstance(value, int) else value

        def mod_group(u):
            return [m for g in range(16) if 2 + g * 10 // 16 == u for m in (16 + 2 * g, 17 + 2 * g)]

        def acc_b(m):
            return 3 * (m - 15)

        def acc_c(j):
            return 3 * (MODS - 16 + j + 1)

        def landed(i, phase_b):
            return lambda n: 16 * (n + 1 + (0 if phase_b or i >= 4 else (MODS - 16) // 4))

        def z_count(s, l, d):
            return (s * (LEVELS - 1) + l - 1) * 2 + d + 1

        MOD_LEVEL = [LEVELS * (j // 4) + 2 * (j % 4) for j in range(MODS // 2)]

        def mod_at(q, lag):
            return [j for j, q0 in enumerate(MOD_LEVEL) if q0 + lag == q]

        def sq_adds(idx):
            return sum(KC if i in POST else 3 for i in range(idx))

        def sq_cols(idx):
            return sum(0 if i in POST else 4 for i in range(idx))

        def rawcount(u, s):
            if isinstance(u, int):
                return sum(16 * (3 if 12 <= v < 16 else 4 if v in (10, 11) else 1) for v in range(s, u + 1, 2))
            return 8 * (u - s) + 16 + 112

        C = lambda k, n=1: const[:, k:k + n, :].rearrange("p k n -> p (k n)")
        ident, ones = C(C_ID), C(C_ONE)
        rv = [view(t, "p (k n) -> p k n", n=UW) for t in raw]
        wh = [view(t, "p (k n) -> p k n", n=UW) for t in whi]
        wl = [view(t, "p (k n) -> p k n", n=UW) for t in wlo]
        f32 = lambda a: a.bitcast(F32)
        ytile = lambda t: y[:, bass.ds(t, 1), :].rearrange("p c t -> p (c t)")

        def bc(a, n):
            return a.unsqueeze(2).to_broadcast([a.shape[0], a.shape[1], n])

        def bh(a, n):
            return a.unsqueeze(1).to_broadcast([a.shape[0], n, a.shape[1]])

        EVENTS = [(u, stream, r) for u in range(U_WOUT) for stream in (("ctx", "lat") if u < 6 else ("lat",))
                  for r in range(1 if u == 5 else 2)]
        EV = {(u, stream): n + 1 for n, (u, stream, r) in enumerate(EVENTS)}
        EV_LAT = [n + 1 for n, (u, stream, r) in enumerate(EVENTS) if stream == "lat"]
        LAT_BANK = {e[::2]: n % 4 for n, e in enumerate(e for e in EVENTS if e[1] == "lat")}
        N_CONV = 20

        def hyb_bank(u, stream, r):
            return bank(4 + u % 2, CTX, r * CTX) if stream == "ctx" else bank(LAT_BANK[u, r])

        def conv_jobs(u):
            if u < 4 or u in (6, 7):
                kind, first = (kT, 0) if u < 2 else (vT, 4) if u < 4 else (qT, 8)
                for stream in ("ctx", "lat") if u < 4 else ("lat",):
                    for r in range(2):
                        hd = 2 * (u % 2) + r
                        cols = slice(0, SEQ) if u > 4 else slice(0, CTX) if stream == "ctx" else slice(CTX, ALL)
                        yield stream, r, kind[:, hd, cols], hyb_bank(u, stream, r), first + hd

        items = ([(kT[:, h, :], ALL) for h in range(HEADS)] + [(qT[:, h, :], SEQ) for h in range(HEADS)]
                 + [(aq[:, h, :], SEQ) for h in range(HEADS)] + [(ak[:, :], ALL)])

        ITEM_GROUPS = [range(0, 4), range(4, 8), range(8, 13)]
        ITEM_BANK = (6, 4, 5)
        ITEMS_IN = {6: (0,), 7: (1, 2), 8: (3,), 9: (4, 5), 10: (6, 7), 11: (8, 9)}

        def item_group(e):
            return min(e // 4, 2)

        def item_col(e, j):
            return e * NT + j if e < 4 else 4 * NT + (e - 4) * NL + j if e < 8 else 4 * (NT + NL) + 2 * (NL * (e - 8) + j)

        item_cols = [slice(0, 4 * NT), slice(4 * NT, 4 * (NT + NL)), slice(4 * (NT + NL), 4 * (NT + NL) + 8 * NL + 2 * NT)]

        def att_part(l):
            if l < 4:
                return aq[:, l, :], item_col(8 + l, 0), vec[:, 0, V_QN:V_QN + 1]
            cols, j = ((slice(CTX, ALL), NTC), (slice(0, CTX), 0))[l - 4]
            return ak[:, cols], item_col(12, j), vec[:, 0, V_KN:V_KN + 1]

        def rope_tile(e):
            return aq[:, e, :] if e < 4 else ak[:, CTX:ALL]

        block = ctx.enter_context(nc.Block())


        @block.sync
        def _(sp):
            w_in = A["hyb_w_in"][0].rearrange("(k p) n -> p k n", p=P)
            w_out = A["hyb_w_out"][0]
            sc_in = A["sc_w_in"][0].rearrange("(k p) n -> p k n", p=P)
            sc_out = A["sc_w_out"][0].rearrange("(k p) n -> p k n", p=P)
            up = [A["ffn_w_up"][f].rearrange("(k p) n -> p k n", p=P) for f in range(2)]
            down = [A["ffn_w_down"][f].rearrange("(k p) n -> p k n", p=P) for f in range(2)]

            sp.dma_start(const[:, :, :].rearrange("p k n -> p (k n)"), A["const"]).then_inc(sem("const_in"), 16)
            rows = lambda a: a.rearrange("l (c p) -> (l c) p", p=P)
            for k, r, a in ((0, V_MIXPRE, rows(A["norm_mix_pre"])), (0, V_MIXPOST, rows(A["norm_mix_post"])),
                            (0, V_FFNPRE, rows(A["norm_ffn_pre"])), (0, V_FFNPOST, rows(A["norm_ffn_post"])),
                            (0, V_C, rows(A["c"])), (0, V_CCTX, A["c_ctx"].rearrange("(c p) -> c p", p=P)),
                            (0, V_DNOUT, A["dn_out_norm"]), (0, V_SCCONV, rows(A["sc_conv_w"][0])),
                            (1, 0, rows(A["mod_b"])), (2, 0, rows(A["dn_conv_w"][0])),
                            (3, 0, rows(A["ffn_conv_w"][0])), (4, 0, rows(A["ffn_conv_w"][1]))):
                sp.dma_start(vrow[r:r + a.shape[0], k, :], a).then_inc(sem("vec_in"), 16)
            for half in range(2):
                sp.dma_start(vrow[V_QN:V_QN + 1, 0, half * HD:(half + 1) * HD], A["att_q_norm"]).then_inc(sem("vec_in"), 16)
                sp.dma_start(vrow[V_KN:V_KN + 1, 0, half * HD:(half + 1) * HD], A["att_k_norm"]).then_inc(sem("vec_in"), 16)
            sp.dma_start(cin[:, :, :], A["ctx"][0].rearrange("(n p) c -> p n c", p=P)).then_inc(sem("ctx_in"), 16)
            sp.dma_start(xin[:, :, :], A["x"][0].rearrange("(n p) c -> p n c", p=P)).then_inc(sem("x_in"), 16)

            def load_mod(m):
                src = A["mod_w"][m // MODS].rearrange("(k p) n -> p k n", p=P)[:, :, (m % MODS) * P:(m % MODS + 1) * P]
                """Modulation tile m, 16 to 47."""
                if m >= 20:
                    sp.wait_ge(sem("mod_acc"), acc_b(m - 4))
                sp.dma_start(mraw_b[m % 4][:, :, :], src).then_inc(sem(f"mod_in{m % 4}"), 16)

            def load_mod_pair(j):
                s = j % MSLOTS
                src = A["mod_w"][1].rearrange("(k p) n -> p k n", p=P)[:, :, j * UW:(j + 1) * UW]
                if j >= MSLOTS:
                    sp.wait_ge(sem("mod_done"), MODS - 16 + 2 * (j - MSLOTS + 1))
                sp.dma_start(mraw_c[s][:, :, :], src).then_inc(sem(f"mod_in{s}"), 16)

            def raw_free(u):
                sp.wait_ge(sem("w_lo"), cnt(u - 1))

            for j in range(8):
                src = A["mod_w"][0].rearrange("(k p) n -> p k n", p=P)[:, :, j * UW:(j + 1) * UW]
                sp.dma_start(mraw_a[j][:, :, :], src).then_inc(sem(f"mod_a{j // 2}"), 16)
            for u in range(2):
                sp.dma_start(rv[u][:, :, :], w_in[:, :, u * UW:(u + 1) * UW]).then_inc(sem(f"w_raw{u}"), 16)
            sp.dma_start(alog[:, 0:8], A["dn_a_log"][0].rearrange("d h -> (d h)").unsqueeze(0).to_broadcast([P, 8])).then_inc(sem("gate_in"), 16)
            sp.dma_start(alog[:, 8:16], A["dn_dt_bias"][0].rearrange("d h -> (d h)").unsqueeze(0).to_broadcast([P, 8])).then_inc(sem("gate_in"), 16)
            for u in range(2, 12):
                s = u % 2
                if u == 4:
                    sp.wait_ge(sem("h"), 2 * KC)
                if u >= 5:
                    for m in mod_group(u - 3):
                        load_mod(m)
                raw_free(u)
                if u < 4:
                    sp.dma_start(rv[s][:, :, :], w_in[:, :, u * UW:(u + 1) * UW]).then_inc(sem(f"w_raw{s}"), 16)
                elif u == 4:
                    sp.dma_start(rv[s][:, :, :], w_in[:, :, O_AK:O_AK + UW]).then_inc(sem(f"w_raw{s}"), 16)
                elif u == 5:
                    sp.dma_start(rv[s][:, :, 0:P], w_in[:, :, O_ALPHA:O_ALPHA + P]).then_inc(sem(f"w_raw{s}"), 16)
                elif u < 8:
                    sp.dma_start(rv[s][:, :, :], w_in[:, :, O_Q + (u - 6) * UW:O_Q + (u - 5) * UW]).then_inc(sem(f"w_raw{s}"), 16)
                elif u < 10:
                    sp.dma_start(rv[s][:, :, :], w_in[:, :, O_G + (u - 8) * UW:O_G + (u - 7) * UW]).then_inc(sem(f"w_raw{s}"), 16)
                else:
                    for r in range(2):
                        for a in range(2):
                            o, to = O_AQ + a * 4 * HD + (2 * (u - 10) + r) * HD, r * P + a * HD
                            sp.dma_start(rv[s][:, :, to:to + HD], w_in[:, :, o:o + HD]).then_inc(sem(f"w_raw{s}"), 16)

            def load_wout(u):
                s, q = u % 2, u - U_WOUT
                raw_free(u)
                cols = slice(q * UW, (q + 1) * UW)
                sp.dma_start(rv[s][:, 0:4, :], w_out[0:512, cols].rearrange("(k p) n -> p k n", p=P)).then_inc(sem(f"w_raw{s}"), 16)
                for a in range(2):
                    part = w_out[512 + 256 * a:768 + 256 * a, cols]
                    sp.dma_start(rv[s][HD * a:HD * (a + 1), 4:8, :], part.rearrange("(t p) n -> p t n", p=HD)).then_inc(sem(f"w_raw{s}"), 16)

            for u in range(9, 12):
                for m in mod_group(u):
                    load_mod(m)
            sp.wait_ge(sem("tile"), 2 * U_WOUT)
            sp.dma_start(cosT[:, :], A["cos"]).then_inc(sem("rope_in"), 16)
            sp.dma_start(sinT[:, :], A["sin"]).then_inc(sem("rope_in"), 16)
            sp.wait_ge(sem("mod_acc"), acc_b(MODS - 1))
            for j in range(MODS // 2):
                load_mod_pair(j)
            sp.wait_ge(sem("mod_done"), 2 * MODS - 16)
            load_wout(12)
            load_wout(13)
            load_wout(14)
            load_wout(15)

            def ffn_loads(f, U_UP, U_DOWN):
                def upb(i):
                    for part in range(2):
                        u = 2 * i + (U_UP + part)
                        raw_free(u)
                        o = i * UW
                        sp.dma_start(rv[part][:, :, :], up[f][:, :, bass.ds(o + part * D_FF, UW)]).then_inc(sem(f"w_raw{part}"), 16)
                rep(sp, FC // 2, upb)

                def downb(i):
                    for q in range(6):
                        u = 6 * i + (U_DOWN + q)
                        k0, nk = DCH[q % 3]
                        raw_free(u)
                        o = i * (2 * UW) + (q // 3) * UW
                        sp.dma_start(rv[q % 2][:, 0:nk, :], down[f][:, k0:k0 + nk, bass.ds(o, UW)]).then_inc(sem(f"w_raw{q % 2}"), 16)
                rep(sp, 2, downb)

            ffn_loads(0, U_UP0, U_DOWN0)

            def cxb(i):
                for part in range(2):
                    raw_free(2 * i + (U_SCIN + part))
                    sp.dma_start(rv[part][:, :, :], sc_in[:, :, bass.ds(i * UW + (1 + part) * D_MODEL, UW)]).then_inc(sem(f"w_raw{part}"), 16)
            rep(sp, 4, cxb)

            def sqb(src, U0):
                def body(i):
                    for s in range(2):
                        raw_free(2 * i + (U0 + s))
                        sp.dma_start(rv[s][:, :, :], src[:, :, bass.ds(i * (2 * UW) + s * UW, UW)]).then_inc(sem(f"w_raw{s}"), 16)
                rep(sp, 2, body)
            sqb(sc_in, U_SCIN + 8)
            sqb(sc_out, U_SCOUT)
            ffn_loads(1, U_UP1, U_DOWN1)
            for n in range(NL):
                sp.wait_ge(sem("out_ev_a"), n + 1)
                sp.wait_ge(sem("out_ev_d"), n + 1)
                sp.dma_start(out[0, n * P:(n + 1) * P, :], xin[:, n, :]).then_inc(sem("stored"), 16)
            sp.wait_ge(sem("stored"), 16 * NL)

        @block.tensor
        def _(pe):
            mm, tr = nc.tensor.matmul, nc.tensor.transpose

            def mm3(dst, cols, nk, xh, xl, s, k0=0, first=True, last=True):
                for k in range(nk):
                    hi, lo = cols(wh, k), cols(wl, k)
                    mm(dst, hi, xh[:, k0 + k, :], start=first and k == 0, stop=False)
                    mm(dst, hi, xl[:, k0 + k, :], start=False, stop=False)
                    i = mm(dst, lo, xh[:, k0 + k, :], start=False, stop=last and k == nk - 1)
                return i

            def mm3_first(banks, s, xh, xl, h_count, names, shared=False):
                for k in range(KC):
                    pe.wait_ge(sem("h"), h_count + k + 1)
                    for r, b in enumerate(banks):
                        hi, lo = (w[s][:, k, r * P:(r + 1) * P] for w in (wh, wl))
                        own = r == 0 or not shared
                        mm(b, hi, xh[:, k, :], start=k == 0 and own, stop=False)
                        mm(b, hi, xl[:, k, :], start=False, stop=False)
                        i = mm(b, lo, xh[:, k, :], start=False, stop=k == KC - 1 and (r == 1 or not shared))
                        if k == KC - 1 and names[r]:
                            i.then_inc(sem(names[r]), 1)

            def mod_column(m, acc):
                mm(bank(7, 1, 16 + m), acc, ones[:, 0:1], start=True, stop=True).then_inc(sem("mod_done"), 1)

            def sum_columns(sq, idx, n, first, last):
                for j in range(n // P):
                    i = mm(bank(6, 1, NL * idx + j), sq[:, j * P:(j + 1) * P], ones[:, 0:1],
                           start=first and j == 0, stop=last and j == n // P - 1)
                return i

            def rows(idx, n, b):
                pe.wait_ge(sem("rstd"), idx + 1)
                for j in range(n // P):
                    i = mm(bank(b, P, j * P), dev[:, NL * idx + j:NL * idx + j + 1].to_broadcast([P, P]), ident,
                           start=True, stop=True)
                i.then_inc(sem("rrow"), 1)

            def pre_stat(idx, n, b):
                t4 = tmp
                for c in range(1, KC, 2):
                    pe.wait_ge(sem("sq"), KC * idx + c + 1)
                    sum_columns(t4[c % 2], idx, n, c == 1, False).then_inc(sem("sqcol"), 1)
                pe.wait_ge(sem("sqadd"), sq_adds(idx + 1))
                sum_columns(t4[2], idx, n, False, True).then_inc(sem("stat"), 1)
                rows(idx, n, b)

            def post_stat(idx, n=SEQ, b=5):
                pe.wait_ge(sem("sqadd"), sq_adds(idx + 1))
                sum_columns((tmp if idx else ctmp)[2], idx, n, True, True).then_inc(sem("stat"), 1)
                rows(idx, n, b)

            pe.wait_ge(sem("const_in"), 16)
            pe.wait_ge(sem("vec_in"), 16 * 16)
            for k, r in enumerate(V_ROWS):
                i = tr(bank(7 if k < 4 else 6, r, P * (k % 4)), vrow[0:r, k, :], const[0:r, C_ID, 0:r])
            i.then_inc(sem("vecT"), 1)
            pe.wait_ge(sem("ctx_in"), 16)
            for c in range(KC):
                if c % 2 == 0:
                    pe.wait_ge(sem("cev"), cnt(c // 2 - 1))
                for n in range(NTC):
                    i = tr(bank(4 + c // 2 % 2, P, (c % 2) * CTX + n * P), cin[:, n, c * P:(c + 1) * P], ident)
                if c % 2:
                    i.then_inc(sem("cT"), 1)
            pe.wait_ge(sem("x_in"), 16)
            for c in range(KC):
                pe.wait_ge(sem("xev"), cnt(c - 3))
                for n in range(NL):
                    i = tr(bank(c % 4, P, n * P), xin[:, n, c * P:(c + 1) * P], ident)
                i.then_inc(sem("xT"), 1)
            pe.wait_ge(sem("vec"), 1)
            pe.wait_ge(sem("cvec"), 2)
            pe.wait_ge(sem("xev"), KC)
            for j in range(8):
                if j % 2 == 0:
                    pe.wait_ge(sem(f"mod_a{j // 2}"), 32)
                if j == 2:
                    post_stat(0, CTX, 5)
                if j == 4:
                    post_stat(1, SEQ, 3)
                if j >= 2:
                    pe.wait_ge(sem("mrow"), j - 1)
                for k in range(KC):
                    i = mm(bank(j % 2, UW)[0:2], cvec[:, k, :], mraw_a[j][:, k, :], start=k == 0, stop=k == KC - 1)
                i.then_inc(sem("mod_a"), 1)
            pe.wait_ge(sem("mrow"), 8)
            for m in range(16):
                i = tr(bank(7, 2, 2 * m), mod_row[0:2, m * P:(m + 1) * P], const[0:2, C_ID, 0:2])
            i.then_inc(sem("mod_a"), 1)

            def item_stat(e):
                g = item_group(e)
                pe.wait_ge(sem("nsq"), e + 1)
                if e == 4:
                    pe.wait_ge(sem("abt"), 1)
                if e == 8:
                    pe.wait_ge(sem("gcv"), 3)
                for j in range(items[e][1] // P):
                    i = mm(bank(ITEM_BANK[g], 1 if e < 8 else 2, item_col(e, j)), sqt[e % 2][:, j * P:(j + 1) * P],
                           ones[:, 0:1] if e < 8 else const[:, C_BLK, 0:P:HD], start=True, stop=True)
                i.then_inc(sem("nst"), 1)

            lat = 2
            pe.wait_ge(sem("w_lo"), 1)
            mm3_first([bank(4, CTX, r * CTX) for r in range(2)], 0, hc_hi, hc_lo, 0, (None, "ctx_tile"), True)
            mm3_first([bank(r) for r in range(2)], 0, h_hi, h_lo, KC, ("tile", "tile"))
            for u in range(1, U_WOUT):
                s = u % 2
                tiles = 1 if u == 5 else 2
                cols = lambda w, k, r: w[s][:, k, r * P:(r + 1) * P]
                pe.wait_ge(sem("w_lo"), u + 1)
                if u < 6:
                    if u >= 2:
                        pe.wait_ge(sem("ev"), cnt(EV[u - 2, "ctx"]))
                    for r in range(tiles):
                        i = mm3(bank(4 + u % 2, CTX, r * CTX), lambda w, k: cols(w, k, r), KC, hc_hi, hc_lo, s)
                    i.then_inc(sem("ctx_tile" if u < 5 else "tile"), 1)
                for r in range(tiles):
                    if lat >= 4:
                        pe.wait_ge(sem("ev"), cnt(EV_LAT[lat - 4]))
                    i = mm3(bank(lat % 4), lambda w, k: cols(w, k, r), KC, h_hi, h_lo, s)
                    i.then_inc(sem("tile"), 1)
                    lat += 1

                for m in mod_group(u - 1):
                    pe.wait_ge(sem("mod_acc"), acc_b(m))
                    mod_column(m, macc_b[m % 4][:, :])
                for e in ITEMS_IN.get(u - 1, ()):
                    item_stat(e)
                if u == 7:
                    pe.wait_ge(sem("ev"), EV[5, "lat"])
                    for n in range(NT):
                        i = tr(bank(4, 16, 16 * n), ab[0:16, n * P:(n + 1) * P], const[0:16, C_ID, 0:16])
                    i.then_inc(sem("abT"), 1)
                if u == 10:
                    pe.wait_ge(sem("g"), 1)
                    gm = smallv[:, 0].rearrange("p n c -> p (n c)")
                    for j, w in enumerate((C(C_TRI), C(C_TRI + 1), ones)):
                        i = mm(bank(5, 8 * NT, 64 * j), w, gm, start=True, stop=True)
                    i.then_inc(sem("gsum"), 1)

            def item_rows(e):
                n = items[e][1]
                b = 2 * (e % 2)
                pe.wait_ge(sem("nrc"), item_group(e) + 1)
                pe.wait_ge(sem("nrm"), cnt(e - 1))
                for j in range(n // P):
                    c0 = item_col(e, j)
                    i = mm(bank(b, P, j * P), nsm[:, c0:c0 + 1].to_broadcast([P, P]), ident, start=True, stop=True)
                i.then_inc(sem("nrow"), 1)

            def att_rows(l):
                t, c0, _ = att_part(l)
                pe.wait_ge(sem("nrc"), 3)
                pe.wait_ge(sem("nrm"), 8 + l)
                for j in range(t.shape[1] // P):
                    for half in range(2):
                        c = c0 + 2 * j + half
                        i = mm(bank(6, P, j * P)[HD * half:HD * (half + 1)], nsm[:, c:c + 1].to_broadcast([P, HD]),
                               ident, start=True, stop=True)
                i.then_inc(sem("nrow"), 1)

            pe.wait_ge(sem("ev"), len(EVENTS))
            for e in ITEM_GROUPS[2]:
                if e < 12:
                    item_rows(e - 8)
                item_stat(e)
            for e in range(4, 8):
                item_rows(e)
            for m in mod_group(U_WOUT - 1):
                pe.wait_ge(sem("mod_acc"), acc_b(m))
                mod_column(m, macc_b[m % 4][:, :])

            def mod_columns(q):
                for j in mod_at(q, 4):
                    pe.wait_ge(sem("mod_acc"), acc_c(j))
                    for part in range(2):
                        mod_column(48 + 2 * j + part, mraw_c[j % MSLOTS][:, 0, part * P:(part + 1) * P])

            def gate_rows(s):
                for d in range(2):
                    k, n = 2 * s + d, CHUNK_ORDER[d][s]
                    if s:
                        pe.wait_ge(sem("vn"), k - 1)
                    for h in range(HEADS):
                        i = mm(bank(3 * d, P, h * P), smallv[:, 0, n, 4 * d + h:4 * d + h + 1].to_broadcast([P, P]),
                               C(C_TRI + d), start=True, stop=True)
                    i.then_inc(sem("gc"), 1)

            pe.wait_ge(sem("dn_ready"), 1)
            gate_rows(0)
            for s in range(NT):
                for d in range(2):
                    k = 2 * s + d
                    n = CHUNK_ORDER[d][s]
                    b0 = 3 * d
                    tok = slice(n * P, (n + 1) * P)
                    if s:
                        pe.wait_ge(sem("S"), k - 1)
                    for h in range(HEADS):
                        i = mm(bank(b0 + 1, P, h * P), kT[:, h, tok], kT[:, h, tok], start=True, stop=True)
                    i.then_inc(sem("G"), 1)
                for d in range(2):
                    n, b0 = CHUNK_ORDER[d][s], 3 * d
                    tok = slice(n * P, (n + 1) * P)
                    if n >= NTC:
                        ql = slice((n - NTC) * P, (n - NTC + 1) * P)
                        for h in range(HEADS):
                            i = mm(bank(b0 + 2, P, h * P), kT[:, h, tok], qT[:, h, ql], start=True, stop=True)
                        i.then_inc(sem("QK"), 1)
                for d in range(2):
                    k, n, b0 = 2 * s + d, CHUNK_ORDER[d][s], 3 * d
                    tok = slice(n * P, (n + 1) * P)
                    pe.wait_ge(sem("GA"), k + 1)
                    for h in range(HEADS):
                        i = tr(bank(b0 + 1, P, h * P), kT[:, h, tok], ident)
                    i.then_inc(sem("Ktr"), 1)
                    if n >= NTC:
                        pe.wait_ge(sem("QB"), cnt(k - 3))
                    for h in range(HEADS):
                        i = tr(bank(b0 + 2, P, h * P), vT[:, h, tok], ident)
                    i.then_inc(sem("Vtr"), 1)
                for l in range(LEVELS):
                    for d in range(2):
                        T, q = DT[d], (s * LEVELS + l) * 2 + d
                        if l == 0:
                            continue
                        pe.wait_ge(sem("Bl"), q + 1)
                        pe.wait_ge(sem("T"), q - 1)
                        for h in range(HEADS):
                            i = mm(bank(3 * d, P, h * P), T["bl"][:, h, :], T["tu"][:, h, :], start=True, stop=True)
                        i.then_inc(sem("Z"), 1)
                    mod_columns(s * LEVELS + l)
                    for d in range(2):
                        T, q, b0 = DT[d], (s * LEVELS + l) * 2 + d, 3 * d
                        if l == 0:
                            pe.wait_ge(sem("Bl"), q + 1)
                            pe.wait_ge(sem("TU0"), 2 * s + d + 1)
                            if CHUNK_ORDER[d][s] >= NTC:
                                pe.wait_ge(sem("egr"), 2 * s + d - 3)
                            pe.wait_ge(sem("bv"), 2 * s + d + 1)
                            for h in range(HEADS):
                                i = mm(bank(b0 + 1, P, h * P), T["bl"][:, h, :], T["tu"][:, h, :], start=True, stop=True)
                            i.then_inc(sem("dT"), 1)
                            for h in range(HEADS):
                                i = mm(bank(b0 + 2, P, h * P), T["tu"][:, 4 + h, :], T["bl"][:, h, :], start=True, stop=True)
                            i.then_inc(sem("dU"), 1)
                            continue
                        pe.wait_ge(sem("Zs"), z_count(s, l, d))
                        pe.wait_ge(sem("U"), q - 1)
                        for h in range(HEADS):
                            i = mm(bank(b0 + 1, P, h * P), T["tu"][:, 4 + h, :], T["zs"][:, h, :], start=True, stop=True)
                        i.then_inc(sem("dT"), 1)
                        for h in range(HEADS):
                            i = mm(bank(b0 + 2, P, h * P), T["zs"][:, h, :], T["tu"][:, 4 + h, :], start=True, stop=True)
                        i.then_inc(sem("dU"), 1)
                    if s == 0 and l < 6:
                        att_rows(l)
                for d in range(2):
                    T, k = DT[d], 2 * s + d
                    pe.wait_ge(sem("U"), (s + 1) * LEVELS * 2 - 1 + d)
                    pe.wait_ge(sem("L"), k + 1)
                    for h in range(HEADS):
                        i = mm(bank(3 * d, P, h * P), T["ta"][:, h, :], f32(T["tu"][:, h, :]), start=True, stop=True)
                    i.then_inc(sem("LU"), 1)
                for d in range(2):
                    T, k = DT[d], 2 * s + d
                    pe.wait_ge(sem("R2"), k + 1)
                    for h in range(HEADS):
                        i = mm(bank(3 * d + 1, P, h * P), T["tu"][:, 4 + h, :], T["bl"][:, h, :], start=True, stop=True)
                    i.then_inc(sem("dN"), 1)
                for d in range(2):
                    T, k = DT[d], 2 * s + d
                    pe.wait_ge(sem("Uf"), k + 1)
                    for h in range(HEADS):
                        i = mm(bank(3 * d + 2, P, h * P), T["kbvn"][:, h, :], T["uf"][:, h, :], start=True, stop=True)
                    i.then_inc(sem("WT"), 1)
                for d in range(2):
                    T, k = DT[d], 2 * s + d
                    pe.wait_ge(sem("nW"), k + 1)
                    for h in range(HEADS):
                        i = mm(bank(3 * d, P, h * P), T["uf"][:, h, :], T["bv"][:, h, :], start=True, stop=s == 0)
                        if s:
                            i = mm(bank(3 * d, P, h * P), T["nw"][:, h, :], S[d][:, h, :], start=False, stop=True)
                    i.then_inc(sem("vnp"), 1)
                if s < NT - 1:
                    gate_rows(s + 1)
                for d in range(2):
                    T, k, n = DT[d], 2 * s + d, CHUNK_ORDER[d][s]
                    pe.wait_ge(sem("vn"), k + 1)
                    if n >= NTC:
                        pe.wait_ge(sem("intra"), cnt(k - 3))
                        pe.wait_ge(sem("qg"), cnt(k - 3))
                        for h in range(HEADS):
                            mm(bank(3 * d + 1, P, h * P), S[d][:, h, :], T["qg"][:, h, :], start=True, stop=False)
                            i = mm(bank(3 * d + 1, P, h * P), T["kbvn"][:, h, :], T["tb"][:, h, :], start=False, stop=True)
                        i.then_inc(sem("o"), 1)
                    for h in range(HEADS):
                        i = mm(bank(3 * d + 2, P, h * P), T["kd"][:, h, :], T["kbvn"][:, h, :], start=True, stop=True)
                    i.then_inc(sem("Sp"), 1)
            for q in range(LEVELS * NT, LEVELS * NT + 5):
                mod_columns(q)
            pe.wait_ge(sem("S"), 2 * NT)
            for n in range(NT):
                i = tr(bank(4 + n // 4, P, P * (n % 4)), av[:, n * P:(n + 1) * P], ident)
            i.then_inc(sem("Vatr"), 1)
            for h in range(HEADS):
                pe.wait_ge(sem("osq"), h + 1)
                for j in range(NL):
                    i = mm(bank(6, 1, NL * (9 + h) + j), tmp[h][:, j * P:(j + 1) * P], ones[:, 0:1], start=True, stop=True)
            i.then_inc(sem("ost"), 1)
            pe.wait_ge(sem("orc"), 1)
            for h in range(HEADS):
                for j in range(NL):
                    i = mm(bank(h, P, j * P), odev[:, NL * h + j:NL * h + j + 1].to_broadcast([P, P]), ident,
                           start=True, stop=True)
                i.then_inc(sem("orow"), 1)

            NQ = SEQ // P

            def turn(i):
                pe.wait_ge(sem("Pn"), i + 1)
                pe.wait_ge(sem("PT"), i)
                for n in range(NT):
                    j = tr(bank(4 + n // 4, P, P * (n % 4)), prob[i % 3][:, n * P:(n + 1) * P], ident)
                j.then_inc(sem("Ptr"), 1)

            def values(hh, part):
                if part == 0:
                    pe.wait_ge(sem("PT"), NQ * (hh + 1))
                    if hh >= 1:
                        pe.wait_ge(sem("mix0"), HEADS + hh)
                b = bank(6)
                for n in (2 * part, 2 * part + 1):
                    mm(b, Vh[:, n, :], PTh[hh % 2][:, n, :], start=n == 0, stop=False)
                    mm(b, Vh[:, n, :], PTl[hh % 2][:, n, :], start=False, stop=False)
                    j = mm(b, Vl[:, n, :], PTh[hh % 2][:, n, :], start=False, stop=n == NT - 1)
                if part == 2:
                    j.then_inc(sem("pv"), 1)

            pe.wait_ge(sem("Va"), 1)
            pe.wait_ge(sem("on"), HEADS)
            for i in range(A_HEADS * NQ + NQ + 1):
                if i < A_HEADS * NQ:
                    hh, qt = divmod(i, NQ)
                    t, half = hh % 4, hh // 4
                    r = slice(HD * half, HD * (half + 1))
                    pe.wait_ge(sem("expd"), cnt(i - 1))
                    b = 2 * (i % 2)
                    mm(bank(b), aq[r, t, qt * P:(qt + 1) * P], ak[r, 0:512], start=True, stop=True)
                    mm(bank(b + 1, CTX), aq[r, t, qt * P:(qt + 1) * P], ak[r, 512:768], start=True, stop=True).then_inc(sem("sc"), 1)
                if 2 <= i < A_HEADS * NQ + 2:
                    turn(i - 2)
                if i >= 6 and (i - 6) % NQ < 3:
                    values((i - 6) // NQ, (i - 6) % NQ)

            tcol = lambda r: (lambda w, k: w[slot[0]][:, k, r * P:(r + 1) * P])
            slot = [0]

            def out_units(u0, yq):
                def body(i):
                    for s in range(2):
                        slot[0] = s
                        pe.wait_ge(sem("w_lo"), 2 * i + (u0 + s + 1))
                        for r in range(2):
                            t = 4 * i + (2 * s + r)
                            pe.wait_ge(sem("yev"), cnt(t + (8 * yq - 3)))
                            mm3(bank(2 * s + r), tcol(r), KC, mix_hi, mix_lo, s).then_inc(sem("tile"), 1)
                rep(pe, 2, body, peel=yq == 0)

            def ffn(f, U_UP, U_DOWN, yq):
                def up_pair(i, par, j0, first=False):
                    for part in range(2):
                        slot[0] = part
                        if first and part == 0:
                            pe.wait_ge(sem("w_lo"), U_UP + 1)
                            mm3_first([bank(r) for r in range(2)], 0, h_hi, h_lo, KC * H_FFN[f], ("tile", "tile"))
                            continue
                        pe.wait_ge(sem("w_lo"), 2 * i + (U_UP + 2 * j0 + part + 1))
                        for r in range(2):
                            pe.wait_ge(sem(("g" if part else "c3") + "_free"), cnt(2 * i + (FC * f + 2 * j0 + r - 3)))
                            mm3(bank(4 * par + 2 * part + r), tcol(r), KC, h_hi, h_lo, part).then_inc(sem("tile"), 1)

                def up4(i):
                    for par in range(2):
                        up_pair(2 * i, par, par, first=isinstance(i, int) and i == par)
                rep(pe, FC // 4, up4, peel=1)
                up_pair(0, 0, FC // 2 - 1)
                pe.wait_ge(sem("mid"), FC * (f + 1))

                def down2(i):
                    for q in range(6):
                        slot[0] = q % 2
                        k0, nk = DCH[q % 3]
                        p = q // 3
                        pe.wait_ge(sem("w_lo"), 6 * i + (U_DOWN + q + 1))
                        for r in range(2):
                            if q % 3 == 0:
                                t = 4 * i + (2 * p + r)
                                pe.wait_ge(sem("yev"), cnt(t + (8 * yq - 3)))
                            mm3(bank(2 * p + r), tcol(r), nk, mid_hi, mid_lo, q % 2, k0,
                                    q % 3 == 0, q % 3 == 2).then_inc(sem("tile"), 1)
                rep(pe, 2, down2)

            def boundary(idx):
                post_stat(idx)
                if idx < 8:
                    pe.wait_ge(sem("x_new"), KC * ((idx - 2) // 2 + 1))
                    pre_stat(idx + 1, SEQ, 5)

            pe.wait_ge(sem("mix0"), HEADS + A_HEADS)
            out_units(U_WOUT, 0)
            boundary(2)
            ffn(0, U_UP0, U_DOWN0, 1)
            boundary(4)

            def cx(i, par, j0):
                for part in range(2):
                    slot[0] = part
                    if isinstance(i, int) and i == j0 == part == 0:
                        pe.wait_ge(sem("w_lo"), U_SCIN + 1)
                        mm3_first([bank(r) for r in range(2)], 0, h_hi, h_lo, KC * H_SC, ("tile", "tile"))
                        continue
                    pe.wait_ge(sem("w_lo"), 2 * i + (U_SCIN + 2 * j0 + part + 1))
                    for r in range(2):
                        pe.wait_ge(sem("scu" if part else "scc"), cnt(2 * i + (2 * j0 + r - 3)))
                        mm3(bank(4 * par + 2 * part + r), tcol(r), KC, h_hi, h_lo, part).then_inc(sem("tile"), 1)

            def cx2(i):
                for par in range(2):
                    cx(2 * i, par, par)
            rep(pe, 2, cx2, peel=1)
            pe.wait_ge(sem("scu"), KC)

            def gate_b(i):
                for s in range(2):
                    slot[0] = s
                    pe.wait_ge(sem("w_lo"), 2 * i + (U_SCIN + 8 + s + 1))
                    for r in range(2):
                        pe.wait_ge(sem("scb"), cnt(4 * i + (2 * s + r - 3)))
                        mm3(bank(2 * s + r), tcol(r), KC, h_hi, h_lo, s).then_inc(sem("tile"), 1)
            rep(pe, 2, gate_b, peel=1)
            pe.wait_ge(sem("mix1"), KC)
            out_units(U_SCOUT, 2)
            boundary(6)
            ffn(1, U_UP1, U_DOWN1, 3)
            boundary(8)
            for half in range(2):
                for c in range(4 * half, 4 * half + 4):
                    pe.wait_ge(sem("x_new"), 3 * KC + (KC if half else c + 1))
                    for n in range(NL):
                        i = tr(bank(2 * n + half, P, (c % 4) * P), x[:, c, n * P:(n + 1) * P], ident)
                i.then_inc(sem("out_T"), 1)

        @block.scalar
        def _(act):
            def split_hi(u, s):
                act.wait_ge(sem(f"w_raw{s}"), rawcount(u, s))
                act.wait_ge(sem("tile"), cnt(2 * u - 2))
                nc.scalar.activation(whi[s][:, :], raw[s][:, :], ACT.Copy).then_inc(sem("w_hi"), 1)

            def squares(idx, src, n, waits):
                t4 = tmp
                for c in range(KC):
                    waits(c)
                    if c >= 3 and c % 2:
                        act.wait_ge(sem("sqcol"), sq_cols(idx) + c // 2)
                    if c >= 4 and c % 2 == 0:
                        act.wait_ge(sem("sqadd"), sq_adds(idx) + c // 2 - 1)
                    nc.scalar.activation(t4[2 if c == 0 else c % 2][:, 0:n], src(c), ACT.Square).then_inc(sem("sq"), 1)

            def first_squares(idx, src, n, waits):
                for c in range(KC):
                    waits(c)
                    if c >= 2:
                        act.wait_ge(sem("sqadd"), sq_adds(idx) + c - 1)
                    nc.scalar.activation((tmp if idx else ctmp)[c % 2][:, 0:n], src(c), ACT.Square).then_inc(sem("sq"), 1)

            def deviation(idx, n):
                act.wait_ge(sem("stat"), idx + 1)
                cols = slice(NL * idx, NL * idx + n // P)
                nc.scalar.activation(dev[:, cols], bank(6)[:, cols], ACT.Sqrt, scale=1.0 / D_MODEL,
                                     bias=eps[:, :]).then_inc(sem("sd"), 1)

            def h_high(hb, out_, n, shift):
                for c in range(KC):
                    act.wait_ge(sem("t"), KC * hb + c + 1)
                    nc.scalar.activation(out_[:, c, :], (ctmp if hb == 0 else tmp)[c % 2][:, 0:n], ACT.Identity, bias=shift(c)).then_inc(sem("h_hi"), 1)

            act.wait_ge(sem("vec"), 1)
            for w, row in enumerate((V_C, V_CCTX)):
                nc.scalar.activation(cvec[:, :, w], vec[:, 0, row:row + KC], ACT.Silu).then_inc(sem("cvec"), 1)
            first_squares(0, lambda c: xc[:, c, :], CTX, lambda c: act.wait_ge(sem("cev"), c // 2 + 1))
            first_squares(1, lambda c: x[:, c, :], SEQ, lambda c: act.wait_ge(sem("xev"), c + 1))
            deviation(0, CTX)
            deviation(1, SEQ)
            act.wait_ge(sem("mod_a"), 8)
            split_hi(0, 0)
            split_hi(1, 1)
            h_high(0, hc_hi, CTX, lambda c: modv[:, 0, c, 1:2])
            h_high(1, h_hi, SEQ, lambda c: modv[:, 0, c, 0:1])

            def products(slot):
                for k in range(KC):
                    i = nc.scalar.activation(slot[:, k, :], slot[:, k, :], ACT.Copy, scale=cvec[:, k, 0:1])
                i.then_inc(sem("mod_prod"), 1)

            def square(e):
                t, n = items[e]
                if e >= 2:
                    act.wait_ge(sem("nst"), e - 1)
                nc.scalar.activation(sqt[e % 2][:, 0:n], t, ACT.Square).then_inc(sem("nsq"), 1)

            def group_sd(g):
                act.wait_ge(sem("nst"), ITEM_GROUPS[g][-1] + 1)
                nc.scalar.activation(nsm[:, item_cols[g]], bank(ITEM_BANK[g])[:, item_cols[g]], ACT.Sqrt,
                                     scale=1.0 / HD if g == 2 else 1.0, bias=eps[:, :]).then_inc(sem("nsd"), 1)

            dnw = lambda k, j: vec[:, 2, 12 * k + j:12 * k + j + 1]
            for u in range(U_WOUT):
                act.wait_ge(sem("tile"), 2 * u + 2)
                if u + 2 < U_WOUT:
                    split_hi(u + 2, u % 2)
                jobs = list(conv_jobs(u))
                for stream, r, dst, ps, j in jobs:
                    if stream == "ctx":
                        act.wait_ge(sem("ctx_tile"), u + 1)
                    else:
                        act.wait_ge(sem("tile"), 2 * u + r + 1)
                    nc.scalar.activation(dst, ps, ACT.Copy, scale=dnw(1, j)).then_inc(sem("cv1"), 1)
                for stream, r, dst, _, _ in jobs:
                    act.wait_ge(sem("ev"), EVENTS.index((u, stream, r)) + 1)
                    nc.scalar.activation(dst, dst, ACT.Silu).then_inc(sem("cvs"), 1)
                if u in (8, 9):
                    for r in range(2):
                        hd = 2 * (u - 8) + r
                        act.wait_ge(sem("ev"), EVENTS.index((u, "lat", r)) + 1)
                        nc.scalar.activation(gT[:, hd, :], gT[:, hd, :], ACT.Silu).then_inc(sem("gate"), 1)
                if u == 8:
                    z, e1 = smallv[:, 7], smallv[:, 6]
                    act.wait_ge(sem("abt"), 1)
                    nc.scalar.activation(smallv[:, 1], abt[:, :, 8:16], ACT.Sigmoid).then_inc(sem("beta"), 1)
                    act.wait_ge(sem("z"), 1)
                    nc.scalar.activation(e1, z, ACT.Abs).then_inc(sem("gate_a"), 1)
                    act.wait_ge(sem("gate_a"), 1)
                    nc.scalar.activation(e1, e1, ACT.Exp, scale=-1.0).then_inc(sem("gate_a"), 1)
                    act.wait_ge(sem("gate_in"), 32)
                    nc.scalar.activation(alog[:, 0:8], alog[:, 0:8], ACT.Exp).then_inc(sem("ea"), 1)
                    act.wait_ge(sem("gate_a"), 2)
                    nc.scalar.activation(e1, e1, ACT.Ln, bias=const[:, C_ONE, 0:1]).then_inc(sem("gate_a"), 1)
                if u == 10:
                    group_sd(0)
                for e in ITEMS_IN.get(u, ()):
                    if e < 4:
                        act.wait_ge(sem("cvs"), 8)
                    elif e < 8:
                        act.wait_ge(sem("cvs"), N_CONV)
                    else:
                        act.wait_ge(sem("ev"), EV[10, "lat"])
                    square(e)
            group_sd(1)
            for e in range(10, 13):
                act.wait_ge(sem("ev"), len(EVENTS))
                square(e)
            group_sd(2)
            act.wait_ge(sem("gcv"), 3)
            for j in range(3):
                nc.scalar.activation(smallv[:, 3 + j], smallv[:, 3 + j], ACT.Exp).then_inc(sem("ge"), 1)

            def start_chunk(s):
                for d in range(2):
                    k, T = 2 * s + d, DT[d]
                    act.wait_ge(sem("dA"), k + 1)
                    nc.scalar.activation(T["ta"][:, :, :], T["ta"][:, :, :], ACT.Exp).then_inc(sem("EA"), 1)
                for d in range(2):
                    T, k = DT[d], 2 * s + d
                    if s:
                        act.wait_ge(sem("Uf"), k - 1)
                    nc.scalar.activation(T["tu"][:, :, :], bh(ident, 8), ACT.Copy).then_inc(sem("TU0"), 1)

            start_chunk(0)
            for s in range(NT):
                for d in range(2):
                    k, n, T = 2 * s + d, CHUNK_ORDER[d][s], DT[d]
                    if n >= NTC:
                        act.wait_ge(sem("dB"), cnt(k - 3))
                        nc.scalar.activation(T["tb"][:, :, :], T["tb"][:, :, :], ACT.Exp).then_inc(sem("EB"), 1)
                        nc.scalar.activation(T["qg"][:, :, :].rearrange("p h t -> p (h t)"), bank(3 * d), ACT.Exp).then_inc(sem("egr"), 1)
                for l in range(LEVELS):
                    for d in range(2 if l else 0):
                        T = DT[d]
                        act.wait_ge(sem("Z"), z_count(s, l, d))
                        nc.scalar.activation(T["zs"][:, :, :].rearrange("p h t -> p (h t)"), bank(3 * d), ACT.Copy).then_inc(sem("Zs"), 1)
                    for j in mod_at(s * LEVELS + l, 0):
                        act.wait_ge(sem(f"mod_in{j % MSLOTS}"), landed(j % MSLOTS, False)(j // MSLOTS))
                        products(mraw_c[j % MSLOTS])
                for d in range(2):
                    T, k = DT[d], 2 * s + d
                    act.wait_ge(sem("WT"), k + 1)
                    nc.scalar.activation(T["nw"][:, :, :].rearrange("p h t -> p (h t)"), bank(3 * d + 2), ACT.Copy, scale=-1.0).then_inc(sem("nW"), 1)
                for d in range(2):
                    T, k = DT[d], 2 * s + d
                    act.wait_ge(sem("vnp"), k + 1)
                    nc.scalar.activation(T["kbvn"][:, :, :].rearrange("p h t -> p (h t)"), bank(3 * d), ACT.Copy).then_inc(sem("vn"), 1)
                if s < NT - 1:
                    start_chunk(s + 1)
            act.wait_ge(sem("oe"), 8)
            act.wait_ge(sem("mod_done"), MODS - 16)
            for h in range(HEADS):
                nc.scalar.activation(tmp[h][:, :], oT[:, h, :], ACT.Square).then_inc(sem("osq"), 1)
            act.wait_ge(sem("ost"), 1)
            nc.scalar.activation(odev[:, :], bank(6, HEADS * NL, 9 * NL), ACT.Sqrt, scale=1.0 / DK,
                                 bias=eps[:, :]).then_inc(sem("osd"), 1)
            act.wait_ge(sem("Vatr"), 1)
            nc.scalar.activation(Vh[:, :, :].rearrange("p n t -> p (n t)"), bank(4, ALL), ACT.Copy).then_inc(sem("Vah"), 1)
            for h in range(HEADS):
                act.wait_ge(sem("on"), h + 1)
                nc.scalar.activation(mix_hi[:, h, :], oT[:, h, :], ACT.Copy).then_inc(sem("on_hi"), 1)

            NQ = SEQ // P

            def turn_hi(i):
                hh, qt = divmod(i, NQ)
                act.wait_ge(sem("Ptr"), i + 1)
                if hh >= 2:
                    act.wait_ge(sem("pv"), cnt(hh - 1))
                nc.scalar.activation(PTh[hh % 2][:, :, qt * P:(qt + 1) * P], bank(4, ALL).rearrange("p (n t) -> p n t", t=P), ACT.Copy).then_inc(sem("PTh"), 1)

            def head_hi(hh):
                half, t = hh // 4, hh % 4
                r = slice(HD * half, HD * (half + 1))
                act.wait_ge(sem("pv"), hh + 1)
                nc.scalar.activation(mix_hi[r, 4 + t, :], bank(6)[r], ACT.Copy).then_inc(sem("ahh"), 1)

            for i in range(A_HEADS * NQ + NQ + 2):
                if 2 <= i < A_HEADS * NQ + 2:
                    turn_hi(i - 2)
                if i < A_HEADS * NQ:
                    act.wait_ge(sem("mx"), i + 1)
                    act.wait_ge(sem("Ptr"), cnt(i - 2))
                    nc.scalar.activation(prob[i % 3][:, :], bank(2 * (i % 2), ALL), ACT.Exp, scale=HD ** -0.5,
                                         bias=stat[:, 32 + i:33 + i], accum_out=stat[:, 64 + i:65 + i]).then_inc(sem("expd"), 1)
                if i >= 9 and (i - 9) % NQ == 0:
                    head_hi((i - 9) // NQ)
                if i == A_HEADS * NQ:
                    act.wait_ge(sem("mod_done"), 2 * MODS - 16)
                    split_hi(U_WOUT, 0)
                    split_hi(U_WOUT + 1, 1)

            def y_squares(u0, yq):
                def body(i):
                    for s in range(2):
                        act.wait_ge(sem("tile"), 4 * i + (2 * u0 + 2 * s + 2))
                        split_hi(2 * i + (u0 + s + 2), s)
                        for r in range(2):
                            t = 4 * i + (2 * s + r)
                            act.wait_ge(sem("sqadd"), t + (sq_adds(2 + 2 * yq) - 1))
                            act.wait_ge(sem("yev"), t + (8 * yq + 1))
                            nc.scalar.activation(tmp[r][:, :], ytile(t), ACT.Square).then_inc(sem("sq"), 1)
                rep(act, 2, body)

            def boundary(idx, hb, shift):
                deviation(idx, SEQ)
                if idx < 8:
                    act.wait_ge(sem("x_new"), cnt(KC * ((idx - 2) // 2) + 1))
                    squares(idx + 1, lambda c: x[:, c, :], SEQ,
                            lambda c: act.wait_ge(sem("x_new"), cnt(KC * ((idx - 2) // 2) + c + 1)))
                    deviation(idx + 1, SEQ)
                    h_high(hb, h_hi, SEQ, shift)

            def ffn(f, U_UP, U_DOWN, yq):
                cw = lambda k, j: vec[:, 3 + f, bass.ds(j + 22 * k, 1)]

                def up_pair(i, par, j0):
                    tl = lambda r: 2 * i + (FC * f + 2 * j0 + r)
                    u = 2 * i + (U_UP + 2 * j0)
                    act.wait_ge(sem("tile"), 4 * i + (2 * (U_UP + 2 * j0) + 2))
                    split_hi(u + 2, 0)
                    for r in range(2):
                        act.wait_ge(sem("mid"), cnt(tl(r) - 3))
                        nc.scalar.activation(tmp[2 * par + r][:, :], bank(4 * par + r), ACT.Copy, scale=cw(1, 2 * i + (2 * j0 + r))).then_inc(sem("c1"), 1)
                    for r in range(2):
                        act.wait_ge(sem("c3_free"), tl(r) + 1)
                        nc.scalar.activation(tmp[2 * par + r][:, :], tmp[2 * par + r][:, :], ACT.Silu).then_inc(sem("sg"), 1)
                    act.wait_ge(sem("tile"), 4 * i + (2 * (U_UP + 2 * j0) + 4))
                    split_hi(u + 3, 1)
                    for r in range(2):
                        act.wait_ge(sem("g_free"), tl(r) + 1)
                        nc.scalar.activation(mid_hi[:, bass.ds(2 * i + (2 * j0 + r), 1), :].rearrange("p c t -> p (c t)"), tmp[2 * par + r][:, :], ACT.Copy).then_inc(sem("ghi"), 1)

                def up4(i):
                    for par in range(2):
                        up_pair(2 * i, par, par)
                rep(act, FC // 4, up4, peel=f == 0)
                up_pair(0, 0, FC // 2 - 1)

                def down2(i, last=False):
                    for q in range(6):
                        act.wait_ge(sem("tile"), 12 * i + (2 * (U_DOWN + q) + 2))
                        if not (last and q >= 4):
                            split_hi(6 * i + (U_DOWN + q + 2), q % 2)
                        if q % 3 == 2:
                            for r in range(2):
                                t = 4 * i + (2 * (q // 3) + r)
                                act.wait_ge(sem("sqadd"), t + (sq_adds(2 + 2 * yq) - 1))
                                act.wait_ge(sem("yev"), t + (8 * yq + 1))
                                nc.scalar.activation(tmp[r][:, :], ytile(t), ACT.Square).then_inc(sem("sq"), 1)
                if f == 0:
                    rep(act, 2, down2)
                else:
                    down2(0)
                    down2(1, True)

            y_squares(U_WOUT, 0)
            boundary(2, 2, lambda c: modv[:, 0, 3 * KC + c, 0:1])
            ffn(0, U_UP0, U_DOWN0, 1)
            boundary(4, 3, lambda c: modv[:, 1, c, 0:1])

            scw = lambda k, j: vec[:, 0, bass.ds(j + (V_SCCONV + 8 * k), 1)]

            def cx(i, par, j0):
                tl = lambda r: 2 * i + (2 * j0 + r)
                for part in range(2):
                    act.wait_ge(sem("tile"), 4 * i + (2 * (U_SCIN + 2 * j0 + part) + 2))
                    split_hi(2 * i + (U_SCIN + 2 * j0 + part + 2), part)
                    for r in range(2):
                        if part == 0:
                            act.wait_ge(sem("scv"), cnt(tl(r) - 3))
                            nc.scalar.activation(tmp[2 * par + r][:, :], bank(4 * par + r), ACT.Copy).then_inc(sem("scc"), 1)
                        else:
                            act.wait_ge(sem("scu"), tl(r) + 1)
                            nc.scalar.activation(cv[:, bass.ds(tl(r), 1), :].rearrange("p c t -> p (c t)"), tmp[2 * par + r][:, :], ACT.Copy, scale=scw(1, tl(r))).then_inc(sem("scv1"), 1)

            def cx2(i):
                for par in range(2):
                    cx(2 * i, par, par)
            rep(act, 2, cx2, peel=1)

            def gate_b(i):
                for s in range(2):
                    act.wait_ge(sem("tile"), 4 * i + (2 * (U_SCIN + 8 + s) + 2))
                    split_hi(2 * i + (U_SCIN + 8 + s + 2), s)
                    for r in range(2):
                        t = 4 * i + (2 * s + r)
                        act.wait_ge(sem("scb"), t + 1)
                        nc.scalar.activation(mix_hi[:, bass.ds(t, 1), :].rearrange("p c t -> p (c t)"), tmp[2 * s + r][:, :], ACT.Copy).then_inc(sem("mhi"), 1)
            rep(act, 2, gate_b)
            y_squares(U_SCOUT, 2)
            boundary(6, 4, lambda c: modv[:, 1, 3 * KC + c, 0:1])
            ffn(1, U_UP1, U_DOWN1, 3)
            boundary(8, 0, None)
            for n in range(NL):
                act.wait_ge(sem("out_T"), 1)
                nc.scalar.activation(xin[:, n, 0:512], bank(2 * n), ACT.Copy).then_inc(sem("out_ev_a"), 1)


        @block.vector
        def _(dve):
            V = nc.vector

            def split_lo(u, s):
                dve.wait_ge(sem("w_hi"), u + 1)
                V.tensor_tensor(wlo[s][:, :], raw[s][:, :], f32(whi[s][:, :]), ALU.subtract).then_inc(sem("w_lo"), 1)

            def rstd(idx, n):
                dve.wait_ge(sem("sd"), idx + 1)
                cols = slice(NL * idx, NL * idx + n // P)
                V.reciprocal(dev[:, cols], dev[:, cols]).then_inc(sem("rstd"), 1)

            def apply_pre(hb, X, t4, row, n, pre, shift, hi, lo):
                def low(c):
                    dve.wait_ge(sem("h_hi"), KC * hb + c + 1)
                    V.scalar_tensor_tensor(out=lo[:, c, :], in0=t4[c % 2][:, 0:n], scalar=shift(c),
                                               in1=f32(hi[:, c, :]), op0=ALU.add, op1=ALU.subtract).then_inc(sem("h"), 1)
                for c in range(KC):
                    if c >= 2:
                        low(c - 2)
                        dve.wait_ge(sem("h"), cnt(KC * hb + c - 1))
                    V.scalar_tensor_tensor(out=t4[c % 2][:, 0:n], in0=X(c), scalar=pre_w[:, pre, c:c + 1],
                                               in1=row, op0=ALU.mult, op1=ALU.mult).then_inc(sem("t"), 1)
                low(KC - 2)
                low(KC - 1)

            V.memset(eps[:, :], EPS)
            dve.wait_ge(sem("vecT"), 1)
            for k, r in enumerate(V_ROWS):
                i = V.tensor_copy(vec[:, k, 0:r], bank(7 if k < 4 else 6, r, P * (k % 4)))
            i.then_inc(sem("vec"), 1)
            for p in range(KC // 2):
                dve.wait_ge(sem("cT"), p + 1)
                V.tensor_copy(xc[:, 2 * p:2 * p + 2, :].rearrange("p c t -> p (c t)"), bank(4 + p % 2)).then_inc(sem("cev"), 1)
            for c in range(KC):
                dve.wait_ge(sem("xT"), c + 1)
                V.tensor_copy(x[:, c, :], bank(c % 4)).then_inc(sem("xev"), 1)
            for j in range(8):
                if j == 2:
                    rstd(0, CTX)
                if j == 4:
                    rstd(1, SEQ)
                dve.wait_ge(sem("mod_a"), j + 1)
                V.tensor_copy(mod_row[0:2, j * UW:(j + 1) * UW], bank(j % 2, UW)[0:2]).then_inc(sem("mrow"), 1)
            dve.wait_ge(sem("mod_a"), 9)
            dve.wait_ge(sem("vec"), 1)
            V.tensor_tensor(modv[:, 0, 0:16, :], bank(7, 32).rearrange("p (m w) -> p m w", w=2),
                            bc(vec[:, 1, 0:16], 2), ALU.add).then_inc(sem("modv"), 1)
            dve.wait_ge(sem("modv"), 1)

            def pre_weights(k, l, m, w, row):
                return V.scalar_tensor_tensor(out=pre_w[:, k, :], in0=modv[:, l, m:m + KC, w], scalar=1.0,
                                              in1=vec[:, 0, row:row + KC], op0=ALU.add, op1=ALU.mult)
            pre_weights(0, 0, KC, 0, V_MIXPRE)
            pre_weights(4, 0, KC, 1, V_MIXPRE).then_inc(sem("norm_w"), 1)
            dve.wait_ge(sem("norm_w"), 1)
            split_lo(0, 0)
            split_lo(1, 1)
            dve.wait_ge(sem("rrow"), 2)
            apply_pre(0, lambda c: xc[:, c, :], ctmp, bank(5, CTX), CTX, 4, lambda c: modv[:, 0, c, 1:2], hc_hi, hc_lo)
            apply_pre(1, lambda c: x[:, c, :], tmp, bank(3), SEQ, 0, lambda c: modv[:, 0, c, 0:1], h_hi, h_lo)

            def recip(g):
                dve.wait_ge(sem("nsd"), g + 1)
                V.reciprocal(nsm[:, item_cols[g]], nsm[:, item_cols[g]]).then_inc(sem("nrc"), 1)

            dnw = lambda k, j: vec[:, 2, 12 * k + j:12 * k + j + 1]
            n1 = n2 = 0
            for u in range(U_WOUT):
                if u + 2 < U_WOUT:
                    split_lo(u + 2, u % 2)
                jobs = list(conv_jobs(u))
                for stream in ("ctx", "lat"):
                    mine = [j for j in jobs if j[0] == stream]
                    for _, r, dst, ps, j in mine:
                        dve.wait_ge(sem("cv1"), cnt(n1 + 2 - r if stream == "ctx" else n1 + 1))
                        n = dst.shape[1]
                        V.scalar_tensor_tensor(out=dst[:, 1:n], in0=ps[:, 0:n - 1], scalar=dnw(0, j), in1=dst[:, 1:n],
                                                   op0=ALU.mult, op1=ALU.add).then_inc(sem("cv2"), 1)
                        n1 += 1
                    for _, r, dst, ps, j in mine:
                        dve.wait_ge(sem("cv2"), n2 + 1)
                        n = dst.shape[1]
                        V.scalar_tensor_tensor(out=dst[:, 0:n - 1], in0=ps[:, 1:n], scalar=dnw(2, j),
                                                   in1=dst[:, 0:n - 1], op0=ALU.mult, op1=ALU.add).then_inc(sem("ev"), 1)
                        n2 += 1
                if not jobs:
                    for e in EVENTS:
                        if e[0] != u:
                            continue
                        _, stream, r = e
                        cols = slice(0, CTX) if stream == "ctx" else slice(CTX, ALL)
                        ps = hyb_bank(*e)
                        if stream == "ctx":
                            dve.wait_ge(sem("ctx_tile" if u < 5 else "tile"), 5 if u < 5 else 11)
                        else:
                            dve.wait_ge(sem("tile"), 12 if u == 5 else 2 * u + r + 1)
                        if u == 4:
                            dst = (ak, av)[r][:, cols]
                        elif u == 5:
                            dst, ps = ab[0:16, cols], ps[0:16]
                        elif u < 10:
                            dst = gT[:, 2 * (u - 8) + r, :]
                        else:
                            dst = aq[:, 2 * (u - 10) + r, :]
                        V.tensor_copy(dst, ps).then_inc(sem("ev"), 1)
                for m in mod_group(u):
                    dve.wait_ge(sem(f"mod_in{m % 4}"), landed(m % 4, True)((m - 16) // 4))
                    V.tensor_tensor(mraw_b[m % 4][:, :, :], mraw_b[m % 4][:, :, :], bc(cvec[:, :, 0], P),
                                    ALU.mult).then_inc(sem("mod_prod"), 1)
                if u == 8:
                    dve.wait_ge(sem("abT"), 1)
                    V.tensor_copy(abt[:, :, :].rearrange("p n c -> p (n c)"), bank(4, 16 * NT)).then_inc(sem("abt"), 1)
                    dve.wait_ge(sem("abt"), 1)
                    dve.wait_ge(sem("gate_in"), 32)
                    V.tensor_tensor(smallv[:, 7], abt[:, :, 0:8], bh(alog[:, 8:16], NT), ALU.add).then_inc(sem("z"), 1)
                    dve.wait_ge(sem("z"), 1)
                    V.tensor_scalar(smallv[:, 5], smallv[:, 7], 0.0, None, ALU.max).then_inc(sem("gate_v"), 1)
                if u == 11:
                    recip(0)
                if u == 9:
                    dve.wait_ge(sem("gate_v"), 1)
                    dve.wait_ge(sem("gate_a"), 3)
                    V.tensor_tensor(smallv[:, 5], smallv[:, 5], smallv[:, 6], ALU.add).then_inc(sem("gate_v"), 1)
                    dve.wait_ge(sem("gate_v"), 2)
                    dve.wait_ge(sem("ea"), 1)
                    V.scalar_tensor_tensor(out=smallv[:, 0], in0=smallv[:, 5], scalar=-1.0, in1=bh(alog[:, 0:8], NT),
                                           op0=ALU.mult, op1=ALU.mult).then_inc(sem("g"), 1)
            dve.wait_ge(sem("gsum"), 1)
            sums = bank(5, 192).rearrange("p (j n c) -> p j n c", j=3, c=8)[:, :, 0:NT]
            for k in (2, 3):
                for d in range(2):
                    i = V.tensor_copy(smallv[:, k, :, 4 * d:4 * d + 4], sums[:, d, :, 4 * d:4 * d + 4])
            i.then_inc(sem("gcv"), 1)
            dve.wait_ge(sem("gcv"), 1)
            V.tensor_tensor(smallv[:, 4], sums[:, 2], smallv[:, 2], ALU.subtract).then_inc(sem("gcv"), 1)
            V.tensor_copy(smallv[:, 5], sums[:, 2]).then_inc(sem("gcv"), 1)
            def normed(e):
                t, n = items[e]
                dve.wait_ge(sem("nrow"), e + 1)
                V.scalar_tensor_tensor(out=t, in0=t, scalar=1.0 if e < 4 else DK ** -0.5, in1=bank(2 * (e % 2), n),
                                       op0=ALU.mult, op1=ALU.mult).then_inc(sem("nrm"), 1)

            def att_normed(l):
                t, _, w = att_part(l)
                dve.wait_ge(sem("nrow"), 9 + l)
                V.scalar_tensor_tensor(out=t, in0=t, scalar=w, in1=bank(6, t.shape[1]), op0=ALU.mult,
                                       op1=ALU.mult).then_inc(sem("nrm"), 1)

            recip(1)
            for e in range(8):
                normed(e)
            recip(2)
            dve.wait_ge(sem("ge"), 3)
            dve.wait_ge(sem("beta"), 1)
            V.tensor_tensor(smallv[:, 6], smallv[:, 1], smallv[:, 3], ALU.mult).then_inc(sem("dn_ready"), 1)
            dve.wait_ge(sem("dn_ready"), 1)

            per = lambda k, n, d: bc(smallv[:, k, n, 4 * d:4 * d + 4], P)

            def rope(l):
                if l < 5:
                    t, b = rope_tile(l), tmp[l % 4][:, :]
                    dve.wait_ge(sem("nrm"), 9 + l)
                    V.stream_shuffle(b, t, [j ^ 1 for j in range(32)]).then_inc(sem("shuf"), 1)
                    dve.wait_ge(sem("shuf"), 2 * l + 1)
                    V.tensor_tensor(b, b, sinT[:, :], ALU.mult).then_inc(sem("shuf"), 1)
                if 1 <= l <= 5:
                    dve.wait_ge(sem("shuf"), 2 * l)
                    dve.wait_ge(sem("rcos"), l)
                    V.tensor_tensor(rope_tile(l - 1), rope_tile(l - 1), tmp[(l - 1) % 4][:, :], ALU.add).then_inc(sem("rope"), 1)

            dve.wait_ge(sem("rope_in"), 32)
            dve.wait_ge(sem("mod_acc"), acc_b(MODS - 1))
            pbank = lambda b: bank(b).rearrange("p (h t) -> p h t", t=P)
            def decays(s):
                for d in range(2):
                    k, n, T = 2 * s + d, CHUNK_ORDER[d][s], DT[d]
                    dve.wait_ge(sem("gc"), k + 1)
                    V.tensor_tensor(T["ta"][:, :, :], per(2, n, d), pbank(3 * d), ALU.subtract).then_inc(sem("dA1"), 1)
                    dve.wait_ge(sem("dA1"), k + 1)
                    V.tensor_scalar(T["ta"][:, :, :], T["ta"][:, :, :], 0.0, None, ALU.min).then_inc(sem("dA"), 1)

            decays(0)
            for s in range(NT):
                for d in range(2):
                    k, n, T, b0 = 2 * s + d, CHUNK_ORDER[d][s], DT[d], 3 * d
                    if n >= NTC:
                        V.tensor_tensor(T["tb"][:, :, :], pbank(b0), per(2, n, d), ALU.subtract).then_inc(sem("dB1"), 1)
                    dve.wait_ge(sem("G"), k + 1)
                    dve.wait_ge(sem("EA"), k + 1)
                    V.tensor_tensor(T["ta"][:, :, :], T["ta"][:, :, :], pbank(b0 + 1), ALU.mult).then_inc(sem("GA"), 1)
                    if n >= NTC:
                        dve.wait_ge(sem("dB1"), k - 3)
                        V.tensor_scalar(T["tb"][:, :, :], T["tb"][:, :, :], 0.0, None, ALU.min).then_inc(sem("dB"), 1)
                for d in range(2):
                    k, n, T, b0 = 2 * s + d, CHUNK_ORDER[d][s], DT[d], 3 * d
                    if n >= NTC:
                        dve.wait_ge(sem("QK"), cnt(k - 3))
                        dve.wait_ge(sem("EB"), cnt(k - 3))
                        V.tensor_tensor(T["tb"][:, :, :], T["tb"][:, :, :], pbank(b0 + 2), ALU.mult).then_inc(sem("QB"), 1)
                for d in range(2):
                    k, n, T, b0 = 2 * s + d, CHUNK_ORDER[d][s], DT[d], 3 * d
                    dve.wait_ge(sem("Ktr"), k + 1)
                    V.tensor_tensor(T["kbvn"][:, :, :], pbank(b0 + 1), per(6, n, d), ALU.mult)
                    V.tensor_tensor(T["kd"][:, :, :], pbank(b0 + 1), per(4, n, d), ALU.mult)
                    dve.wait_ge(sem("Vtr"), k + 1)
                    V.tensor_tensor(T["bv"][:, :, :], pbank(b0 + 2), per(1, n, d), ALU.mult).then_inc(sem("bv"), 1)

                def block_mask(l):
                    for d in range(2):
                        T = DT[d]
                        if l == 1:
                            dve.wait_ge(sem("L"), 2 * s + d + 1)
                            dve.wait_ge(sem("dU"), s * LEVELS * 2 + d + 1)
                        else:
                            dve.wait_ge(sem("Z"), z_count(s, l - 1, d))
                        V.tensor_tensor(T["bl"][:, :, :], T["ta"][:, :, :], bh(C(C_LVL + LEVELS * d + l), HEADS),
                                        ALU.mult).then_inc(sem("Bl"), 1)

                for l in range(LEVELS):
                    if 1 <= l < LEVELS - 1:
                        block_mask(l + 1)
                    for d in range(2):
                        T, q = DT[d], (s * LEVELS + l) * 2 + d
                        for o, name in ((0, "T"), (HEADS, "U")):
                            dve.wait_ge(sem("d" + name), q + 1)
                            t = T["tu"][:, o:o + HEADS, :].rearrange("p h t -> p (h t)")
                            V.tensor_tensor(t, f32(t), bank(3 * d + 1 + o // HEADS), ALU.subtract).then_inc(sem(name), 1)
                    if l == 0:
                        block_mask(1)
                    if s == 0:
                        if l == 5:
                            dve.wait_ge(sem("rope"), 1)
                        if l:
                            rope(l - 1)
                        if l < 6:
                            att_normed(l)
                for d in range(2):
                    T, k = DT[d], 2 * s + d
                    dve.wait_ge(sem("LU"), k + 1)
                    dve.wait_ge(sem("t0"), k + 1)
                    V.tensor_tensor(T["bl"][:, :, :], T["nw"][:, :, :], pbank(3 * d), ALU.subtract).then_inc(sem("R2"), 1)
                for d in range(2):
                    T, k = DT[d], 2 * s + d
                    dve.wait_ge(sem("dN"), k + 1)
                    V.tensor_tensor(T["uf"][:, :, :], f32(T["tu"][:, 0:4, :]), pbank(3 * d + 1), ALU.add).then_inc(sem("Uf"), 1)
                if s < NT - 1:
                    decays(s + 1)
                for d in range(2):
                    T, k, n = DT[d], 2 * s + d, CHUNK_ORDER[d][s]
                    if n >= NTC:
                        dve.wait_ge(sem("o"), cnt(k - 3))
                        dst = oT[:, :, (n - NTC) * P:(n - NTC + 1) * P]
                        if s < 4:
                            i = V.tensor_copy(dst, pbank(3 * d + 1))
                        else:
                            dve.wait_ge(sem("oe"), 4)
                            i = V.tensor_tensor(dst, dst, pbank(3 * d + 1), ALU.add)
                        i.then_inc(sem("oe"), 1)
                    dve.wait_ge(sem("Sp"), k + 1)
                    if s == 0:
                        i = V.tensor_copy(S[d][:, :, :], pbank(3 * d + 2))
                    else:
                        dve.wait_ge(sem("S"), cnt(k - 1))
                        for h in range(HEADS):
                            i = V.scalar_tensor_tensor(out=S[d][:, h, :], in0=S[d][:, h, :],
                                                       scalar=smallv[:, 5, n, 4 * d + h:4 * d + h + 1],
                                                       in1=bank(3 * d + 2, P, h * P), op0=ALU.mult, op1=ALU.add)
                    i.then_inc(sem("S"), 1)
            dve.wait_ge(sem("mod_done"), 2 * MODS - 16)
            V.tensor_tensor(modv[:, 0, 16:MODS, 0], bank(7, MODS - 16, 32), vec[:, 1, 16:MODS], ALU.add).then_inc(sem("modv"), 1)
            V.tensor_tensor(modv[:, 1, :, 0], bank(7, MODS, 16 + MODS), vec[:, 1, MODS:2 * MODS], ALU.add).then_inc(sem("modv"), 1)
            dve.wait_ge(sem("modv"), 3)
            pre_weights(1, 0, 4 * KC, 0, V_FFNPRE)
            pre_weights(2, 1, KC, 0, V_MIXPRE + KC)
            pre_weights(3, 1, 4 * KC, 0, V_FFNPRE + KC)
            for k, l, m, row in ((0, 0, 2, V_MIXPOST), (1, 0, 5, V_FFNPOST), (2, 1, 2, V_MIXPOST + KC), (3, 1, 5, V_FFNPOST + KC)):
                i = V.tensor_tensor(post_w[:, k, :], modv[:, l, m * KC:(m + 1) * KC, 0], vec[:, 0, row:row + KC], ALU.mult)
            i.then_inc(sem("norm_w"), 1)

            dve.wait_ge(sem("gate"), HEADS)
            dve.wait_ge(sem("osd"), 1)
            V.reciprocal(odev[:, :], odev[:, :]).then_inc(sem("orc"), 1)
            dve.wait_ge(sem("Vah"), 1)
            V.tensor_tensor(Vl[:, :, :].rearrange("p n t -> p (n t)"), bank(4, ALL),
                                f32(Vh[:, :, :]).rearrange("p n t -> p (n t)"), ALU.subtract).then_inc(sem("Va"), 1)
            for h in range(HEADS):
                dve.wait_ge(sem("orow"), h + 1)
                V.scalar_tensor_tensor(out=oT[:, h, :], in0=oT[:, h, :], scalar=vec[:, 0, V_DNOUT:V_DNOUT + 1],
                                           in1=bank(h), op0=ALU.mult, op1=ALU.mult).then_inc(sem("on1"), 1)
                dve.wait_ge(sem("on1"), h + 1)
                V.tensor_tensor(oT[:, h, :], oT[:, h, :], gT[:, h, :], ALU.mult).then_inc(sem("on"), 1)
            for h in range(HEADS):
                dve.wait_ge(sem("on_hi"), h + 1)
                V.tensor_tensor(mix_lo[:, h, :], oT[:, h, :], f32(mix_hi[:, h, :]), ALU.subtract).then_inc(sem("mix0"), 1)

            NQ = SEQ // P

            def normalize(i):
                dve.wait_ge(sem("expd"), i + 1)
                V.reciprocal(stat[:, 96 + i:97 + i], stat[:, 64 + i:65 + i]).then_inc(sem("rc1"), 1)
                dve.wait_ge(sem("rc1"), i + 1)
                V.tensor_scalar(prob[i % 3][:, :], prob[i % 3][:, :], stat[:, 96 + i:97 + i], None, ALU.mult).then_inc(sem("Pn"), 1)

            def turn_lo(i):
                hh, qt = divmod(i, NQ)
                dve.wait_ge(sem("PTh"), i + 1)
                dst = slice(qt * P, (qt + 1) * P)
                V.tensor_tensor(PTl[hh % 2][:, :, dst], bank(4, ALL).rearrange("p (n t) -> p n t", t=P),
                                    f32(PTh[hh % 2][:, :, dst]), ALU.subtract).then_inc(sem("PT"), 1)

            def head_lo(hh):
                half, t = hh // 4, hh % 4
                r = slice(HD * half, HD * (half + 1))
                dve.wait_ge(sem("ahh"), hh + 1)
                V.tensor_tensor(mix_lo[r, 4 + t, :], bank(6)[r], f32(mix_hi[r, 4 + t, :]), ALU.subtract).then_inc(sem("mix0"), 1)

            for i in range(A_HEADS * NQ + NQ + 2):
                if i < A_HEADS * NQ:
                    dve.wait_ge(sem("sc"), i + 1)
                    V.tensor_reduce(stat[:, i:i + 1], bank(2 * (i % 2), ALL), AX.X, ALU.max).then_inc(sem("mx1"), 1)
                    dve.wait_ge(sem("mx1"), i + 1)
                    V.tensor_scalar(stat[:, 32 + i:33 + i], stat[:, i:i + 1], -HD ** -0.5, None, ALU.mult).then_inc(sem("mx"), 1)
                if 1 <= i <= A_HEADS * NQ:
                    normalize(i - 1)
                if 2 <= i < A_HEADS * NQ + 2:
                    turn_lo(i - 2)
                if i >= 9 and (i - 9) % NQ == 0:
                    head_lo((i - 9) // NQ)
                if i == A_HEADS * NQ:
                    split_lo(U_WOUT, 0)
                    split_lo(U_WOUT + 1, 1)

            def y_out(u0, yq):
                def body(i):
                    for s in range(2):
                        for r in range(2):
                            dve.wait_ge(sem("tile"), 4 * i + (2 * (u0 + s) + r + 1))
                            V.tensor_copy(y[:, bass.ds(4 * i + (2 * s + r), 1), :].rearrange("p c t -> p (c t)"),
                                              bank(2 * s + r)).then_inc(sem("yev"), 1)
                        split_lo(2 * i + (u0 + s + 2), s)
                rep(dve, 2, body)

            def boundary(idx, post, pre, hb, shift):
                rstd(idx, SEQ)
                dve.wait_ge(sem("rrow"), idx + 1)
                dve.wait_ge(sem("norm_w"), 2)
                dve.wait_ge(sem("yev"), cnt(KC * ((idx - 2) // 2 + 1)))
                b = KC * ((idx - 2) // 2)
                for c in range(KC + 1):
                    if c < KC:
                        V.scalar_tensor_tensor(out=y[:, c, :], in0=y[:, c, :], scalar=post_w[:, post, c:c + 1],
                                                   in1=bank(5), op0=ALU.mult, op1=ALU.mult).then_inc(sem("yn"), 1)
                    if c:
                        dve.wait_ge(sem("yn"), b + c)
                        V.tensor_tensor(x[:, c - 1, :], x[:, c - 1, :], y[:, c - 1, :], ALU.add).then_inc(sem("x_new"), 1)
                if idx < 8:
                    rstd(idx + 1, SEQ)
                    dve.wait_ge(sem("rrow"), idx + 2)
                    apply_pre(hb, lambda c: x[:, c, :], tmp, bank(5), SEQ, pre, shift, h_hi, h_lo)

            def conv(src, acc, w, name, count, last):
                for r in range(2):
                    V.scalar_tensor_tensor(out=acc(r)[:, 1:SEQ], in0=src(r)[:, 0:SEQ - 1], scalar=w(0, r),
                                               in1=acc(r)[:, 1:SEQ], op0=ALU.mult, op1=ALU.add).then_inc(sem(name), 1)
                for r in range(2):
                    dve.wait_ge(sem(name), count(r))
                    V.scalar_tensor_tensor(out=acc(r)[:, 0:SEQ - 1], in0=src(r)[:, 1:SEQ], scalar=w(2, r),
                                               in1=acc(r)[:, 0:SEQ - 1], op0=ALU.mult, op1=ALU.add).then_inc(sem(last), 1)

            def ffn(f, U_UP, U_DOWN, yq):
                def up_pair(i, par, j0):
                    tl = lambda r: 2 * i + (FC * f + 2 * j0 + r)
                    u = 2 * i + (U_UP + 2 * j0)
                    split_lo(u + 2, 0)
                    dve.wait_ge(sem("c1"), tl(1) + 1)
                    conv(lambda r: bank(4 * par + r), lambda r: tmp[2 * par + r],
                         lambda k, r: vec[:, 3 + f, bass.ds(2 * i + (2 * j0 + r + 22 * k), 1)],
                         "c2", lambda r: tl(r) + 1, "c3_free")
                    split_lo(u + 3, 1)
                    for r in range(2):
                        dve.wait_ge(sem("sg"), tl(r) + 1)
                        V.tensor_tensor(tmp[2 * par + r][:, :], tmp[2 * par + r][:, :], bank(4 * par + 2 + r), ALU.mult).then_inc(sem("g_free"), 1)
                    for r in range(2):
                        dve.wait_ge(sem("ghi"), tl(r) + 1)
                        j = 2 * i + (2 * j0 + r)
                        flat = lambda m: m[:, bass.ds(j, 1), :].rearrange("p c t -> p (c t)")
                        V.tensor_tensor(flat(mid_lo), tmp[2 * par + r][:, :], f32(flat(mid_hi)), ALU.subtract).then_inc(sem("mid"), 1)

                def up4(i):
                    for par in range(2):
                        up_pair(2 * i, par, par)
                rep(dve, FC // 4, up4)
                up_pair(0, 0, FC // 2 - 1)

                def down2(i, last=False):
                    for q in range(6):
                        if q % 3 == 2:
                            for r in range(2):
                                dve.wait_ge(sem("tile"), 12 * i + (2 * (U_DOWN + q) + r + 1))
                                t = 4 * i + (2 * (q // 3) + r)
                                V.tensor_copy(y[:, bass.ds(t, 1), :].rearrange("p c t -> p (c t)"),
                                                  bank(2 * (q // 3) + r)).then_inc(sem("yev"), 1)
                        if not (last and q >= 4):
                            split_lo(6 * i + (U_DOWN + q + 2), q % 2)
                if f == 0:
                    rep(dve, 2, down2)
                else:
                    down2(0)
                    down2(1, True)

            y_out(U_WOUT, 0)
            boundary(2, 0, 1, 2, lambda c: modv[:, 0, 3 * KC + c, 0:1])
            ffn(0, U_UP0, U_DOWN0, 1)
            boundary(4, 1, 2, 3, lambda c: modv[:, 1, c, 0:1])

            def cx(i, par, j0):
                tl = lambda r: 2 * i + (2 * j0 + r)
                flat = lambda r: cv[:, bass.ds(tl(r), 1), :].rearrange("p c t -> p (c t)")
                split_lo(2 * i + (U_SCIN + 2 * j0 + 2), 0)
                split_lo(2 * i + (U_SCIN + 2 * j0 + 3), 1)
                for r in range(2):
                    dve.wait_ge(sem("scc"), tl(r) + 1)
                    V.tensor_tensor(tmp[2 * par + r][:, :], tmp[2 * par + r][:, :], bank(4 * par + 2 + r), ALU.mult).then_inc(sem("scu"), 1)
                dve.wait_ge(sem("scu"), tl(1) + 1)
                dve.wait_ge(sem("scv1"), tl(1) + 1)
                conv(lambda r: tmp[2 * par + r], flat,
                     lambda k, r: vec[:, 0, bass.ds(2 * i + (2 * j0 + r + V_SCCONV + 8 * k), 1)],
                     "scv2", lambda r: tl(r) + 1, "scv")

            def cx2(i):
                for par in range(2):
                    cx(2 * i, par, par)
            rep(dve, 2, cx2)

            def gate_b(i):
                for s in range(2):
                    split_lo(2 * i + (U_SCIN + 8 + s + 2), s)
                    for r in range(2):
                        t = 4 * i + (2 * s + r)
                        dve.wait_ge(sem("tile"), 4 * i + (2 * (U_SCIN + 8 + s) + r + 1))
                        dve.wait_ge(sem("scv"), KC)
                        V.tensor_tensor(tmp[2 * s + r][:, :], bank(2 * s + r),
                                            cv[:, bass.ds(t, 1), :].rearrange("p c t -> p (c t)"), ALU.mult).then_inc(sem("scb"), 1)
                    for r in range(2):
                        t = 4 * i + (2 * s + r)
                        flat = lambda m: m[:, bass.ds(t, 1), :].rearrange("p c t -> p (c t)")
                        dve.wait_ge(sem("mhi"), t + 1)
                        V.tensor_tensor(flat(mix_lo), tmp[2 * s + r][:, :], f32(flat(mix_hi)), ALU.subtract).then_inc(sem("mix1"), 1)
            rep(dve, 2, gate_b)
            y_out(U_SCOUT, 2)
            boundary(6, 2, 3, 4, lambda c: modv[:, 1, 3 * KC + c, 0:1])
            ffn(1, U_UP1, U_DOWN1, 3)
            boundary(8, 3, None, None, None)
            for n in range(NL):
                dve.wait_ge(sem("out_T"), 2)
                V.tensor_copy(xin[:, n, 512:1024], bank(2 * n + 1)).then_inc(sem("out_ev_d"), 1)

        @block.gpsimd
        def _(pool):
            G = nc.gpsimd

            def pre_squares(idx):
                t4, n = tmp, SEQ
                for c in range(2, KC, 2):
                    pool.wait_ge(sem("sq"), KC * idx + c + 1)
                    if c > 2:
                        pool.wait_ge(sem("sqadd"), sq_adds(idx) + c // 2 - 1)
                    G.tensor_tensor(t4[2][:, 0:n], t4[2][:, 0:n], t4[c % 2][:, 0:n], ALU.add).then_inc(sem("sqadd"), 1)

            def post_squares(idx):
                t4, n = (tmp, SEQ) if idx else (ctmp, CTX)
                if idx >= 2:
                    pool.wait_ge(sem("stat"), idx)
                for c in range(KC):
                    pool.wait_ge(sem("sq"), KC * idx + c + 1)
                    if c == 0:
                        i = G.tensor_copy(t4[2][:, 0:n], t4[0][:, 0:n])
                    else:
                        pool.wait_ge(sem("sqadd"), sq_adds(idx) + c)
                        i = G.tensor_tensor(t4[2][:, 0:n], t4[2][:, 0:n], t4[c % 2][:, 0:n], ALU.add)
                    i.then_inc(sem("sqadd"), 1)

            def mod_add(n, dst, a, b):
                if n % 3:
                    pool.wait_ge(sem("mod_acc"), n)
                G.tensor_tensor(dst, a, b, ALU.add).then_inc(sem("mod_acc"), 1)

            def mod_half(n, slot):
                w = 4 >> (n % 3)
                mod_add(n, slot[:, 0:w, :], slot[:, 0:w, :], slot[:, w:2 * w, :])

            post_squares(0)
            post_squares(1)
            pool.wait_ge(sem("h"), KC)
            for m in range(16, MODS):
                pool.wait_ge(sem("mod_prod"), m - 15)
                mod_half(3 * (m - 16), mraw_b[m % 4])
                mod_half(3 * (m - 16) + 1, mraw_b[m % 4])
                if m >= 20:
                    pool.wait_ge(sem("mod_done"), m - 19)
                mod_add(3 * (m - 16) + 2, macc_b[m % 4][:, :], mraw_b[m % 4][:, 0, :], mraw_b[m % 4][:, 1, :])
            pool.wait_ge(sem("rope_in"), 32)

            def mod_level(q):
                for lag, parts in ((3, (1, 2)), (2, (0,))):
                    for j in mod_at(q, lag):
                        pool.wait_ge(sem("mod_prod"), MODS - 16 + j + 1)
                        for part in parts:
                            mod_half(3 * (MODS - 16 + j) + part, mraw_c[j % MSLOTS])

            pool.wait_ge(sem("dn_ready"), 1)
            for s in range(NT):
                for d in range(2):
                    k, n, T = 2 * s + d, CHUNK_ORDER[d][s], DT[d]
                    pool.wait_ge(sem("GA"), k + 1)
                    G.tensor_tensor(T["ta"][:, :, :], T["ta"][:, :, :], bc(smallv[:, 1, n, 4 * d:4 * d + 4], P), ALU.mult).then_inc(sem("Lb"), 1)
                    pool.wait_ge(sem("Lb"), k + 1)
                    pool.wait_ge(sem("dN"), cnt(k - 1))
                    G.tensor_tensor(T["bl"][:, :, :], T["ta"][:, :, :], bh(C(C_LVL + LEVELS * d), HEADS), ALU.mult).then_inc(sem("Bl"), 1)
                for d in range(2):
                    T = DT[d]
                    pool.wait_ge(sem("Bl"), s * LEVELS * 2 + d + 1)
                    G.tensor_tensor(T["ta"][:, :, :], T["ta"][:, :, :], bh(C(C_STRICT + d), HEADS), ALU.mult).then_inc(sem("L"), 1)
                for l in range(LEVELS):
                    if l == 0:
                        for d in range(2):
                            k, n, T = 2 * s + d, CHUNK_ORDER[d][s], DT[d]
                            if n >= NTC:
                                pool.wait_ge(sem("egr"), cnt(k - 3))
                                G.tensor_tensor(T["qg"][:, :, :], T["qg"][:, :, :], qT[:, :, (n - NTC) * P:(n - NTC + 1) * P],
                                                ALU.mult).then_inc(sem("qg"), 1)
                    if l == 1:
                        for d in range(2):
                            k, n, T = 2 * s + d, CHUNK_ORDER[d][s], DT[d]
                            if n >= NTC:
                                pool.wait_ge(sem("QB"), cnt(k - 3))
                                G.tensor_tensor(T["tb"][:, :, :], T["tb"][:, :, :], bh(C(C_TRI + d), HEADS), ALU.mult).then_inc(sem("intra"), 1)
                    if s == 0 and 1 <= l < 6:
                        pool.wait_ge(sem("shuf"), 2 * l - 1)
                        G.tensor_tensor(rope_tile(l - 1), rope_tile(l - 1), cosT[:, :], ALU.mult).then_inc(sem("rcos"), 1)
                    mod_level(s * LEVELS + l)
                for d in range(2):
                    T, k = DT[d], 2 * s + d
                    pool.wait_ge(sem("T"), (s + 1) * LEVELS * 2 - 1 + d)
                    G.tensor_tensor(T["nw"][:, :, :], bh(ident, HEADS), f32(T["tu"][:, 0:4, :]), ALU.subtract).then_inc(sem("t0"), 1)
            for q in range(LEVELS * NT, LEVELS * NT + 4):
                mod_level(q)
            for idx in range(2, 9):
                if idx in POST:
                    post_squares(idx)
                else:
                    pre_squares(idx)


def constants():
    c = np.zeros((P, NCONST, P), np.float32)
    i = np.arange(P)
    r, q = i[:, None], i[None, :]
    c[:, C_ID] = r == q
    c[:, C_ONE] = 1
    c[:, C_TRI], c[:, C_TRI + 1] = r <= q, r >= q
    c[:, C_STRICT], c[:, C_STRICT + 1] = r > q, r < q
    for l in range(LEVELS):
        s = 1 << l
        low = (r // (2 * s) == q // (2 * s)) & (r // s % 2 == 1) & (q // s % 2 == 0)
        c[:, C_LVL + l], c[:, C_LVL + LEVELS + l] = low, low.T
    c[:, C_BLK] = r // HD == q // HD
    t = np.arange(SEQ)
    inv = (np.float32(ROPE_THETA) ** (-np.arange(0, HD // 2, 2, dtype=np.float32) / np.float32(HD // 2))).astype(np.float32)
    ang = np.concatenate([(t // GRID_W).astype(np.float32)[:, None] * inv, (t % GRID_W).astype(np.float32)[:, None] * inv], 1)
    pair = (i % HD) // 2
    cos = np.cos(ang).T[pair].astype(np.float32)
    sin = np.sin(ang).T[pair].astype(np.float32) * np.where(i % 2 == 0, -1, 1).astype(np.float32)[:, None]
    return {"const": c.reshape(P, NCONST * P), "cos": np.ascontiguousarray(cos), "sin": np.ascontiguousarray(sin)}


_INS = ['x', 'c', 'ctx', 'c_ctx', 'mod_w', 'mod_b', 'norm_mix_pre', 'norm_mix_post', 'norm_ffn_pre', 'norm_ffn_post',
        'hyb_w_in', 'hyb_w_out', 'dn_conv_w', 'dn_a_log', 'dn_dt_bias', 'dn_out_norm', 'att_q_norm', 'att_k_norm',
        'sc_w_in', 'sc_conv_w', 'sc_w_out', 'ffn_w_up', 'ffn_conv_w', 'ffn_w_down']


def kernel(**inputs):
    import concourse.bacc as bacc
    from concourse.bass_utils import run_bass_kernel_spmd

    nc = bacc.Bacc("TRN2", target_bir_lowering=False, num_devices=1)
    arrays = {name: np.ascontiguousarray(inputs[name]) for name in _INS}
    arrays.update(constants())
    args = {name: nc.dram_tensor(f"in_{name}", a.shape, mybir.dt.from_np(a.dtype), kind="ExternalInput").ap()
            for name, a in arrays.items()}
    out = nc.dram_tensor("out", (1, SEQ, D_MODEL), F32, kind="ExternalOutput").ap()
    hybrid_trunk(nc, args, out)
    r = run_bass_kernel_spmd(nc, [{f"in_{name}": a for name, a in arrays.items()}], core_ids=[0])
    return r.results[0]["out"]
```
